# Optimizing a Trainium2 kernel written in Bass

```python
import math
import jax, jax.numpy as jnp
from jax import lax
import numpy as np

D_MODEL = 1024
BATCH = 1
SEQ = 512
DEPTH = 2

N_MEM = 256
D_MIX = D_MODEL
D_RWKV = D_MIX // 2
RW_HEAD = 64
RW_HEADS = D_RWKV // RW_HEAD
RW_W_RANK = 64
RW_A_RANK = 64
RW_G_RANK = 128
RW_V_RANK = 32
RW_SPLITS = [D_RWKV, 2 * D_RWKV, 3 * D_RWKV, 3 * D_RWKV + RW_W_RANK, 3 * D_RWKV + RW_W_RANK + RW_A_RANK]
RW_COLS = 3 * D_RWKV + RW_W_RANK + RW_A_RANK + RW_G_RANK
D_S5 = D_MIX - D_RWKV
S5_CH = 16
S5_GROUPS = D_S5 // S5_CH
S5_STATE = 64
D_IN = RW_COLS + D_S5
XA_HEADS = 4
XA_HEAD = D_MODEL // XA_HEADS
PEER_HEADS = 8
PEER_NKEYS = 128
PEER_N = PEER_NKEYS * PEER_NKEYS
PEER_DQ = 256
PEER_DHALF = PEER_DQ // 2
PEER_TOPK = 16
PEER_BLOCK = 128
RMS_EPS = 1e-6
GN_EPS = 64e-5

kernel_name = 'hybrid_rwkv7_s5_peer_memxattn'

def rmsnorm(x, g):
    xf = x.astype(jnp.float32)
    y = xf * lax.rsqrt(jnp.mean(xf * xf, axis=-1, keepdims=True) + RMS_EPS)
    return (y * g.astype(jnp.float32)).astype(x.dtype)

def token_shift(z):
    return jnp.pad(z[:, :-1], ((0, 0), (1, 0), (0, 0)))

def rwkv7_recurrence(r, decay, k, v, a_vec, b_vec):
    bsz, _, nh, n = r.shape

    def step(state, inp):
        r_t, w_t, k_t, v_t, a_t, b_t = inp
        sa = jnp.einsum('bhij,bhj->bhi', state, a_t)
        state = (state * w_t[:, :, None, :] + sa[..., :, None] * b_t[..., None, :]
                 + v_t[..., :, None] * k_t[..., None, :])
        return state, jnp.einsum('bhij,bhj->bhi', state, r_t)

    xs = tuple(jnp.swapaxes(t, 0, 1) for t in (r, decay, k, v, a_vec, b_vec))
    s0 = jnp.zeros((bsz, nh, n, n), jnp.float32)
    _, y = lax.scan(step, s0, xs)
    return jnp.swapaxes(y, 0, 1)

def rwkv7_mix(z, h, mu, w0, w2, a0, a2, g2, k_k, k_a, r_k, lnx_g, lnx_b, v_first, vres):
    f32 = jnp.float32
    bsz, s, _ = z.shape
    z = z + (token_shift(z) - z) * mu
    r, k, v, wd, ad, gd = jnp.split(z, RW_SPLITS, axis=-1)
    w = -jax.nn.softplus(-(w0 + jnp.tanh(wd) @ w2)) - 0.5
    decay = jnp.exp(-jnp.exp(w.astype(f32)))
    if vres is None:
        v_first = v
    else:
        v0, v1, v2 = vres
        v = v + (v_first - v) * jax.nn.sigmoid(v0 + (h @ v1) @ v2)
    a = jax.nn.sigmoid(a0 + ad @ a2)
    g = jax.nn.sigmoid(gd) @ g2

    def heads(t):
        return t.reshape(bsz, s, RW_HEADS, RW_HEAD).astype(f32)

    kk = heads(k * k_k)
    kk = kk / jnp.maximum(jnp.sqrt(jnp.sum(kk * kk, axis=-1, keepdims=True)), 1e-12)
    k = k * (1.0 + (a - 1.0) * k_a)
    rh, kh, vh, ah = heads(r), heads(k), heads(v), heads(a)
    y = rwkv7_recurrence(rh, heads(decay), kh, vh, -kk, kk * ah)
    mean = jnp.mean(y, axis=-1, keepdims=True)
    var = jnp.mean(jnp.square(y - mean), axis=-1, keepdims=True)
    y = ((y - mean) * lax.rsqrt(var + GN_EPS)).reshape(bsz, s, D_RWKV)
    y = y * lnx_g.astype(f32) + lnx_b.astype(f32)
    bonus = jnp.sum(rh * kh * r_k.astype(f32), axis=-1, keepdims=True) * vh
    out = (y + bonus.reshape(bsz, s, D_RWKV)) * g.astype(f32)
    return out.astype(z.dtype), v_first

def complex_affine_combine(e1, e2):
    a1r, a1i, b1r, b1i = e1
    a2r, a2i, b2r, b2i = e2
    ar = a2r * a1r - a2i * a1i
    ai = a2r * a1i + a2i * a1r
    wr, wi = a2r[:, None], a2i[:, None]
    br = wr * b1r - wi * b1i + b2r
    bi = wr * b1i + wi * b1r + b2i
    return ar, ai, br, bi

def s5_mix(u, a_re, a_im, log_dt, b_re, b_im, c_re, c_im, d_skip, glu_w, glu_b, out_g):
    f32 = jnp.float32
    bsz, s, _ = u.shape
    uf = u.astype(f32).reshape(bsz, s, S5_GROUPS, S5_CH)
    lam_re = jnp.minimum(a_re.astype(f32), -1e-4)
    lam_im = a_im.astype(f32)
    dt = jnp.exp(log_dt.astype(f32))[:, None]
    mag = jnp.exp(lam_re * dt)
    lb_re = mag * jnp.cos(lam_im * dt)
    lb_im = mag * jnp.sin(lam_im * dt)
    den = lam_re * lam_re + lam_im * lam_im
    c1_re = ((lb_re - 1.0) * lam_re + lb_im * lam_im) / den
    c1_im = (lb_im * lam_re - (lb_re - 1.0) * lam_im) / den
    br, bi = b_re.astype(f32), b_im.astype(f32)
    bb_re = c1_re[..., None] * br - c1_im[..., None] * bi
    bb_im = c1_re[..., None] * bi + c1_im[..., None] * br
    bu_re = jnp.einsum('bsgc,gpc->sbgp', uf, bb_re)
    bu_im = jnp.einsum('bsgc,gpc->sbgp', uf, bb_im)
    ar_seq = jnp.broadcast_to(lb_re, (s, S5_GROUPS, S5_STATE))
    ai_seq = jnp.broadcast_to(lb_im, (s, S5_GROUPS, S5_STATE))
    _, _, x_re, x_im = lax.associative_scan(complex_affine_combine, (ar_seq, ai_seq, bu_re, bu_im), axis=0)
    y = (jnp.einsum('sbgp,gcp->bsgc', x_re, c_re.astype(f32))
         - jnp.einsum('sbgp,gcp->bsgc', x_im, c_im.astype(f32)))
    y = y.reshape(bsz, s, D_S5) + d_skip.astype(f32) * uf.reshape(bsz, s, D_S5)
    y = jax.nn.gelu(y)
    y = y * jax.nn.sigmoid(y @ glu_w.astype(f32) + glu_b.astype(f32))
    return rmsnorm(y, out_g).astype(u.dtype)

def mem_cross_attention(h, m, wq, wk, wv, wo):
    bsz, s, _ = h.shape
    q = (h @ wq).reshape(bsz, s, XA_HEADS, XA_HEAD)
    k = (m @ wk).reshape(bsz, N_MEM, XA_HEADS, XA_HEAD)
    v = (m @ wv).reshape(bsz, N_MEM, XA_HEADS, XA_HEAD)
    sc = jnp.einsum('bshd,bmhd->bhsm', q, k).astype(jnp.float32) * (XA_HEAD ** -0.5)
    p = jax.nn.softmax(sc, axis=-1).astype(v.dtype)
    o = jnp.einsum('bhsm,bmhd->bshd', p, v).reshape(bsz, s, D_MODEL)
    return o @ wo

def peer_ffn(h, wq, keys, u_tab, v_tab):
    bsz, s, d = h.shape
    hb = h.reshape(-1, PEER_BLOCK, d)

    def block(hc):
        q = (hc @ wq).reshape(PEER_BLOCK, PEER_HEADS, 2, PEER_DHALF)
        sc = jnp.einsum('thcd,hckd->thck', q, keys).astype(jnp.float32)
        s1, i1 = lax.top_k(sc[:, :, 0], PEER_TOPK)
        s2, i2 = lax.top_k(sc[:, :, 1], PEER_TOPK)
        cand = (s1[..., :, None] + s2[..., None, :]).reshape(PEER_BLOCK, PEER_HEADS, PEER_TOPK * PEER_TOPK)
        cidx = (i1[..., :, None] * PEER_NKEYS + i2[..., None, :]).reshape(PEER_BLOCK, PEER_HEADS, PEER_TOPK * PEER_TOPK)
        top, pos = lax.top_k(cand, PEER_TOPK)
        eidx = jnp.take_along_axis(cidx, pos, axis=-1)
        gate = jax.nn.softmax(top, axis=-1)
        ue = jnp.take(u_tab, eidx, axis=0)
        act = jax.nn.gelu(jnp.einsum('thkd,td->thk', ue, hc).astype(jnp.float32))
        ve = jnp.take(v_tab, eidx, axis=0)
        return jnp.einsum('thk,thkd->td', (gate * act).astype(ve.dtype), ve)

    return lax.map(block, hb).reshape(bsz, s, d)

def setup_inputs(seed: int = 0) -> dict:
    key = jax.random.key(seed)
    ks = iter(jax.random.split(key, 48))
    L = DEPTH
    LV = max(DEPTH - 1, 0)
    f32 = jnp.float32

    def nrm(shape, scale):
        return scale * jax.random.normal(next(ks), shape, f32)

    def gain(shape):
        return 1.0 + nrm(shape, 0.02)

    def unif(shape, lo, hi):
        return jax.random.uniform(next(ks), shape, f32, lo, hi)

    n_idx = jnp.arange(S5_STATE, dtype=f32)
    return {
        'x': nrm((BATCH, SEQ, D_MODEL), 1.0),
        'mem': nrm((BATCH, N_MEM, D_MODEL), 1.0),
        'norm_mix': gain((L, D_MODEL)),
        'w_in': nrm((L, D_MODEL, D_IN), D_MODEL ** -0.5),
        'rw_mu': unif((L, RW_COLS), 0.0, 1.0),
        'rw_w0': unif((L, D_RWKV), -6.0, -1.0),
        'rw_w2': nrm((L, RW_W_RANK, D_RWKV), 0.3 * RW_W_RANK ** -0.5),
        'rw_a0': nrm((L, D_RWKV), 0.3),
        'rw_a2': nrm((L, RW_A_RANK, D_RWKV), 0.3 * RW_A_RANK ** -0.5),
        'rw_g2': nrm((L, RW_G_RANK, D_RWKV), RW_G_RANK ** -0.5),
        'rw_kk': 0.85 + nrm((L, D_RWKV), 0.02),
        'rw_ka': gain((L, D_RWKV)),
        'rw_rk': nrm((L, RW_HEADS, RW_HEAD), 0.1),
        'rw_v0': 1.0 + nrm((LV, D_RWKV), 0.1),
        'rw_v1': nrm((LV, D_MODEL, RW_V_RANK), D_MODEL ** -0.5),
        'rw_v2': nrm((LV, RW_V_RANK, D_RWKV), 0.3 * RW_V_RANK ** -0.5),
        'rw_lnx_g': gain((L, D_RWKV)),
        'rw_lnx_b': nrm((L, D_RWKV), 0.01),
        's5_a_re': -0.5 + nrm((L, S5_GROUPS, S5_STATE), 0.01),
        's5_a_im': math.pi * n_idx + nrm((L, S5_GROUPS, S5_STATE), 0.01),
        's5_log_dt': unif((L, S5_GROUPS), math.log(1e-3), math.log(1e-1)),
        's5_b_re': nrm((L, S5_GROUPS, S5_STATE, S5_CH), (2 * S5_CH) ** -0.5),
        's5_b_im': nrm((L, S5_GROUPS, S5_STATE, S5_CH), (2 * S5_CH) ** -0.5),
        's5_c_re': nrm((L, S5_GROUPS, S5_CH, S5_STATE), S5_STATE ** -0.5),
        's5_c_im': nrm((L, S5_GROUPS, S5_CH, S5_STATE), S5_STATE ** -0.5),
        's5_d': nrm((L, D_S5), 1.0),
        's5_glu_w': nrm((L, D_S5, D_S5), D_S5 ** -0.5),
        's5_glu_b': nrm((L, D_S5), 0.01),
        's5_out_g': gain((L, D_S5)),
        'w_out': nrm((L, D_MIX, D_MODEL), D_MIX ** -0.5),
        'norm_xa': gain((L, D_MODEL)),
        'norm_mem': gain((L, D_MODEL)),
        'xa_wq': nrm((L, D_MODEL, D_MODEL), D_MODEL ** -0.5),
        'xa_wk': nrm((L, D_MODEL, D_MODEL), D_MODEL ** -0.5),
        'xa_wv': nrm((L, D_MODEL, D_MODEL), D_MODEL ** -0.5),
        'xa_wo': nrm((L, D_MODEL, D_MODEL), D_MODEL ** -0.5),
        'norm_ffn': gain((L, D_MODEL)),
        'peer_wq': nrm((L, D_MODEL, PEER_HEADS * PEER_DQ), D_MODEL ** -0.5),
        'peer_keys': nrm((L, PEER_HEADS, 2, PEER_NKEYS, PEER_DHALF), PEER_DHALF ** -0.5),
        'peer_u': nrm((L, PEER_N, D_MODEL), D_MODEL ** -0.5),
        'peer_v': nrm((L, PEER_N, D_MODEL), PEER_HEADS ** -0.5),
        'norm_final': gain((D_MODEL,)),
    }

def reference(x, mem, norm_mix, w_in, rw_mu, rw_w0, rw_w2, rw_a0, rw_a2, rw_g2, rw_kk, rw_ka, rw_rk,
              rw_v0, rw_v1, rw_v2, rw_lnx_g, rw_lnx_b, s5_a_re, s5_a_im, s5_log_dt, s5_b_re, s5_b_im,
              s5_c_re, s5_c_im, s5_d, s5_glu_w, s5_glu_b, s5_out_g, w_out, norm_xa, norm_mem,
              xa_wq, xa_wk, xa_wv, xa_wo, norm_ffn, peer_wq, peer_keys, peer_u, peer_v, norm_final):
    v_first = None
    for l in range(DEPTH):
        h = rmsnorm(x, norm_mix[l])
        z = h @ w_in[l]
        z_rw, u_s5 = z[..., :RW_COLS], z[..., RW_COLS:]
        vres = None if l == 0 else (rw_v0[l - 1], rw_v1[l - 1], rw_v2[l - 1])
        y_rw, v_first = rwkv7_mix(z_rw, h, rw_mu[l], rw_w0[l], rw_w2[l], rw_a0[l], rw_a2[l], rw_g2[l],
                                  rw_kk[l], rw_ka[l], rw_rk[l], rw_lnx_g[l], rw_lnx_b[l], v_first, vres)
        y_s5 = s5_mix(u_s5, s5_a_re[l], s5_a_im[l], s5_log_dt[l], s5_b_re[l], s5_b_im[l],
                      s5_c_re[l], s5_c_im[l], s5_d[l], s5_glu_w[l], s5_glu_b[l], s5_out_g[l])
        x = x + jnp.concatenate([y_rw, y_s5], axis=-1) @ w_out[l]
        x = x + mem_cross_attention(rmsnorm(x, norm_xa[l]), rmsnorm(mem, norm_mem[l]),
                                    xa_wq[l], xa_wk[l], xa_wv[l], xa_wo[l])
        x = x + peer_ffn(rmsnorm(x, norm_ffn[l]), peer_wq[l], peer_keys[l], peer_u[l], peer_v[l])
    return rmsnorm(x, norm_final)


_drawn_inputs = setup_inputs


def setup_inputs(seed=0):
    import zlib

    import numpy as np

    out = dict(_drawn_inputs(seed))
    spreads = {}
    factors = {'rw_w2': 3.166,
     'rw_kk': 3.061,
     'rw_v0': 17.189,
     'rw_lnx_g': 2.769,
     'rw_lnx_b': 3.934,
     's5_a_re': 63.824,
     's5_glu_b': 4.47,
     'norm_xa': 4.951,
     'norm_mem': 4.515,
     'norm_final': 8.409,
     'rw_v1': 5.934,
     'rw_v2': 5.876,
     'norm_ffn': 2.792}
    for name, (base, spread) in spreads.items():
        noise = np.random.default_rng([zlib.crc32(name.encode()), seed]).standard_normal(out[name].shape)
        drawn = base * np.exp(spread * noise) if base else spread * noise
        out[name] = __import__('jax').numpy.asarray(drawn.astype(out[name].dtype))
    for name, factor in factors.items():
        out[name] = (out[name] * factor).astype(out[name].dtype)
    return out
```

```python
import math
from contextlib import ExitStack

import concourse.bass as bass
from concourse import mybir

F32 = mybir.dt.float32
ALU = mybir.AluOpType
ACT = mybir.ActivationFunctionType
AX = mybir.AxisListType

P = 128
D = 1024
KD = D // P
T = 512
DEPTH = 2
N_MEM = 256
D_HALF = 512
KH = D_HALF // P
RW_TILES = 14
IN_TILES = 18
HEADS, HEAD = 8, 64
CH = 64
NCH = T // CH
TB = T // P
S5_PAIRS = 16
S5_C = 16
SC = 8
SN = T // SC
XA_HEADS, XA_HEAD = 4, 256
PH, NKEY, TOPK = 8, 128, 16
HALF_KEYS = NKEY // 2
RMS_EPS, GN_EPS = 1e-6, 64e-5
DECAY_SCALE = -math.exp(-0.5)
TWO_PI_HI, TWO_PI_LO = 6.28125, 2 * math.pi - 6.28125
PI_IN = 3.1415925
ROUND = 12582912.0
LOWEST = -3.0e38

VEC = {}
_at = 0
for _name, _n in (("norm_mix", 8), ("norm_xa", 8), ("norm_mem", 8), ("norm_ffn", 8), ("norm_final", 8),
                  ("mu", 14), ("w0", 4), ("a0", 4), ("kk", 4), ("ka", 4), ("rk", 4), ("v0", 4),
                  ("lnx_g", 4), ("lnx_b", 4), ("s5_d", 4), ("glu_b", 4), ("out_g", 4)):
    VEC[_name] = _at
    _at += _n
NVEC = _at


FREEING = ["proj_summed0", "proj_summed1", "proj_taken0", "proj_taken1", "gates_summed0", "gates_summed1",
           "gates_taken0", "gates_taken1"] + [f"{n}{b}" for n in ("u_summed", "u_gelued", "u_weighed", "down_used")
                                              for b in range(4)]


class Signal:

    def __init__(self, sem):
        self.sem, self.base, self.n = sem, 0, 0

    def at(self, n):
        return self.base + n

    def passed(self, n):
        self.base += n


class Program:

    def __init__(self, nc, ctx, dram):
        self.nc, self.ctx, self.dram, self.known = nc, ctx, dram, {}
        self.c, self.made = {}, 0
        self.xT = self.vec = None

    def counts(self, name):
        if name not in self.known:
            self.known[name] = Signal(self.ctx.enter_context(self.nc.semaphore(name)))
            self.known[name].base = int(name in FREEING)
        return self.known[name]

    def sbuf(self, name, shape, dt):
        self.made += 1
        return self.nc.sbuf_tensor(f"{name}_{self.made}", shape, dt)

    def psum(self, name, shape, dt):
        self.made += 1
        return self.nc.psum_tensor(f"{name}_{self.made}", shape, dt)


def linker(engine, s):
    def link(ins):
        s.n += 1
        ins.then_inc(s.sem, 1)
        engine.wait_ge(s.sem, s.n)
    return link


def constants(pg):
    nc, c = pg.nc, pg.c
    made = pg.counts("constants_made")
    pool_step = pg.counts("pool_step")
    with nc.Block() as block:
        @block.gpsimd
        def _(pool):
            link = linker(pool, pool_step)
            for name in FREEING:
                pool.sem_inc(pg.counts(name).sem, 1)
            link(pool.memset(c["ones"][:, :], 1.0))
            link(pool.memset(c["ident"][:, :], 0.0))
            link(pool.affine_select(out=c["ident"][:, :], in_=c["ident"][:, :], compare_op=ALU.not_equal, fill=1.0,
                                    base=0, pattern=[[-1, P]], channel_multiplier=1))
            link(pool.memset(c["head_ones"][:, :], 0.0))
            link(pool.memset(c["head_ones"][0:64, 0:64], 1.0))
            link(pool.memset(c["head_ones"][64:128, 64:128], 1.0))
            hm = c["head_ones"][:, :]
            m = c["gram_mask"]
            for k in range(4):
                strict = k % 2 == 0
                link(pool.affine_select(out=m[:, k, :], in_=hm, compare_op=ALU.is_gt if strict else ALU.is_ge,
                                        fill=0.0, base=0, pattern=[[1, P]], channel_multiplier=-1))
            link(pool.affine_select(out=c["lower_mask"][:, :], in_=hm, compare_op=ALU.is_gt, fill=0.0, base=0,
                                    pattern=[[-1, P]], channel_multiplier=1))
            for lv in range(6):
                b = 1 << lv
                o = c["level_mask"][:, lv, :].rearrange("p (g h b) -> p g h b", h=2, b=b)
                link(pool.memset(c["level_mask"][:, lv, :], 0.0))
                link(pool.memset(o[:, :, 1, :], 1.0))
                link(pool.affine_select(out=o[:, :, 1, :], in_=o[:, :, 1, :], compare_op=ALU.is_ge, fill=0.0,
                                        base=0, pattern=[[-2 * b, P // (2 * b)], [0, b]], channel_multiplier=1))
                link(pool.affine_select(out=o[:, :, 1, :], in_=o[:, :, 1, :], compare_op=ALU.is_gt, fill=0.0,
                                        base=b, pattern=[[2 * b, P // (2 * b)], [0, b]], channel_multiplier=-1))
            link(pool.memset(c["chunk_keep"][:, :], 1.0))
            link(pool.memset(c["chunk_keep"][:, :].rearrange("p (n s) -> p n s", s=CH)[:, :, 0:1], 0.0))
            link(pool.memset(c["level0_lower"][:, :], 0.0))
            ev = c["level0_lower"][:, :].rearrange("p (g h) -> p g h", h=2)[:, :, 0:1]
            link(pool.affine_select(out=ev, in_=ev, compare_op=ALU.not_equal, fill=1.0, base=-1,
                                    pattern=[[-2, P // 2], [0, 1]], channel_multiplier=1))
            pool.iota(c["ramp"][:, :], pattern=[[1, NKEY]], base=0, channel_multiplier=0,
                      allow_small_or_imprecise_dtypes=True).then_inc(made.sem, 1)
            pool.wait_ge(made.sem, made.at(1))
        @block.sync
        def _(sp):
            sp.dma_start(pg.xT[:, :, :], pg.dram["xT"]).then_inc(pg.counts("x_loaded").sem, 16)
            sp.wait_ge(pg.counts("x_loaded").sem, 16)
    made.passed(1)


def norm(pg, src, gain, dst, n):
    nc = pg.nc
    squared, summed, meaned, rooted = (pg.counts(s) for s in ("norm_squared", "norm_summed", "norm_meaned", "norm_rooted"))
    vec_step = pg.counts("vec_step")
    with ExitStack() as ctx:
        sq = ctx.enter_context(pg.sbuf("norm_sq", [P, KD, n], F32))
        root = ctx.enter_context(pg.sbuf("norm_root", [P, n], F32))
        rstd = ctx.enter_context(pg.sbuf("norm_rstd", [P, n], F32))
        ps = ctx.enter_context(pg.psum("norm_ps", [P, n], F32))
        block = ctx.enter_context(nc.Block())

        @block.scalar
        def _(act):
            for k in range(KD):
                act.activation(sq[:, k, :], src[:, k, :], ACT.Square).then_inc(squared.sem, 1)
            act.wait_ge(meaned.sem, meaned.at(1))
            act.activation(root[:, :], rstd[:, :], ACT.Sqrt).then_inc(rooted.sem, 1)

        @block.tensor
        def _(pe):
            for k in range(KD):
                pe.wait_ge(squared.sem, squared.at(k + 1))
                last = pe.matmul(ps[:, :], pg.c["ones"][:, :], sq[:, k, :], start=(k == 0), stop=(k == KD - 1))
            last.then_inc(summed.sem, 1)

        @block.vector
        def _(dve):
            link = linker(dve, vec_step)
            dve.wait_ge(summed.sem, summed.at(1))
            dve.tensor_scalar(rstd[:, :], ps[:, :], 1.0 / D, RMS_EPS, ALU.mult, ALU.add).then_inc(meaned.sem, 1)
            dve.wait_ge(rooted.sem, rooted.at(1))
            link(dve.reciprocal(rstd[:, :], root[:, :]))
            for k in range(KD):
                last = dve.scalar_tensor_tensor(out=dst[:, k, :], in0=src[:, k, :], scalar=gain[:, k:k + 1],
                                                in1=rstd[:, :], op0=ALU.mult, op1=ALU.mult)
            link(last)
    squared.passed(KD)
    for s in (summed, meaned, rooted):
        s.passed(1)


def project(pg, weights, tiles, kt, rhs, n, dest, add=False):
    nc = pg.nc
    loaded = [pg.counts(f"w_loaded{b}") for b in range(2)]
    summed = [pg.counts(f"proj_summed{b}") for b in range(2)]
    taken = [pg.counts(f"proj_taken{b}") for b in range(2)]
    turns = tiles // 2
    with ExitStack() as ctx:
        w = [ctx.enter_context(pg.sbuf(f"proj_w{b}", [P, kt, P], F32)) for b in range(2)]
        ps = [ctx.enter_context(pg.psum(f"proj_ps{b}", [P, n], F32)) for b in range(2)]
        block = ctx.enter_context(nc.Block())

        @block.sync
        def _(sp):
            with sp.Fori(0, turns) as i:
                for b in range(2):
                    sp.wait_ge(summed[b].sem, summed[b].at(0) + i)
                    sp.dma_start(w[b][:, :, :], weights[bass.ds(i * 2 + b, 1), :, :].rearrange("a p (k n) -> p (a k) n", n=P)) \
                        .then_inc(loaded[b].sem, 16)

        @block.tensor
        def _(pe):
            with pe.Fori(0, turns) as i:
                for b in range(2):
                    pe.wait_ge(loaded[b].sem, loaded[b].at(16) + i * 16)
                    pe.wait_ge(taken[b].sem, taken[b].at(0) + i)
                    for k in range(kt):
                        last = pe.matmul(ps[b][:, :], w[b][:, k, :], rhs[:, k, :], start=(k == 0), stop=(k == kt - 1))
                    last.then_inc(summed[b].sem, 1)

        if add:
            @block.vector
            def _(dve):
                with dve.Fori(0, turns) as i:
                    for b in range(2):
                        dve.wait_ge(summed[b].sem, summed[b].at(1) + i)
                        o = dest[:, bass.ds(i * 2 + b, 1), :].rearrange("p a n -> p (a n)")
                        dve.tensor_tensor(o, o, ps[b][:, :], ALU.add).then_inc(taken[b].sem, 1)
        else:
            @block.scalar
            def _(act):
                with act.Fori(0, turns) as i:
                    for b in range(2):
                        act.wait_ge(summed[b].sem, summed[b].at(1) + i)
                        o = dest[:, bass.ds(i * 2 + b, 1), :].rearrange("p a n -> p (a n)")
                        act.activation(o, ps[b][:, :], ACT.Copy).then_inc(taken[b].sem, 1)
    for b in range(2):
        loaded[b].passed(16 * turns)
        for s in (summed[b], taken[b]):
            s.passed(turns)


def vec(pg, name):
    n = {"mu": RW_TILES}.get(name, KD if name.startswith("norm") else KH)
    return pg.vec[:, VEC[name]:VEC[name] + n]


def load_vectors(pg, layer):
    loaded = pg.counts("vectors_loaded")
    with pg.nc.Block() as block:
        @block.sync
        def _(sp):
            sp.dma_start(pg.vec[:, :], pg.dram["vec"][layer]).then_inc(loaded.sem, 16)
            sp.wait_ge(loaded.sem, loaded.at(16))
    loaded.passed(16)


def mixer(pg, layer):
    nc, dram = pg.nc, pg.dram

    def buf(own, name, shape):
        return own.enter_context(pg.sbuf(name, shape, F32))

    with ExitStack() as whole:
        mixT = buf(whole, "mixT", [P, KD, T])
        with ExitStack() as rw:
            r = {n: buf(rw, n, s) for n, s in (
                ("v", [P, KH, T]), ("bonus", [P, KH, T]), ("ar", [P, KH, TB, 2, P]),
                ("b", [P, KH, T]), ("k", [P, KH, T]), ("b_end", [P, KH, T]), ("k_end", [P, KH, T]),
                ("p_end", [P, KH, NCH]))}
            with ExitStack() as own:
                rk = buf(own, "rk", [P, 2, KH, T])
                wag = buf(own, "wag", [P, 2, T])
                h = buf(own, "h", [P, KD, T])
                norm(pg, pg.xT, vec(pg, "norm_mix"), h, T)
                with ExitStack() as first:
                    zb = buf(first, "zb", [P, IN_TILES, T + 1])
                    project(pg, dram["w_in"][layer], IN_TILES, KD, h, T, zb[:, :, 1:T + 1])
                    token_shift(pg, layer, zb, rk, r["v"], wag, mixT)
                rwkv_prepare(pg, layer, rk, wag, h, r, mixT)
            with ExitStack() as own:
                st = {n: buf(own, n, s) for n, s in (
                    ("f", [P, NCH, KH, P]), ("hh", [P, NCH, KH, P]), ("rq", [P, KH, T]), ("y", [P, KH, T]))}
                rwkv_chunks(pg, r, st)
                rwkv_states(pg, st)
                rwkv_finish(pg, r, st, mixT)
        s5(pg, layer, mixT)
        project(pg, dram["w_out"][layer], KD, KD, mixT, T, pg.xT, add=True)


def token_shift(pg, layer, zb, rk, v, wag, mixT):
    nc = pg.nc
    cleared, moved = pg.counts("shift_cleared"), pg.counts("u_moved")
    vec_step = pg.counts("vec_step")
    mu = vec(pg, "mu")
    with ExitStack() as ctx:
        diff = [ctx.enter_context(pg.sbuf(f"shift_diff{b}", [P, T], F32)) for b in range(2)]
        block = ctx.enter_context(nc.Block())
        places = [rk[:, 0, i, :] for i in range(4)] + [rk[:, 1, i, :] for i in range(4)] + \
                 [v[:, i, :] for i in range(4)] + [wag[:, i, :] for i in range(2)]

        @block.gpsimd
        def _(pool):
            pool.memset(zb[:, :, 0:1], 0.0).then_inc(cleared.sem, 1)

        @block.scalar
        def _(act):
            act.activation(mixT[:, KH:KD, :], zb[:, RW_TILES:IN_TILES, 1:T + 1], ACT.Copy).then_inc(moved.sem, 1)

        @block.vector
        def _(dve):
            link = linker(dve, vec_step)
            dve.wait_ge(cleared.sem, cleared.at(1))
            for i in range(RW_TILES):
                link(dve.tensor_tensor(diff[i % 2][:, :], zb[:, i, 0:T], zb[:, i, 1:T + 1], ALU.subtract))
                link(dve.scalar_tensor_tensor(out=places[i], in0=diff[i % 2][:, :], scalar=mu[:, i:i + 1],
                                              in1=zb[:, i, 1:T + 1], op0=ALU.mult, op1=ALU.add))
            if layer == 0:
                link(dve.tensor_copy(pg.v_first[:, :, :], v[:, :, :]))
    cleared.passed(1)
    moved.passed(1)


def rwkv_prepare(pg, layer, rk, wag, h, r, mixT):
    nc, dram = pg.nc, pg.dram
    gate = mixT[:, 0:KH, :]
    rT, kT, v = rk[:, 0], rk[:, 1], r["v"]
    small_loaded, squashed = pg.counts("lora_loaded"), pg.counts("lora_squashed")
    lora_in, lora_in_taken = pg.counts("v1_summed"), pg.counts("v1_taken")
    low, low_taken = pg.counts("lora_summed"), pg.counts("lora_taken")
    kk_made, kk_squared, kk_summed, kk_rooted = (pg.counts(s) for s in ("kk_made", "kk_squared", "kk_summed", "kk_rooted"))
    logs_made, exps_made = pg.counts("logs_made"), pg.counts("exps_made")
    rk_made, rk_summed = pg.counts("rk_made"), pg.counts("rk_summed")
    vec_step, act_step = pg.counts("vec_step"), pg.counts("act_step")
    kinds = (["v"] if layer else []) + ["w", "a", "g"]
    with ExitStack() as ctx:
        def buf(name, shape):
            return ctx.enter_context(pg.sbuf(name, shape, F32))
        lw, cum, e, av, kk = (buf(n, [P, KH, T]) for n in ("lw", "cum", "e", "av", "kk"))
        wa, g2 = kk[:, 0, :], kk[:, 1, :]
        v1, v2, vl = kk[:, 2, 0:256].rearrange("p (k n) -> p k n", k=KD), kk[0:32, 3, :], kk[32:64, 3, :]
        vl = cum[0:32, 0, :]
        ps = [ctx.enter_context(pg.psum(f"prep_ps{b}", [P, T], F32)) for b in range(8)]
        block = ctx.enter_context(nc.Block())
        loads = 5 if layer else 3

        @block.sync
        def _(sp):
            sp.dma_start(wa[0:64], dram["w2"][layer]).then_inc(small_loaded.sem, 16)
            sp.dma_start(wa[64:128], dram["a2"][layer]).then_inc(small_loaded.sem, 16)
            sp.dma_start(g2, dram["g2"][layer]).then_inc(small_loaded.sem, 16)
            if layer:
                sp.dma_start(v1, dram["v1"][layer - 1]).then_inc(small_loaded.sem, 16)
                sp.dma_start(v2, dram["v2"][layer - 1]).then_inc(small_loaded.sem, 16)

        @block.tensor
        def _(pe):
            pe.wait_ge(small_loaded.sem, small_loaded.at(16 * loads))
            if layer:
                for k in range(KD):
                    last = pe.matmul(ps[7][0:32, :], v1[:, k, :], h[:, k, :], start=(k == 0), stop=(k == KD - 1))
                last.then_inc(lora_in.sem, 1)
                pe.wait_ge(lora_in_taken.sem, lora_in_taken.at(1))
            pe.wait_ge(squashed.sem, squashed.at(2))
            for m in range(4 * len(kinds)):
                kind, t = kinds[m // 4], m % 4
                if m >= 4:
                    pe.wait_ge(low_taken.sem, low_taken.at(m - 3))
                cols = slice(t * P, (t + 1) * P)
                lhs, rhs = {"v": (v2[:, cols], vl), "w": (wa[0:64, cols], wag[0:64, 0, :]),
                            "a": (wa[64:128, cols], wag[64:128, 0, :]), "g": (g2[:, cols], wag[:, 1, :])}[kind]
                pe.matmul(ps[m % 4][:, :], lhs, rhs, start=True, stop=True).then_inc(low.sem, 1)
            for t in range(KH):
                pe.wait_ge(kk_squared.sem, kk_squared.at(t + 1))
                last = pe.matmul(ps[4 + t][:, :], pg.c["head_ones"][:, :], e[:, t, :], start=True, stop=True)
            last.then_inc(kk_summed.sem, 1)
            pe.wait_ge(rk_made.sem, rk_made.at(1))
            for t in range(KH):
                last = pe.matmul(ps[t][:, :], pg.c["head_ones"][:, :], e[:, t, :], start=True, stop=True)
            last.then_inc(rk_summed.sem, 1)

        @block.scalar
        def _(act):
            link = linker(act, act_step)
            act.activation(wag[0:64, 0, :], wag[0:64, 0, :], ACT.Tanh).then_inc(squashed.sem, 1)
            act.activation(wag[:, 1, :], wag[:, 1, :], ACT.Sigmoid).then_inc(squashed.sem, 1)
            if layer:
                act.wait_ge(lora_in.sem, lora_in.at(1))
                act.activation(vl, ps[7][0:32, :], ACT.Copy).then_inc(lora_in_taken.sem, 1)
            for m in range(4 * len(kinds)):
                kind, t = kinds[m // 4], m % 4
                act.wait_ge(low.sem, low.at(m + 1))
                if kind == "g":
                    act.activation(gate[:, t, :], ps[m % 4][:, :], ACT.Copy).then_inc(low_taken.sem, 1)
                else:
                    out, bias = {"v": (e, "v0"), "w": (lw, "w0"), "a": (av, "a0")}[kind]
                    act.activation(out[:, t, :], ps[m % 4][:, :], ACT.Sigmoid,
                                   bias=vec(pg, bias)[:, t:t + 1]).then_inc(low_taken.sem, 1)
            act.wait_ge(kk_made.sem, kk_made.at(1))
            for t in range(KH):
                act.activation(e[:, t, :], kk[:, t, :], ACT.Square).then_inc(kk_squared.sem, 1)
            act.wait_ge(kk_summed.sem, kk_summed.at(1))
            for t in range(KH):
                last = act.activation(e[:, t, :], ps[4 + t][:, :], ACT.Sqrt)
            last.then_inc(kk_rooted.sem, 1)
            act.wait_ge(logs_made.sem, logs_made.at(1))
            act.activation(lw[:, :, :], lw[:, :, :], ACT.Exp)
            link(act.activation(e[:, :, :], cum[:, :, :], ACT.Exp))
            act.activation(cum[:, :, :], cum[:, :, :], ACT.Exp, scale=-1.0).then_inc(exps_made.sem, 1)

        @block.vector
        def _(dve):
            link = linker(dve, vec_step)
            if layer:
                dve.wait_ge(low_taken.sem, low_taken.at(4))
                difference = r["bonus"]
                link(dve.tensor_tensor(difference[:, :, :], pg.v_first[:, :, :], v[:, :, :], ALU.subtract))
                link(dve.tensor_tensor(e[:, :, :], difference[:, :, :], e[:, :, :], ALU.mult))
                link(dve.tensor_tensor(v[:, :, :], v[:, :, :], e[:, :, :], ALU.add))
            dve.wait_ge(low_taken.sem, low_taken.at(4 * len(kinds)))
            link(dve.tensor_scalar(lw[:, :, :], lw[:, :, :], DECAY_SCALE, None, ALU.mult))
            for t in range(KH):
                dve.tensor_tensor_scan(cum[:, t, :], pg.c["chunk_keep"][:, :], lw[:, t, :], 0.0, ALU.mult, ALU.add)
            for t in range(KH):
                last = dve.tensor_scalar(kk[:, t, :], kT[:, t, :], vec(pg, "kk")[:, t:t + 1], None, ALU.mult)
            link(last)
            dve.sem_inc(kk_made.sem, 1)
            link(dve.tensor_tensor(lw[:, :, :], cum[:, :, :], lw[:, :, :], ALU.subtract))
            dve.wait_ge(kk_rooted.sem, kk_rooted.at(1))
            link(dve.tensor_scalar(e[:, :, :], e[:, :, :], 1e-12, None, ALU.max))
            link(dve.reciprocal(e[:, :, :], e[:, :, :]))
            link(dve.tensor_tensor(kk[:, :, :], kk[:, :, :], e[:, :, :], ALU.mult))
            for t in range(KH):
                last = dve.tensor_scalar(e[:, t, :], av[:, t, :], -1.0, vec(pg, "ka")[:, t:t + 1], ALU.add, ALU.mult)
            link(last)
            link(dve.scalar_tensor_tensor(out=kT, in0=e[:, :, :], scalar=1.0, in1=kT, op0=ALU.add, op1=ALU.mult))
            dve.sem_inc(logs_made.sem, 1)
            dve.wait_ge(exps_made.sem, exps_made.at(1))
            ar = r["ar"]
            view = lambda x: x.rearrange("p t (b s) -> p t b s", s=P)
            chunks = lambda x: x.rearrange("p t (n s) -> p t n s", s=CH)
            for t in range(KH):
                dve.scalar_tensor_tensor(out=ar[:, t, :, 0, :], in0=view(kk[:, :, :])[:, t], scalar=-1.0,
                                         in1=view(lw[:, :, :])[:, t], op0=ALU.mult, op1=ALU.mult)
                dve.tensor_tensor(ar[:, t, :, 1, :], view(rT)[:, t], view(e[:, :, :])[:, t], ALU.mult)
            link(dve.tensor_copy(r["p_end"][:, :, :], chunks(e[:, :, :])[:, :, :, CH - 1]))
            link(dve.tensor_tensor(kk[:, :, :], kk[:, :, :], av[:, :, :], ALU.mult))
            link(dve.tensor_tensor(r["b"][:, :, :], kk[:, :, :], cum[:, :, :], ALU.mult))
            link(dve.tensor_tensor(r["k"][:, :, :], kT, cum[:, :, :], ALU.mult))
            for x in ("b", "k"):
                for t in range(KH):
                    dve.tensor_tensor(chunks(r[x + "_end"][:, :, :])[:, t], chunks(r[x][:, :, :])[:, t],
                                      r["p_end"][:, t, :].rearrange("p (n a) -> p n a", a=1).to_broadcast([P, NCH, CH]),
                                      ALU.mult)
            link(dve.tensor_tensor(e[:, :, :], rT, kT, ALU.mult))
            for t in range(KH):
                last = dve.tensor_scalar(e[:, t, :], e[:, t, :], vec(pg, "rk")[:, t:t + 1], None, ALU.mult)
            link(last)
            dve.sem_inc(rk_made.sem, 1)
            dve.wait_ge(rk_summed.sem, rk_summed.at(1))
            for t in range(KH):
                last = dve.tensor_tensor(r["bonus"][:, t, :], ps[t][:, :], v[:, t, :], ALU.mult)
            link(last)
    small_loaded.passed(16 * loads)
    squashed.passed(2)
    for s in (low, low_taken):
        s.passed(4 * len(kinds))
    kk_squared.passed(KH)
    for s in (kk_made, kk_summed, kk_rooted, logs_made, exps_made, rk_made, rk_summed) + \
            ((lora_in, lora_in_taken) if layer else ()):
        s.passed(1)


LEVELS = 5
TOK, GRAM, LOW = 1, 2, 3
INNER = lambda level: 2 + 2 * level
OUTER = lambda level: 3 + 2 * level
AKV, XZ, RQ, Y, FH = 14, 15, 16, 17, 18
BATCHES = 18
V_GRAM, V_LOW = 1, 2
V_INNER = lambda level: 1 + 2 * level
V_OUTER = lambda level: 2 + 2 * level
V_RQ, V_F = 13, 14
V_BATCHES = 14
A_TOK, A_AKV, A_XZ, A_Y, A_H = 1, 2, 3, 4, 5
A_BATCHES = 5


def rwkv_chunks(pg, r, st):
    nc, c = pg.nc, pg.c
    done, v_taken, a_taken = pg.counts("chunk_summed"), pg.counts("chunk_vector_taken"), pg.counts("chunk_scalar_taken")
    cleared, vec_step = pg.counts("chunk_cleared"), pg.counts("vec_step")
    groups = [(tb, pp) for tb in range(TB) for pp in range(2)]
    with ExitStack() as ctx:
        def buf(name, shape):
            return ctx.enter_context(pg.sbuf(name, shape, F32))
        tok = buf("tok", [P, 2, 4, P])
        gram = buf("gram", [P, 4, 4, P])
        low = buf("low", [P, 4, P])
        inv, invT, inner = (buf(n, [P, 4, P]) for n in ("inv", "invT", "inner"))
        akv = buf("akv", [P, 4, HEAD])
        xz = buf("xz", [P, 4, 2, HEAD])
        ps = [ctx.enter_context(pg.psum(f"chunk_ps{b}", [P, 4, P], F32)) for b in range(8)]
        block = ctx.enter_context(nc.Block())

        def units(pp):
            return [(u, 2 * pp + u // 2, u // 2, u % 2, slice(64 * (u % 2), 64 * (u % 2) + 64)) for u in range(4)]

        @block.gpsimd
        def _(pool):
            pool.memset(st["f"][:, :, :, :], 0.0).then_inc(cleared.sem, 1)
            pool.memset(st["hh"][:, :, :, :], 0.0).then_inc(cleared.sem, 1)

        @block.tensor
        def _(pe):
            for g, (tb, pp) in enumerate(groups):
                tok_s = slice(tb * P, (tb + 1) * P)
                D0, V0, A0 = done.at(g * BATCHES), v_taken.at(g * V_BATCHES), a_taken.at(g * A_BATCHES)
                if g:
                    pe.wait_ge(v_taken.sem, V0)
                    pe.wait_ge(a_taken.sem, A0)
                for q in range(2):
                    p = 2 * pp + q
                    for j, x in enumerate((r["ar"][:, p, tb, 0, :], r["b_end"][:, p, tok_s], r["k_end"][:, p, tok_s],
                                           r["v"][:, p, tok_s])):
                        last = pe.transpose(ps[q][:, j, :], x, c["ident"][:, :])
                last.then_inc(done.sem, 1)
                for u, p, q, hh, hs in units(pp):
                    rhs = r["ar"][hs, p, tb, :, :]
                    pe.matmul(ps[2 + u][:, 0:2, :], r["b"][hs, p, tok_s], rhs, start=True, stop=True)
                    last = pe.matmul(ps[2 + u][:, 2:4, :], r["k"][hs, p, tok_s], rhs, start=True, stop=True)
                last.then_inc(done.sem, 1)
                for u, p, q, hh, hs in units(pp):
                    last = pe.matmul(ps[6 + hh][:, q, :], r["ar"][hs, p, tb, 0, :], r["b"][hs, p, tok_s],
                                     start=True, stop=True)
                last.then_inc(done.sem, 1)
                for lv in range(1, LEVELS + 1):
                    pe.wait_ge(v_taken.sem, V0 + (V_OUTER(lv - 1) if lv > 1 else V_LOW))
                    for u in range(4):
                        last = pe.matmul(ps[2][:, u, :], low[:, u, :], invT[:, u, :], start=True, stop=True)
                    last.then_inc(done.sem, 1)
                    pe.wait_ge(v_taken.sem, V0 + V_INNER(lv))
                    for u in range(4):
                        last = pe.matmul(ps[3][:, u, :], inv[:, u, :], inner[:, u, :], start=True, stop=True)
                    if lv < LEVELS:
                        for u in range(4):
                            last = pe.matmul(ps[4][:, u, :], inner[:, u, :], inv[:, u, :], start=True, stop=True)
                    last.then_inc(done.sem, 1)
                pe.wait_ge(a_taken.sem, A0 + A_TOK)
                for u, p, q, hh, hs in units(pp):
                    last = pe.matmul(ps[5][:, u, 0:HEAD], gram[:, u, 2, :], tok[:, q, 3, hs], start=True, stop=True)
                last.then_inc(done.sem, 1)
                pe.wait_ge(v_taken.sem, V0 + V_OUTER(LEVELS))
                pe.wait_ge(a_taken.sem, A0 + A_AKV)
                for u, p, q, hh, hs in units(pp):
                    pe.matmul(ps[6][:, u, 0:HEAD], invT[:, u, :], tok[:, q, 0, hs], start=True, stop=True)
                    last = pe.matmul(ps[6][:, u, HEAD:P], invT[:, u, :], akv[:, u, :], start=True, stop=True)
                last.then_inc(done.sem, 1)
                pe.wait_ge(a_taken.sem, A0 + A_XZ)
                for u, p, q, hh, hs in units(pp):
                    last = pe.matmul(ps[7][hs, q, :], xz[:, u, 0, :], gram[:, u, 1, :], start=True, stop=True)
                last.then_inc(done.sem, 1)
                for u, p, q, hh, hs in units(pp):
                    pe.matmul(ps[0][hs, q, :], xz[:, u, 1, :], gram[:, u, 1, :], start=True, stop=False)
                    last = pe.matmul(ps[0][hs, q, :], tok[:, q, 3, hs], gram[:, u, 3, :], start=False, stop=True)
                last.then_inc(done.sem, 1)
                for ch in range(2):
                    rows, f_bank, h_bank = slice(64 * ch, 64 * ch + 64), ps[2 + ch], ps[4 + ch]
                    for u, p, q, hh, hs in units(pp):
                        pe.matmul(f_bank[hs, q, 0:HEAD], xz[rows, u, 0, :], tok[rows, q, 1, hs], start=True, stop=True)
                        pe.matmul(h_bank[hs, q, 0:HEAD], tok[rows, q, 1, hs], xz[rows, u, 1, :], start=True, stop=False)
                        last = pe.matmul(h_bank[hs, q, 0:HEAD], tok[rows, q, 2, hs], tok[rows, q, 3, hs],
                                         start=False, stop=True)
                last.then_inc(done.sem, 1)

        @block.vector
        def _(dve):
            link = linker(dve, vec_step)
            four = lambda x: x.rearrange("p (a n) -> p a n", a=1).to_broadcast([P, 4, P])
            for g, (tb, pp) in enumerate(groups):
                D0 = done.at(g * BATCHES)
                dve.wait_ge(done.sem, D0 + GRAM)
                for u in range(4):
                    last = dve.tensor_tensor(gram[:, u, :, :], ps[2 + u][:, :, :], c["gram_mask"][:, :, :], ALU.mult)
                last.then_inc(v_taken.sem, 1)
                dve.wait_ge(v_taken.sem, v_taken.at(g * V_BATCHES + V_GRAM))
                link(dve.tensor_tensor(invT[:, :, :], gram[:, :, 0, :], four(c["level_mask"][:, 0, :]), ALU.mult))
                link(dve.tensor_tensor(invT[:, :, :], invT[:, :, :], four(c["ident"][:, :]), ALU.add))
                dve.wait_ge(done.sem, D0 + LOW)
                for u in range(4):
                    last = dve.tensor_tensor(low[:, u, :], ps[6 + u % 2][:, u // 2, :], c["lower_mask"][:, :], ALU.mult)
                link(last)
                link(dve.tensor_tensor(inv[:, :, :], low[:, :, :], four(c["level0_lower"][:, :]), ALU.mult))
                dve.tensor_tensor(inv[:, :, :], inv[:, :, :], four(c["ident"][:, :]), ALU.add).then_inc(v_taken.sem, 1)
                for lv in range(1, LEVELS + 1):
                    dve.wait_ge(done.sem, D0 + INNER(lv))
                    dve.tensor_tensor(inner[:, :, :], ps[2][:, :, :], four(c["level_mask"][:, lv, :]), ALU.mult) \
                        .then_inc(v_taken.sem, 1)
                    dve.wait_ge(done.sem, D0 + OUTER(lv))
                    dve.wait_ge(v_taken.sem, v_taken.at(g * V_BATCHES) + V_INNER(lv))
                    last = dve.tensor_tensor(invT[:, :, :], invT[:, :, :], ps[3][:, :, :], ALU.add)
                    if lv < LEVELS:
                        last = dve.tensor_tensor(inv[:, :, :], inv[:, :, :], ps[4][:, :, :], ALU.add)
                    last.then_inc(v_taken.sem, 1)
                dve.wait_ge(done.sem, D0 + RQ)
                dve.tensor_tensor(st["rq"][:, 2 * pp:2 * pp + 2, tb * P:(tb + 1) * P], ps[7][:, 0:2, :],
                                  r["ar"][:, 2 * pp:2 * pp + 2, tb, 1, :], ALU.add).then_inc(v_taken.sem, 1)
                if g == 0:
                    dve.wait_ge(cleared.sem, cleared.at(2))
                dve.wait_ge(done.sem, D0 + FH)
                for ch in range(2):
                    for u, p, q, hh, hs in units(pp):
                        last = dve.scalar_tensor_tensor(
                            out=st["f"][hs, 2 * tb + ch, p, hs], in0=c["ident"][hs, hs],
                            scalar=r["p_end"][hs, p, 2 * tb + ch:2 * tb + ch + 1], in1=ps[2 + ch][hs, q, 0:HEAD],
                            op0=ALU.mult, op1=ALU.add)
                last.then_inc(v_taken.sem, 1)

        @block.scalar
        def _(act):
            for g, (tb, pp) in enumerate(groups):
                D0 = done.at(g * BATCHES)
                act.wait_ge(done.sem, D0 + TOK)
                for q in range(2):
                    last = act.activation(tok[:, q, :, :], ps[q][:, :, :], ACT.Copy)
                last.then_inc(a_taken.sem, 1)
                act.wait_ge(done.sem, D0 + AKV)
                act.activation(akv[:, :, :], ps[5][:, :, 0:HEAD], ACT.Copy).then_inc(a_taken.sem, 1)
                act.wait_ge(done.sem, D0 + XZ)
                act.activation(xz[:, :, :, :].rearrange("p u a n -> p u (a n)"), ps[6][:, :, :], ACT.Copy) \
                    .then_inc(a_taken.sem, 1)
                act.wait_ge(done.sem, D0 + Y)
                act.activation(st["y"][:, 2 * pp:2 * pp + 2, tb * P:(tb + 1) * P], ps[0][:, 0:2, :], ACT.Copy) \
                    .then_inc(a_taken.sem, 1)
                if g == 0:
                    act.wait_ge(cleared.sem, cleared.at(2))
                act.wait_ge(done.sem, D0 + FH)
                for ch in range(2):
                    for hh in range(2):
                        hs = slice(64 * hh, 64 * hh + 64)
                        last = act.activation(st["hh"][hs, 2 * tb + ch, 2 * pp:2 * pp + 2, hs],
                                              ps[4 + ch][hs, 0:2, 0:HEAD], ACT.Copy)
                last.then_inc(a_taken.sem, 1)
    n = len(groups)
    done.passed(BATCHES * n)
    v_taken.passed(V_BATCHES * n)
    a_taken.passed(A_BATCHES * n)
    cleared.passed(2)


def rwkv_states(pg, st):
    nc = pg.nc
    moved, stepped = pg.counts("state_multiplied"), pg.counts("state_stepped")
    y_summed, y_taken = pg.counts("y_summed"), pg.counts("y_taken")
    with ExitStack() as ctx:
        ps = [ctx.enter_context(pg.psum(f"state_ps{b}", [P, KH, P], F32)) for b in range(2)]
        yps = [ctx.enter_context(pg.psum(f"state_yps{t}", [P, T], F32)) for t in range(KH)]
        block = ctx.enter_context(nc.Block())

        @block.tensor
        def _(pe):
            for n in range(1, NCH):
                if n >= 2:
                    pe.wait_ge(stepped.sem, stepped.at(n - 1))
                for p in range(KH):
                    last = pe.matmul(ps[n % 2][:, p, :], st["f"][:, n, p, :], st["hh"][:, n - 1, p, :],
                                     start=True, stop=True)
                last.then_inc(moved.sem, 1)
                for t in range(KH):
                    last = pe.matmul(yps[t][:, n * CH:(n + 1) * CH], st["hh"][:, n - 1, t, :],
                                     st["rq"][:, t, n * CH:(n + 1) * CH], start=True, stop=True)
                if n == NCH - 1:
                    last.then_inc(y_summed.sem, 1)

        @block.vector
        def _(dve):
            for n in range(1, NCH):
                dve.wait_ge(moved.sem, moved.at(n))
                dve.tensor_tensor(st["hh"][:, n, :, :], st["hh"][:, n, :, :], ps[n % 2][:, :, :], ALU.add) \
                    .then_inc(stepped.sem, 1)
            dve.wait_ge(y_summed.sem, y_summed.at(1))
            for t in range(KH):
                last = dve.tensor_tensor(st["y"][:, t, CH:T], st["y"][:, t, CH:T], yps[t][:, CH:T], ALU.add)
            last.then_inc(y_taken.sem, 1)
    moved.passed(NCH - 1)
    stepped.passed(NCH - 1)
    y_summed.passed(1)
    y_taken.passed(1)


def rwkv_finish(pg, r, st, mixT):
    nc, y, v = pg.nc, st["y"], st["rq"]
    summed, squared, rooted = pg.counts("gn_summed"), pg.counts("gn_squared"), pg.counts("gn_rooted")
    centred, varied = pg.counts("gn_centred"), pg.counts("gn_varied")
    vec_step = pg.counts("vec_step")
    with ExitStack() as ctx:
        ps = [ctx.enter_context(pg.psum(f"gn_ps{b}", [P, T], F32)) for b in range(8)]
        block = ctx.enter_context(nc.Block())

        @block.tensor
        def _(pe):
            for t in range(KH):
                last = pe.matmul(ps[t][:, :], pg.c["head_ones"][:, :], y[:, t, :], start=True, stop=True)
            last.then_inc(summed.sem, 1)
            pe.wait_ge(squared.sem, squared.at(1))
            for t in range(KH):
                last = pe.matmul(ps[4 + t][:, :], pg.c["head_ones"][:, :], v[:, t, :], start=True, stop=True)
            last.then_inc(summed.sem, 1)

        @block.scalar
        def _(act):
            act.wait_ge(centred.sem, centred.at(1))
            act.activation(v[:, :, :], y[:, :, :], ACT.Square).then_inc(squared.sem, 1)
            act.wait_ge(varied.sem, varied.at(1))
            act.activation(v[:, :, :], v[:, :, :], ACT.Sqrt).then_inc(rooted.sem, 1)

        @block.vector
        def _(dve):
            link = linker(dve, vec_step)
            dve.wait_ge(summed.sem, summed.at(1))
            for t in range(KH):
                last = dve.scalar_tensor_tensor(out=y[:, t, :], in0=ps[t][:, :], scalar=-1.0 / HEAD, in1=y[:, t, :],
                                                op0=ALU.mult, op1=ALU.add)
            link(last)
            dve.sem_inc(centred.sem, 1)
            dve.wait_ge(summed.sem, summed.at(2))
            for t in range(KH):
                last = dve.tensor_scalar(v[:, t, :], ps[4 + t][:, :], 1.0 / HEAD, GN_EPS, ALU.mult, ALU.add)
            link(last)
            dve.sem_inc(varied.sem, 1)
            dve.wait_ge(rooted.sem, rooted.at(1))
            link(dve.reciprocal(v[:, :, :], v[:, :, :]))
            link(dve.tensor_tensor(y[:, :, :], y[:, :, :], v[:, :, :], ALU.mult))
            for t in range(KH):
                last = dve.tensor_scalar(y[:, t, :], y[:, t, :], vec(pg, "lnx_g")[:, t:t + 1],
                                         vec(pg, "lnx_b")[:, t:t + 1], ALU.mult, ALU.add)
            link(last)
            link(dve.tensor_tensor(y[:, :, :], y[:, :, :], r["bonus"][:, :, :], ALU.add))
            link(dve.tensor_tensor(mixT[:, 0:KH, :], y[:, :, :], mixT[:, 0:KH, :], ALU.mult))
    summed.passed(2)
    for s in (squared, rooted, centred, varied):
        s.passed(1)


def s5(pg, layer, mixT):
    nc = pg.nc
    with ExitStack() as whole:
        def buf(own, name, shape):
            return own.enter_context(pg.sbuf(name, shape, F32))
        s = {n: buf(whole, n, sh) for n, sh in (
            ("e_in", [P, 2, SC, 4, P]),
            ("g_re", [P, SC + 1, S5_PAIRS, 32]), ("g_im", [P, SC + 1, S5_PAIRS, 32]),
            ("taps", [P, 4, SC, P]), ("rot", [P, 2, S5_PAIRS, SN]), ("keep", [P, S5_PAIRS, SN]))}
        s5_tables(pg, layer, s)
        s5_run(pg, layer, s, mixT)


def s5_tables(pg, layer, s):
    nc, dram = pg.nc, pg.dram
    loaded, cleared = pg.counts("s5_loaded"), pg.counts("s5_cleared")
    dt_made, ready, trig = pg.counts("s5_dt_made"), pg.counts("s5_angles_made"), pg.counts("s5_trig_made")
    powers, in_made, out_made = pg.counts("s5_powers_made"), pg.counts("s5_in_made"), pg.counts("s5_out_made")
    flipped, flip_taken = pg.counts("s5_flipped"), pg.counts("s5_flip_taken")
    tapped, vec_step, pool_step = pg.counts("s5_tapped"), pg.counts("vec_step"), pg.counts("pool_step")
    taps_cleared = pg.counts("s5_taps_cleared")
    with ExitStack() as ctx:
        def buf(name, shape):
            return ctx.enter_context(pg.sbuf(name, shape, F32))
        small = buf("s5_small", [P, 24, S5_PAIRS])
        are, aim, dt, lre, ang, ang8, cosv, sinv, mag, den, c1r, c1i, t0, t1, t2, t3, cos8, sin8, m8, er, ei, sq8 = \
            (small[:, i, :] for i in range(22))
        lam = buf("s5_lam", [P, 2, SC + 1, S5_PAIRS])
        b_raw, c_raw = buf("s5_b_raw", [P, 2, S5_PAIRS, 32]), buf("s5_c_raw", [P, 2, S5_PAIRS, 32])
        bb = buf("s5_bb", [P, 2, S5_PAIRS, 32])
        lb = buf("s5_lb", [P, 2, SC, S5_PAIRS, 32])
        tmp_v = buf("s5_tmp_v", [P, 2, S5_PAIRS * 32])
        tmp_p = buf("s5_tmp_p", [P, 2, S5_PAIRS * 32])
        ps = [ctx.enter_context(pg.psum(f"s5t_ps{b}", [P, 4, P], F32)) for b in range(8)]
        block = ctx.enter_context(nc.Block())

        @block.sync
        def _(sp):
            for x, n in ((are, "s5_are"), (aim, "s5_aim"), (dt, "s5_dt")):
                sp.dma_start(x, dram[n][layer]).then_inc(loaded.sem, 16)
            sp.wait_ge(cleared.sem, cleared.at(2))
            for raw, names in ((b_raw, ("s5_bre", "s5_bim")), (c_raw, ("s5_cre", "s5_cim"))):
                for part, n in enumerate(names):
                    view = dram[n][layer].rearrange("(q g) p c -> g p q c", g=2)
                    for g in range(2):
                        sp.dma_start(raw[64 * g:64 * g + 64, part, :, 16 * g:16 * g + 16], view[g]).then_inc(loaded.sem, 16)

        @block.scalar
        def _(act):
            act.wait_ge(loaded.sem, loaded.at(16 * 11))
            act.activation(dt, dt, ACT.Exp).then_inc(dt_made.sem, 1)
            act.wait_ge(ready.sem, ready.at(1))
            act.activation(mag, t0, ACT.Exp)
            act.activation(m8, t0, ACT.Exp, scale=8.0).then_inc(trig.sem, 1)
            act.activation(sinv, t1, ACT.Sin)
            act.activation(cosv, t2, ACT.Sin).then_inc(trig.sem, 1)
            act.wait_ge(ready.sem, ready.at(2))
            act.activation(sin8, t1, ACT.Sin)
            act.activation(cos8, t2, ACT.Sin).then_inc(trig.sem, 1)
            for m in range(16):
                act.wait_ge(flipped.sem, flipped.at(m + 1))
                act.activation(s["e_in"][:, m // 8, m % 8, :, :], ps[m % 4][:, :, :], ACT.Copy).then_inc(flip_taken.sem, 1)

        @block.tensor
        def _(pe):
            for m in range(16):
                part, k = m // 8, m % 8
                if m >= 4:
                    pe.wait_ge(flip_taken.sem, flip_taken.at(m - 3))
                if m == 0:
                    pe.wait_ge(in_made.sem, in_made.at(1))
                for t in range(4):
                    last = pe.transpose(ps[m % 4][:, t, :],
                                        lb[:, part, SC - 1 - k, 4 * t:4 * t + 4, :].rearrange("p q c -> p (q c)"),
                                        pg.c["ident"][:, :])
                last.then_inc(flipped.sem, 1)
            pe.wait_ge(out_made.sem, out_made.at(1))
            for q in range(S5_PAIRS):
                rows = slice(32 * (q % 4), 32 * (q % 4) + 32)
                o = ps[4 + q // 4][rows, :, :].rearrange("p a n -> p (a n)")[:, 0:SC * 32]
                pe.matmul(o, bb[:, 0, q, :], s["g_re"][:, 0:SC, q, :], start=True, stop=False)
                last = pe.matmul(o, bb[:, 1, q, :], s["g_im"][:, 0:SC, q, :], start=False, stop=True)
            last.then_inc(tapped.sem, 1)

        @block.gpsimd
        def _(pool):
            link = linker(pool, pool_step)
            pool.memset(b_raw[:, :, :, :], 0.0).then_inc(cleared.sem, 1)
            pool.memset(c_raw[:, :, :, :], 0.0).then_inc(cleared.sem, 1)
            pool.memset(s["taps"][:, :, :, :], 0.0).then_inc(taps_cleared.sem, 1)
            pool.wait_ge(powers.sem, powers.at(1))
            for k in range(SC):
                lr, li = (lam[:, part, k, :].rearrange("p (q a) -> p q a", a=1).to_broadcast([P, S5_PAIRS, 32])
                          for part in range(2))
                ta, tb = (tmp_p[:, j, :].rearrange("p (q c) -> p q c", c=32) for j in range(2))
                pool.tensor_tensor(ta, bb[:, 0], lr, ALU.mult)
                link(pool.tensor_tensor(tb, bb[:, 1], li, ALU.mult))
                link(pool.tensor_tensor(lb[:, 0, k], ta, tb, ALU.subtract))
                pool.tensor_tensor(ta, bb[:, 0], li, ALU.mult)
                link(pool.tensor_tensor(tb, bb[:, 1], lr, ALU.mult))
                link(pool.tensor_tensor(lb[:, 1, k], ta, tb, ALU.add))
            pool.sem_inc(in_made.sem, 1)

        @block.vector
        def _(dve):
            link = linker(dve, vec_step)
            tt = lambda o, a, b, op: link(dve.tensor_tensor(o, a, b, op))

            def reduce_angle(out, angle, shift):
                link(dve.tensor_scalar(t3, angle, shift, None, ALU.add))
                link(dve.tensor_scalar(den, t3, 1.0 / (2 * math.pi), None, ALU.mult))
                link(dve.tensor_scalar(den, den, ROUND, None, ALU.add))
                link(dve.tensor_scalar(den, den, -ROUND, None, ALU.add))
                link(dve.scalar_tensor_tensor(out=t3, in0=den, scalar=-TWO_PI_HI, in1=t3, op0=ALU.mult, op1=ALU.add))
                link(dve.scalar_tensor_tensor(out=t3, in0=den, scalar=-TWO_PI_LO, in1=t3, op0=ALU.mult, op1=ALU.add))
                link(dve.tensor_scalar(out, t3, PI_IN, -PI_IN, ALU.min, ALU.max))

            dve.wait_ge(dt_made.sem, dt_made.at(1))
            link(dve.tensor_scalar(lre, are, -1e-4, None, ALU.min))
            tt(t0, lre, dt, ALU.mult)
            tt(ang, aim, dt, ALU.mult)
            reduce_angle(t1, ang, 0.0)
            link(dve.tensor_copy(ang, t1))
            reduce_angle(t2, ang, math.pi / 2)
            dve.sem_inc(ready.sem, 1)
            dve.wait_ge(trig.sem, trig.at(2))
            link(dve.tensor_scalar(ang8, ang, float(SC), None, ALU.mult))
            reduce_angle(t1, ang8, 0.0)
            link(dve.tensor_copy(ang8, t1))
            reduce_angle(t2, ang8, math.pi / 2)
            dve.sem_inc(ready.sem, 1)
            link(dve.memset(lam[:, 0, 0, :], 1.0))
            link(dve.memset(lam[:, 1, 0, :], 0.0))
            tt(lam[:, 0, 1, :], mag, cosv, ALU.mult)
            tt(lam[:, 1, 1, :], mag, sinv, ALU.mult)
            dve.wait_ge(trig.sem, trig.at(3))
            lbr, lbi = lam[:, 0, 1, :], lam[:, 1, 1, :]
            tt(t0, lre, lre, ALU.mult)
            tt(t1, aim, aim, ALU.mult)
            tt(den, t0, t1, ALU.add)
            link(dve.reciprocal(den, den))
            link(dve.tensor_scalar(t3, lbr, -1.0, None, ALU.add))
            tt(t0, t3, lre, ALU.mult)
            tt(t1, lbi, aim, ALU.mult)
            tt(t0, t0, t1, ALU.add)
            tt(c1r, t0, den, ALU.mult)
            tt(t0, lbi, lre, ALU.mult)
            tt(t1, t3, aim, ALU.mult)
            tt(t0, t0, t1, ALU.subtract)
            tt(c1i, t0, den, ALU.mult)
            for k in range(2, SC + 1):
                a, b = lam[:, 0, k - 1, :], lam[:, 1, k - 1, :]
                tt(t0, a, lbr, ALU.mult)
                tt(t1, b, lbi, ALU.mult)
                tt(lam[:, 0, k, :], t0, t1, ALU.subtract)
                tt(t0, a, lbi, ALU.mult)
                tt(t1, b, lbr, ALU.mult)
                tt(lam[:, 1, k, :], t0, t1, ALU.add)
            wide = lambda x: x.rearrange("p (q a) -> p q a", a=1).to_broadcast([P, S5_PAIRS, 32])
            ta, tb = (tmp_v[:, j, :].rearrange("p (q c) -> p q c", c=32) for j in range(2))
            dve.wait_ge(loaded.sem, loaded.at(16 * 11))
            tt(ta, b_raw[:, 0], wide(c1r), ALU.mult)
            tt(tb, b_raw[:, 1], wide(c1i), ALU.mult)
            tt(bb[:, 0], ta, tb, ALU.subtract)
            tt(ta, b_raw[:, 1], wide(c1r), ALU.mult)
            tt(tb, b_raw[:, 0], wide(c1i), ALU.mult)
            tt(bb[:, 1], ta, tb, ALU.add)
            dve.sem_inc(powers.sem, 1)
            for k in range(SC + 1):
                lr, li = wide(lam[:, 0, k, :]), wide(lam[:, 1, k, :])
                tt(ta, c_raw[:, 0], lr, ALU.mult)
                tt(tb, c_raw[:, 1], li, ALU.mult)
                tt(s["g_re"][:, k], ta, tb, ALU.subtract)
                tt(ta, c_raw[:, 0], li, ALU.mult)
                tt(tb, c_raw[:, 1], lr, ALU.mult)
                link(dve.scalar_tensor_tensor(out=s["g_im"][:, k], in0=ta, scalar=-1.0, in1=tb, op0=ALU.mult, op1=ALU.subtract))
            dve.sem_inc(out_made.sem, 1)
            rr, ri = s["rot"][:, 0], s["rot"][:, 1]
            link(dve.memset(rr[:, :, 0:1], 1.0))
            link(dve.memset(ri[:, :, 0:1], 0.0))
            link(dve.tensor_copy(er, cos8))
            link(dve.tensor_copy(ei, sin8))
            n = 1
            while n < SN:
                er_n, ei_n = (x.rearrange("p (q a) -> p q a", a=1).to_broadcast([P, S5_PAIRS, n]) for x in (er, ei))
                ta, tb = (tmp_v[:, j, 0:S5_PAIRS * n].rearrange("p (q c) -> p q c", c=n) for j in range(2))
                tt(ta, rr[:, :, 0:n], er_n, ALU.mult)
                tt(tb, ri[:, :, 0:n], ei_n, ALU.mult)
                tt(rr[:, :, n:2 * n], ta, tb, ALU.subtract)
                tt(ta, rr[:, :, 0:n], ei_n, ALU.mult)
                tt(tb, ri[:, :, 0:n], er_n, ALU.mult)
                tt(ri[:, :, n:2 * n], ta, tb, ALU.add)
                tt(t0, er, er, ALU.mult)
                tt(t1, ei, ei, ALU.mult)
                tt(t2, er, ei, ALU.mult)
                tt(er, t0, t1, ALU.subtract)
                tt(ei, t2, t2, ALU.add)
                n *= 2
            link(dve.tensor_copy(s["keep"][:, :, :], m8.rearrange("p (q a) -> p q a", a=1).to_broadcast([P, S5_PAIRS, SN])))
            link(dve.memset(s["keep"][:, :, 0:1], 0.0))
            dve.wait_ge(tapped.sem, tapped.at(1))
            dve.wait_ge(taps_cleared.sem, taps_cleared.at(1))
            for t in range(4):
                for g in range(4):
                    rows = slice(32 * g, 32 * g + 32)
                    last = dve.tensor_copy(s["taps"][rows, t, :, rows],
                                           ps[4 + t][rows, :, :].rearrange("p a n -> p (a n)")[:, 0:SC * 32]
                                           .rearrange("p (k n) -> p k n", n=32))
            link(last)
    loaded.passed(16 * 11)
    for x, k in ((cleared, 2), (dt_made, 1), (ready, 2), (trig, 3), (powers, 1), (in_made, 1), (out_made, 1),
                 (flipped, 16), (flip_taken, 16), (tapped, 1), (taps_cleared, 1)):
        x.passed(k)


def s5_run(pg, layer, s, mixT):
    nc = pg.nc
    uT = mixT[:, KH:KD, :]
    u8 = uT.rearrange("p t (n s) -> p t n s", s=SC)
    s_in, turned, scanned, x_made = (pg.counts(n) for n in ("s5_in_summed", "s5_turned", "s5_scanned", "s5_states_made"))
    y_in, skipped, gelued = pg.counts("s5_y_summed"), pg.counts("s5_skipped"), pg.counts("s5_gelued")
    cleared, vec_step = pg.counts("s5_state_cleared"), pg.counts("vec_step")
    with ExitStack() as ctx:
        def buf(name, shape):
            return ctx.enter_context(pg.sbuf(name, shape, F32))
        rot, sc, x = buf("s5_rot_in", [P, 2, S5_PAIRS, SN]), buf("s5_scan", [P, 2, S5_PAIRS, SN]), buf("s5_x", [P, 2, S5_PAIRS, SN + 1])
        tmp = buf("s5_tmp", [P, 2, S5_PAIRS, SN])
        yT = buf("s5_y", [P, KH, T])
        with ExitStack() as one:
            sps = [one.enter_context(pg.psum(f"s5s_ps{b}", [P, 4, 2, SN], F32)) for b in range(4)]
            yps = [one.enter_context(pg.psum(f"s5y_ps{b}", [P, SN, SC], F32)) for b in range(4)]
            block = one.enter_context(nc.Block())

            @block.gpsimd
            def _(pool):
                pool.memset(x[:, :, :, 0:1], 0.0).then_inc(cleared.sem, 1)

            @block.tensor
            def _(pe):
                for t in range(4):
                    for part in range(2):
                        for g in range(4):
                            rows = slice(32 * g, 32 * g + 32)
                            for k in range(SC):
                                last = pe.matmul(sps[g][:, t, part, :], s["e_in"][rows, part, k, t, :],
                                                 u8[rows, t, :, k], start=(k == 0), stop=(k == SC - 1))
                last.then_inc(s_in.sem, 1)
                for t in range(4):
                    for k in range(SC):
                        pe.matmul(yps[t][:, :, k:SC], s["taps"][:, t, k, :], u8[:, t, :, 0:SC - k],
                                  start=(k == 0), stop=False, skip_group_check=True)
                    if t == 0:
                        pe.wait_ge(x_made.sem, x_made.at(1))
                        pe.wait_ge(cleared.sem, cleared.at(1))
                    for g in range(4):
                        q, rows = 4 * t + g, slice(32 * g, 32 * g + 32)
                        for k in range(SC):
                            pe.matmul(yps[t][rows, :, k], s["g_re"][:, k + 1, q, :], x[:, 0, q, 0:SN],
                                      start=False, stop=False, skip_group_check=True)
                            last = pe.matmul(yps[t][rows, :, k], s["g_im"][:, k + 1, q, :], x[:, 1, q, 0:SN],
                                             start=False, stop=True, skip_group_check=True)
                    last.then_inc(y_in.sem, 1)

            @block.vector
            def _(dve):
                link = linker(dve, vec_step)
                tt = lambda o, a, b, op: link(dve.tensor_tensor(o, a, b, op))
                dve.wait_ge(s_in.sem, s_in.at(1))
                by_row = lambda v: v.rearrange("p (t g) n -> p g t n", g=4)
                for g in range(4):
                    sr, si = sps[g][:, :, 0, :], sps[g][:, :, 1, :]
                    cr, ci = by_row(s["rot"][:, 0])[:, g], by_row(s["rot"][:, 1])[:, g]
                    dve.tensor_tensor(by_row(tmp[:, 0])[:, g], sr, cr, ALU.mult)
                    dve.tensor_tensor(by_row(tmp[:, 1])[:, g], si, ci, ALU.mult)
                    dve.tensor_tensor(by_row(sc[:, 0])[:, g], sr, ci, ALU.mult)
                    last = dve.tensor_tensor(by_row(sc[:, 1])[:, g], si, cr, ALU.mult)
                link(last)
                dve.tensor_tensor(rot[:, 0], tmp[:, 0], tmp[:, 1], ALU.add)
                tt(rot[:, 1], sc[:, 1], sc[:, 0], ALU.subtract)
                flat = lambda v: v.rearrange("p q n -> p (q n)")
                for part in range(2):
                    last = dve.tensor_tensor_scan(flat(sc[:, part]), flat(s["keep"][:, :, :]), flat(rot[:, part]),
                                                  0.0, ALU.mult, ALU.add)
                link(last)
                dve.tensor_tensor(tmp[:, 0], sc[:, 0], s["rot"][:, 0], ALU.mult)
                tt(tmp[:, 1], sc[:, 1], s["rot"][:, 1], ALU.mult)
                dve.tensor_tensor(x[:, 0, :, 1:SN + 1], tmp[:, 0], tmp[:, 1], ALU.subtract)
                dve.tensor_tensor(rot[:, 0], sc[:, 0], s["rot"][:, 1], ALU.mult)
                tt(rot[:, 1], sc[:, 1], s["rot"][:, 0], ALU.mult)
                tt(x[:, 1, :, 1:SN + 1], rot[:, 0], rot[:, 1], ALU.add)
                dve.sem_inc(x_made.sem, 1)
                for t in range(4):
                    dve.wait_ge(y_in.sem, y_in.at(t + 1))
                    dve.scalar_tensor_tensor(out=yT[:, t, :], in0=uT[:, t, :], scalar=vec(pg, "s5_d")[:, t:t + 1],
                                             in1=yps[t][:, :, :].rearrange("p n s -> p (n s)"),
                                             op0=ALU.mult, op1=ALU.add).then_inc(skipped.sem, 1)

            @block.scalar
            def _(act):
                for t in range(4):
                    act.wait_ge(skipped.sem, skipped.at(t + 1))
                    act.activation(yT[:, t, :], yT[:, t, :], ACT.Gelu_apprx_tanh).then_inc(gelued.sem, 1)
        glu = buf("s5_glu", [P, KH, T])
        project(pg, pg.dram["glu_w"][layer], KH, KH, yT, T, glu)
        s5_gate(pg, yT, glu, mixT)
    for a, k in ((s_in, 1), (x_made, 1), (y_in, 4), (skipped, 4), (gelued, 4), (cleared, 1)):
        a.passed(k)


def s5_gate(pg, yT, glu, mixT):
    nc = pg.nc
    gated, multiplied, squared, summed = (pg.counts(n) for n in ("glu_gated", "glu_multiplied", "glu_squared", "glu_summed"))
    meaned, rooted, vec_step = pg.counts("glu_meaned"), pg.counts("glu_rooted"), pg.counts("vec_step")
    with ExitStack() as ctx:
        rstd = ctx.enter_context(pg.sbuf("glu_rstd", [P, T], F32))
        ps = ctx.enter_context(pg.psum("glu_ps", [P, T], F32))
        block = ctx.enter_context(nc.Block())

        @block.scalar
        def _(act):
            for t in range(KH):
                act.activation(glu[:, t, :], glu[:, t, :], ACT.Sigmoid, bias=vec(pg, "glu_b")[:, t:t + 1]) \
                    .then_inc(gated.sem, 1)
            for t in range(KH):
                act.wait_ge(multiplied.sem, multiplied.at(t + 1))
                act.activation(glu[:, t, :], yT[:, t, :], ACT.Square).then_inc(squared.sem, 1)
            act.wait_ge(meaned.sem, meaned.at(1))
            act.activation(rstd[:, :], rstd[:, :], ACT.Sqrt).then_inc(rooted.sem, 1)

        @block.tensor
        def _(pe):
            for t in range(KH):
                pe.wait_ge(squared.sem, squared.at(t + 1))
                last = pe.matmul(ps[:, :], pg.c["ones"][:, :], glu[:, t, :], start=(t == 0), stop=(t == KH - 1))
            last.then_inc(summed.sem, 1)

        @block.vector
        def _(dve):
            link = linker(dve, vec_step)
            for t in range(KH):
                dve.wait_ge(gated.sem, gated.at(t + 1))
                dve.tensor_tensor(yT[:, t, :], yT[:, t, :], glu[:, t, :], ALU.mult).then_inc(multiplied.sem, 1)
            dve.wait_ge(summed.sem, summed.at(1))
            dve.tensor_scalar(rstd[:, :], ps[:, :], 1.0 / D_HALF, RMS_EPS, ALU.mult, ALU.add).then_inc(meaned.sem, 1)
            dve.wait_ge(rooted.sem, rooted.at(1))
            link(dve.reciprocal(rstd[:, :], rstd[:, :]))
            for t in range(KH):
                last = dve.scalar_tensor_tensor(out=mixT[:, KH + t, :], in0=yT[:, t, :],
                                                scalar=vec(pg, "out_g")[:, t:t + 1], in1=rstd[:, :],
                                                op0=ALU.mult, op1=ALU.mult)
            link(last)
    for a, k in ((gated, KH), (multiplied, KH), (squared, KH), (summed, 1), (meaned, 1), (rooted, 1)):
        a.passed(k)


def cross_attention(pg, layer):
    nc, dram = pg.nc, pg.dram
    loaded = pg.counts("mem_loaded")

    def buf(own, name, shape):
        return own.enter_context(pg.sbuf(name, shape, F32))

    with ExitStack() as whole:
        v = buf(whole, "xa_v", [P, 2, D])
        kT, qT, h = buf(whole, "xa_k", [P, KD, N_MEM]), buf(whole, "xa_q", [P, KD, T]), buf(whole, "xa_h", [P, KD, T])
        with ExitStack() as own:
            mem, mh = buf(own, "mem", [P, KD, N_MEM]), buf(own, "mem_h", [P, KD, N_MEM])
            with nc.Block() as block:
                @block.sync
                def _(sp):
                    sp.dma_start(mem[:, :, :], dram["memT"]).then_inc(loaded.sem, 16)
                    sp.wait_ge(loaded.sem, loaded.at(16))
            loaded.passed(16)
            norm(pg, mem, vec(pg, "norm_mem"), mh, N_MEM)
            project(pg, dram["xa_wk"][layer], KD, KD, mh, N_MEM, kT)
            memory_values(pg, layer, mh, v)
        norm(pg, pg.xT, vec(pg, "norm_xa"), h, T)
        project(pg, dram["xa_wq"][layer], KD, KD, h, T, qT)
        attend(pg, qT, kT, v, h)
        project(pg, dram["xa_wo"][layer], KD, KD, h, T, pg.xT, add=True)


def memory_values(pg, layer, mh, v):
    nc = pg.nc
    loaded, summed, taken = pg.counts("wv_loaded"), pg.counts("v_summed"), pg.counts("v_taken")
    with ExitStack() as ctx:
        w = ctx.enter_context(pg.sbuf("xa_wv", [P, KD, D], F32))
        ps = [ctx.enter_context(pg.psum(f"v_ps{b}", [P, T], F32)) for b in range(4)]
        block = ctx.enter_context(nc.Block())

        @block.sync
        def _(sp):
            sp.dma_start(w[:, :, :], pg.dram["xa_wv"][layer]).then_inc(loaded.sem, 16)

        @block.tensor
        def _(pe):
            pe.wait_ge(loaded.sem, loaded.at(16))
            for m in range(2):
                for half in range(2):
                    for k in range(KD):
                        last = pe.matmul(ps[2 * m + half][:, :], mh[:, k, m * P:(m + 1) * P],
                                         w[:, k, half * T:(half + 1) * T], start=(k == 0), stop=(k == KD - 1))
                    last.then_inc(summed.sem, 1)

        @block.scalar
        def _(act):
            for m in range(2):
                for half in range(2):
                    act.wait_ge(summed.sem, summed.at(2 * m + half + 1))
                    act.activation(v[:, m, half * T:(half + 1) * T], ps[2 * m + half][:, :], ACT.Copy) \
                        .then_inc(taken.sem, 1)
    loaded.passed(16)
    summed.passed(4)
    taken.passed(4)


def attend(pg, qT, kT, v, oT):
    nc = pg.nc
    scale = XA_HEAD ** -0.5
    scored, maxed, exped = pg.counts("xa_scored"), pg.counts("xa_maxed"), pg.counts("xa_exped")
    normed, flipped, flip_taken = pg.counts("xa_normed"), pg.counts("xa_flipped"), pg.counts("xa_flip_taken")
    mixed, mix_taken, vec_step = pg.counts("xa_mixed"), pg.counts("xa_mix_taken"), pg.counts("vec_step")
    units = [(hd, tb) for hd in range(XA_HEADS) for tb in range(TB)]
    n = len(units)
    with ExitStack() as ctx:
        def buf(name, shape):
            return ctx.enter_context(pg.sbuf(name, shape, F32))
        prob, probT = buf("xa_prob", [P, 2, N_MEM]), buf("xa_probT", [P, 2, 2, T])
        stats = buf("xa_stats", [P, 3, n])
        sps = [ctx.enter_context(pg.psum(f"xas_ps{b}", [P, N_MEM], F32)) for b in range(2)]
        fps = [ctx.enter_context(pg.psum(f"xaf_ps{b}", [P, 2, P], F32)) for b in range(2)]
        ops = [ctx.enter_context(pg.psum(f"xao_ps{b}", [P, T], F32)) for b in range(2)]
        block = ctx.enter_context(nc.Block())

        @block.tensor
        def _(pe):
            def scores(i):
                hd, tb = units[i]
                if i >= 2:
                    pe.wait_ge(exped.sem, exped.at(i - 1))
                for j in range(2):
                    last = pe.matmul(sps[i % 2][:, :], qT[:, 2 * hd + j, tb * P:(tb + 1) * P], kT[:, 2 * hd + j, :],
                                     start=(j == 0), stop=(j == 1))
                last.then_inc(scored.sem, 1)

            scores(0)
            for i, (hd, tb) in enumerate(units):
                if i + 1 < n:
                    scores(i + 1)
                pe.wait_ge(normed.sem, normed.at(i + 1))
                if i >= 2:
                    pe.wait_ge(flip_taken.sem, flip_taken.at(i - 1))
                for m in range(2):
                    last = pe.transpose(fps[i % 2][:, m, :], prob[:, i % 2, m * P:(m + 1) * P], pg.c["ident"][:, :])
                last.then_inc(flipped.sem, 1)
                if tb == TB - 1:
                    pe.wait_ge(flip_taken.sem, flip_taken.at(i + 1))
                    for j in range(2):
                        o = 2 * hd + j
                        if o >= 2:
                            pe.wait_ge(mix_taken.sem, mix_taken.at(o - 1))
                        for m in range(2):
                            last = pe.matmul(ops[j][:, :], v[:, m, o * P:(o + 1) * P], probT[:, hd % 2, m, :],
                                             start=(m == 0), stop=(m == 1))
                        last.then_inc(mixed.sem, 1)

        @block.vector
        def _(dve):
            link = linker(dve, vec_step)

            def maximum(i):
                dve.wait_ge(scored.sem, scored.at(i + 1))
                link(dve.reduce_max(stats[:, 0, i:i + 1], sps[i % 2][:, :], AX.X))
                dve.tensor_scalar(stats[:, 0, i:i + 1], stats[:, 0, i:i + 1], -scale, None, ALU.mult).then_inc(maxed.sem, 1)

            maximum(0)
            for i, (hd, tb) in enumerate(units):
                if i + 1 < n:
                    maximum(i + 1)
                dve.wait_ge(exped.sem, exped.at(i + 1))
                link(dve.reciprocal(stats[:, 2, i:i + 1], stats[:, 1, i:i + 1]))
                dve.tensor_scalar(prob[:, i % 2, :], prob[:, i % 2, :], stats[:, 2, i:i + 1], None, ALU.mult) \
                    .then_inc(normed.sem, 1)
                if tb == TB - 1:
                    for j in range(2):
                        o = 2 * hd + j
                        dve.wait_ge(mixed.sem, mixed.at(o + 1))
                        dve.tensor_copy(oT[:, o, :], ops[j][:, :]).then_inc(mix_taken.sem, 1)

        @block.scalar
        def _(act):
            def exponential(i):
                act.wait_ge(maxed.sem, maxed.at(i + 1))
                if i >= 2:
                    act.wait_ge(flipped.sem, flipped.at(i - 1))
                act.activation(prob[:, i % 2, :], sps[i % 2][:, :], ACT.Exp, bias=stats[:, 0, i:i + 1], scale=scale,
                               accum_out=stats[:, 1, i:i + 1]).then_inc(exped.sem, 1)

            exponential(0)
            for i, (hd, tb) in enumerate(units):
                if i + 1 < n:
                    exponential(i + 1)
                act.wait_ge(flipped.sem, flipped.at(i + 1))
                if tb == 0 and hd >= 2:
                    act.wait_ge(mixed.sem, mixed.at(2 * (hd - 1)))
                act.activation(probT[:, hd % 2, :, tb * P:(tb + 1) * P], fps[i % 2][:, :, :], ACT.Copy) \
                    .then_inc(flip_taken.sem, 1)
    for s in (scored, maxed, exped, normed, flipped, flip_taken):
        s.passed(n)
    mixed.passed(KD)
    mix_taken.passed(KD)


def peer(pg, layer):
    nc = pg.nc

    def buf(own, name, shape):
        return own.enter_context(pg.sbuf(name, shape, F32))

    with ExitStack() as whole:
        route = buf(whole, "route", [P, 3, T])
        h = buf(whole, "peer_h", [P, KD, T])
        norm(pg, pg.xT, vec(pg, "norm_ffn"), h, T)
        with ExitStack() as own:
            qT = buf(own, "peer_q", [P, 2 * PH, T])
            project(pg, pg.dram["peer_wq"][layer], 2 * PH, KD, h, T, qT)
            peer_route(pg, layer, qT, route)
        gates = buf(whole, "gates", [P, HALF_KEYS, T])
        for half in range(2):
            peer_gates(pg, half, route, gates)
            peer_up(pg, layer, half, h, gates)
            peer_down(pg, layer, half, gates)


def peer_route(pg, layer, qT, route):
    nc = pg.nc
    U32 = mybir.dt.uint32
    loaded, scored, score_taken = pg.counts("keys_loaded"), pg.counts("key_scored"), pg.counts("key_score_taken")
    searched, shifted, exped = pg.counts("key_searched"), pg.counts("top_shifted"), pg.counts("top_exped")
    found, flipped, flip_taken = pg.counts("route_found"), pg.counts("route_flipped"), pg.counts("route_flip_taken")
    vec_step = pg.counts("vec_step")
    with ExitStack() as ctx:
        def buf(name, shape, dt=F32):
            return ctx.enter_context(pg.sbuf(name, shape, dt))
        keys = buf("keys", [P, 2 * PH, NKEY])
        sc = buf("key_scores", [P, 2, 2 * PH, NKEY])
        rest = buf("key_rest", [P, 4, 2 * NKEY])
        top, at, atf = buf("key_top", [P, 2 * PH, TOPK]), buf("key_at", [P, 2 * PH, TOPK], U32), buf("key_atf", [P, 2 * PH, TOPK])
        cand = buf("cand", [P, PH, TOPK, TOPK])
        best, pos = buf("best", [P, PH, TOPK]), buf("pos", [P, PH, TOPK], U32)
        pos1, pos2 = buf("pos1", [P, PH, TOPK], U32), buf("pos2", [P, PH, TOPK], U32)
        pos1f, pos2f = buf("pos1f", [P, PH, TOPK]), buf("pos2f", [P, PH, TOPK])
        hit = buf("hit", [P, PH, TOPK, TOPK])
        chosen = buf("chosen", [P, 3, PH * TOPK])
        total = buf("total", [P, PH, 1])
        sps = [ctx.enter_context(pg.psum(f"key_ps{b}", [P, 4, NKEY], F32)) for b in range(4)]
        fps = ctx.enter_context(pg.psum("route_ps", [P, 3, P], F32))
        block = ctx.enter_context(nc.Block())

        @block.sync
        def _(sp):
            sp.dma_start(keys[:, :, :], pg.dram["peer_keys"][layer]).then_inc(loaded.sem, 16)

        @block.tensor
        def _(pe):
            pe.wait_ge(loaded.sem, loaded.at(16))
            for tb in range(TB + 1):
                if tb < TB:
                    for m in range(4):
                        if tb:
                            pe.wait_ge(score_taken.sem, score_taken.at(4 * (tb - 1) + m + 1))
                        for j in range(4):
                            c = 4 * m + j
                            last = pe.matmul(sps[m][:, j, :], qT[:, c, tb * P:(tb + 1) * P], keys[:, c, :],
                                             start=True, stop=True)
                        last.then_inc(scored.sem, 1)
                if tb:
                    pe.wait_ge(found.sem, found.at(tb))
                    if tb > 1:
                        pe.wait_ge(flip_taken.sem, flip_taken.at(tb - 1))
                    for j in range(3):
                        last = pe.transpose(fps[:, j, :], chosen[:, j, :], pg.c["ident"][:, :])
                    last.then_inc(flipped.sem, 1)

        @block.scalar
        def _(act):
            for tb in range(TB):
                if tb >= 2:
                    act.wait_ge(searched.sem, searched.at(tb - 1))
                for m in range(4):
                    act.wait_ge(scored.sem, scored.at(4 * tb + m + 1))
                    act.activation(sc[:, tb % 2, 4 * m:4 * m + 4, :], sps[m][:, :, :], ACT.Copy).then_inc(score_taken.sem, 1)
                act.wait_ge(shifted.sem, shifted.at(tb + 1))
                act.activation(best[:, :, :], best[:, :, :], ACT.Exp).then_inc(exped.sem, 1)
                act.wait_ge(flipped.sem, flipped.at(tb + 1))
                act.activation(route[:, :, tb * P:(tb + 1) * P], fps[:, :, :], ACT.Copy).then_inc(flip_taken.sem, 1)

        @block.vector
        def _(dve):
            link = linker(dve, vec_step)

            def top16(rows):
                for i in range(0, len(rows), 4):
                    some = rows[i:i + 4]
                    for x, r, v, a in some:
                        last = dve.max(v[:, 0:8], x)
                    link(last)
                    for x, r, v, a in some:
                        dve.max_index(a[:, 0:8], v[:, 0:8], x)
                        last = dve.match_replace(out=r, in_to_replace=v[:, 0:8], in_values=x, imm_value=LOWEST)
                    link(last)
                    for x, r, v, a in some:
                        last = dve.max(v[:, 8:16], r)
                    link(last)
                    for x, r, v, a in some:
                        last = dve.max_index(a[:, 8:16], v[:, 8:16], r)
                    link(last)

            for tb in range(TB):
                dve.wait_ge(score_taken.sem, score_taken.at(4 * tb + 4))
                top16([(sc[:, tb % 2, c, :], rest[:, c % 4, 0:NKEY], top[:, c, :], at[:, c, :]) for c in range(2 * PH)])
                dve.sem_inc(searched.sem, 1)
                link(dve.tensor_copy(atf[:, :, :], at[:, :, :]))
                pair = top[:, :, :].rearrange("p (h c) k -> p h c k", c=2)
                for hd in range(PH):
                    s1 = pair[:, hd, 0, :].rearrange("p (k a) -> p k a", a=1).to_broadcast([P, TOPK, TOPK])
                    s2 = pair[:, hd, 1, :].rearrange("p (a k) -> p a k", a=1).to_broadcast([P, TOPK, TOPK])
                    last = dve.tensor_tensor(cand[:, hd, :, :], s1, s2, ALU.add)
                link(last)
                top16([(cand[:, hd, :, :].rearrange("p a b -> p (a b)"), rest[:, hd % 4, :], best[:, hd, :], pos[:, hd, :])
                       for hd in range(PH)])
                first = total
                link(dve.tensor_copy(first[:, :, :], best[:, :, 0:1]))
                link(dve.tensor_tensor(best[:, :, :], best[:, :, :], first[:, :, :].to_broadcast([P, PH, TOPK]),
                                       ALU.subtract))
                dve.sem_inc(shifted.sem, 1)
                dve.tensor_scalar(pos1[:, :, :], pos[:, :, :], 4, None, ALU.logical_shift_right)
                link(dve.tensor_scalar(pos2[:, :, :], pos[:, :, :], TOPK - 1, None, ALU.bitwise_and))
                dve.tensor_copy(pos1f[:, :, :], pos1[:, :, :])
                link(dve.tensor_copy(pos2f[:, :, :], pos2[:, :, :]))
                if tb:
                    dve.wait_ge(flipped.sem, flipped.at(tb))
                keyed = atf[:, :, :].rearrange("p (h c) k -> p h c k", c=2)
                for j, which in enumerate((pos1f, pos2f)):
                    for hd in range(PH):
                        w = which[:, hd, :].rearrange("p (k a) -> p k a", a=1).to_broadcast([P, TOPK, TOPK])
                        ramp = pg.c["ramp"][:, 0:TOPK].rearrange("p (a k) -> p a k", a=1).to_broadcast([P, TOPK, TOPK])
                        last = dve.tensor_tensor(hit[:, hd, :, :], w, ramp, ALU.is_equal)
                    link(last)
                    for hd in range(PH):
                        key = keyed[:, hd, j, :].rearrange("p (a k) -> p a k", a=1).to_broadcast([P, TOPK, TOPK])
                        last = dve.tensor_tensor(hit[:, hd, :, :], hit[:, hd, :, :], key, ALU.mult)
                    link(last)
                    link(dve.reduce_sum(chosen[:, j, :], hit[:, :, :, :].rearrange("p h k a -> p (h k) a"), AX.X))
                dve.wait_ge(exped.sem, exped.at(tb + 1))
                link(dve.reduce_sum(total[:, :, :].rearrange("p h a -> p (h a)"), best[:, :, :], AX.X))
                link(dve.reciprocal(total[:, :, :], total[:, :, :]))
                link(dve.tensor_tensor(chosen[:, 2, :].rearrange("p (h k) -> p h k", k=TOPK), best[:, :, :],
                                       total[:, :, :].to_broadcast([P, PH, TOPK]), ALU.mult))
                dve.sem_inc(found.sem, 1)
    loaded.passed(16)
    scored.passed(4 * TB)
    score_taken.passed(4 * TB)
    for s in (searched, shifted, exped, found, flipped, flip_taken):
        s.passed(TB)


GT = 8


def peer_gates(pg, half, route, gates):
    nc = pg.nc
    first = [pg.counts(f"first_made{b}") for b in range(2)]
    second = [pg.counts(f"second_made{b}") for b in range(2)]
    equal = [pg.counts(f"second_equal{b}") for b in range(2)]
    spread = [pg.counts(f"gates_summed{b}") for b in range(2)]
    taken = [pg.counts(f"gates_taken{b}") for b in range(2)]
    turns = T // (2 * GT)
    with ExitStack() as ctx:
        one = [ctx.enter_context(pg.sbuf(f"onehot1_{b}", [P, GT, NKEY], F32)) for b in range(2)]
        two = [ctx.enter_context(pg.sbuf(f"onehot2_{b}", [P, GT, HALF_KEYS], F32)) for b in range(2)]
        ps = [ctx.enter_context(pg.psum(f"gate_ps{b}", [P, GT, HALF_KEYS], F32)) for b in range(2)]
        block = ctx.enter_context(nc.Block())
        ramp = lambda lo, n: pg.c["ramp"][:, lo:lo + n].rearrange("p (a k) -> p a k", a=1).to_broadcast([P, GT, n])
        tokens = lambda row, i, b, n: route[:, row, bass.ds(i * 2 * GT + b * GT, GT)] \
            .rearrange("p (t a) -> p t a", a=1).to_broadcast([P, GT, n])

        @block.vector
        def _(dve):
            with dve.Fori(0, turns) as i:
                for b in range(2):
                    dve.wait_ge(spread[b].sem, spread[b].at(0) + i)
                    dve.tensor_tensor(one[b][:, :, :], ramp(0, NKEY), tokens(0, i, b, NKEY), ALU.is_equal) \
                        .then_inc(first[b].sem, 1)
                    dve.tensor_tensor(two[b][:, :, :], ramp(half * HALF_KEYS, HALF_KEYS), tokens(1, i, b, HALF_KEYS),
                                      ALU.is_equal).then_inc(equal[b].sem, 1)
                    dve.wait_ge(equal[b].sem, equal[b].at(1) + i)
                    dve.tensor_tensor(two[b][:, :, :], two[b][:, :, :], tokens(2, i, b, HALF_KEYS), ALU.mult) \
                        .then_inc(second[b].sem, 1)

        @block.tensor
        def _(pe):
            with pe.Fori(0, turns) as i:
                for b in range(2):
                    pe.wait_ge(first[b].sem, first[b].at(1) + i)
                    pe.wait_ge(second[b].sem, second[b].at(1) + i)
                    pe.wait_ge(taken[b].sem, taken[b].at(0) + i)
                    for t in range(GT):
                        last = pe.matmul(ps[b][:, t, :], one[b][:, t, :], two[b][:, t, :], start=True, stop=True)
                    last.then_inc(spread[b].sem, 1)

        @block.scalar
        def _(act):
            with act.Fori(0, turns) as i:
                for b in range(2):
                    act.wait_ge(spread[b].sem, spread[b].at(1) + i)
                    act.activation(gates[:, :, bass.ds(i * 2 * GT + b * GT, GT)].rearrange("p k t -> p t k"),
                                   ps[b][:, :, :], ACT.Copy).then_inc(taken[b].sem, 1)
    for b in range(2):
        for s in (first[b], second[b], equal[b], spread[b], taken[b]):
            s.passed(turns)


UP_BUFS = 4


def peer_up(pg, layer, half, h, gates):
    nc = pg.nc
    loaded = [pg.counts(f"u_loaded{b}") for b in range(UP_BUFS)]
    summed = [pg.counts(f"u_summed{b}") for b in range(UP_BUFS)]
    gelued = [pg.counts(f"u_gelued{b}") for b in range(UP_BUFS)]
    weighed = [pg.counts(f"u_weighed{b}") for b in range(UP_BUFS)]
    turns = HALF_KEYS // UP_BUFS
    with ExitStack() as ctx:
        u = [ctx.enter_context(pg.sbuf(f"u{b}", [P, KD, P], F32)) for b in range(UP_BUFS)]
        a = [ctx.enter_context(pg.sbuf(f"u_act{b}", [P, T], F32)) for b in range(2)]
        ps = [ctx.enter_context(pg.psum(f"u_ps{b}", [P, T], F32)) for b in range(UP_BUFS)]
        block = ctx.enter_context(nc.Block())
        table = pg.dram["peer_u"][layer]

        @block.sync
        def _(sp):
            with sp.Fori(0, turns) as i:
                for b in range(UP_BUFS):
                    sp.wait_ge(summed[b].sem, summed[b].at(0) + i)
                    sp.dma_start(u[b][:, :, :].rearrange("p k n -> p (k n)"),
                                 table[bass.ds(i * UP_BUFS + (b + half * HALF_KEYS), 1), :, :].rearrange("a p n -> p (a n)")) \
                        .then_inc(loaded[b].sem, 16)

        @block.tensor
        def _(pe):
            with pe.Fori(0, turns) as i:
                for b in range(UP_BUFS):
                    pe.wait_ge(loaded[b].sem, loaded[b].at(16) + i * 16)
                    pe.wait_ge(gelued[b].sem, gelued[b].at(0) + i)
                    for k in range(KD):
                        last = pe.matmul(ps[b][:, :], u[b][:, k, :], h[:, k, :], start=(k == 0), stop=(k == KD - 1))
                    last.then_inc(summed[b].sem, 1)

        @block.scalar
        def _(act):
            with act.Fori(0, turns) as i:
                for b in range(UP_BUFS):
                    act.wait_ge(summed[b].sem, summed[b].at(1) + i)
                    before = weighed[(b - 2) % UP_BUFS]
                    act.wait_ge(before.sem, before.at(0 if b < 2 else 1) + i)
                    act.activation(a[b % 2][:, :], ps[b][:, :], ACT.Gelu_apprx_tanh).then_inc(gelued[b].sem, 1)

        @block.vector
        def _(dve):
            with dve.Fori(0, turns) as i:
                for b in range(UP_BUFS):
                    dve.wait_ge(gelued[b].sem, gelued[b].at(1) + i)
                    g = gates[:, bass.ds(i * UP_BUFS + b, 1), :].rearrange("p a t -> p (a t)")
                    dve.tensor_tensor(g, g, a[b % 2][:, :], ALU.mult).then_inc(weighed[b].sem, 1)
    for b in range(UP_BUFS):
        loaded[b].passed(16 * turns)
        for s in (summed[b], gelued[b], weighed[b]):
            s.passed(turns)


DOWN_BUFS = 4


def peer_down(pg, layer, half, gates):
    nc = pg.nc
    loaded = [pg.counts(f"down_loaded{b}") for b in range(DOWN_BUFS)]
    used = [pg.counts(f"down_used{b}") for b in range(DOWN_BUFS)]
    added = pg.counts("down_added")
    turns = HALF_KEYS // DOWN_BUFS
    with ExitStack() as ctx:
        v = [ctx.enter_context(pg.sbuf(f"down{b}", [P, D], F32)) for b in range(DOWN_BUFS)]
        ps = [ctx.enter_context(pg.psum(f"down_ps{b}", [P, T], F32)) for b in range(KD)]
        block = ctx.enter_context(nc.Block())
        table = pg.dram["peer_v"][layer]

        @block.sync
        def _(sp):
            with sp.Fori(0, turns) as i:
                for b in range(DOWN_BUFS):
                    sp.wait_ge(used[b].sem, used[b].at(0) + i)
                    sp.dma_start(v[b][:, :], table[bass.ds(i * DOWN_BUFS + (b + half * HALF_KEYS), 1), :, :]
                                 .rearrange("a p n -> p (a n)")).then_inc(loaded[b].sem, 16)

        @block.tensor
        def _(pe):
            def turn(i, first, last_turn):
                for b in range(DOWN_BUFS):
                    pe.wait_ge(loaded[b].sem, loaded[b].at(16) + i * 16)
                    for k in range(KD):
                        g = gates[:, bass.ds(i * DOWN_BUFS + b, 1), :].rearrange("p a t -> p (a t)") \
                            if not isinstance(i, int) else gates[:, i * DOWN_BUFS + b, :]
                        last = pe.matmul(ps[k][:, :], v[b][:, k * P:(k + 1) * P], g,
                                         start=first and b == 0, stop=last_turn and b == DOWN_BUFS - 1)
                    last.then_inc(used[b].sem, 1)

            turn(0, True, False)
            with pe.Fori(1, turns - 1) as i:
                turn(i, False, False)
            turn(turns - 1, False, True)

        @block.vector
        def _(dve):
            dve.wait_ge(used[-1].sem, used[-1].at(turns))
            for k in range(KD):
                last = dve.tensor_tensor(pg.xT[:, k, :], pg.xT[:, k, :], ps[k][:, :], ALU.add)
            last.then_inc(added.sem, 1)
            dve.wait_ge(added.sem, added.at(1))
    added.passed(1)
    for b in range(DOWN_BUFS):
        loaded[b].passed(16 * turns)
        used[b].passed(turns)


def build(nc, dram, out):
    with ExitStack() as ctx:
        def keep(name, shape, dt=F32):
            return ctx.enter_context(nc.sbuf_tensor(name, shape, dt))

        pg = Program(nc, ctx, dram)
        pg.xT = keep("xT", [P, KD, T])
        pg.vec = keep("vec", [P, NVEC])
        pg.v_first = keep("v_first", [P, KH, T])
        for name, shape in (("ones", [P, P]), ("ident", [P, P]), ("head_ones", [P, P]), ("gram_mask", [P, 4, P]),
                            ("lower_mask", [P, P]), ("level_mask", [P, 6, P]), ("level0_lower", [P, P]),
                            ("chunk_keep", [P, T]), ("ramp", [P, NKEY])):
            pg.c[name] = keep(name, shape)
        constants(pg)
        for layer in range(DEPTH):
            load_vectors(pg, layer)
            mixer(pg, layer)
            cross_attention(pg, layer)
            peer(pg, layer)
        with ExitStack() as own:
            yT = own.enter_context(pg.sbuf("yT", [P, KD, T], F32))
            norm(pg, pg.xT, vec(pg, "norm_final"), yT, T)
            stored = pg.counts("out_stored")
            with nc.Block() as block:
                @block.sync
                def _(sp):
                    sp.dma_start(out, yT[:, :, :]).then_inc(stored.sem, 16)
                    sp.wait_ge(stored.sem, stored.at(16))


def kernel(**inputs):
    import numpy as np
    import concourse.bacc as bacc
    from concourse.bass_utils import run_bass_kernel_spmd

    a = {k: np.asarray(v) for k, v in inputs.items()}
    L = DEPTH

    def tiles(w):
        n, k, m = w.shape
        return w.reshape(n, k // P, P, m // P, P).transpose(0, 3, 2, 1, 4).reshape(n, m // P, P, k)

    def rows(w):
        s = w.shape
        w = w.reshape(*s[:-2], s[-2] // P, P, s[-1])
        return np.moveaxis(w, -2, -3)

    def columns(v):
        return v.reshape(v.shape[0], -1, P).transpose(0, 2, 1)

    per_layer = {
        "norm_mix": a["norm_mix"], "norm_xa": a["norm_xa"], "norm_mem": a["norm_mem"], "norm_ffn": a["norm_ffn"],
        "norm_final": np.broadcast_to(a["norm_final"], (L, D)), "mu": a["rw_mu"], "w0": a["rw_w0"], "a0": a["rw_a0"],
        "kk": a["rw_kk"], "ka": a["rw_ka"], "rk": a["rw_rk"].reshape(L, D_HALF),
        "v0": a["rw_v0"][[max(l - 1, 0) for l in range(L)]], "lnx_g": a["rw_lnx_g"], "lnx_b": a["rw_lnx_b"],
        "s5_d": a["s5_d"], "glu_b": a["s5_glu_b"], "out_g": a["s5_out_g"],
    }
    pairs = lambda v: v.reshape(L, S5_PAIRS, P).transpose(0, 2, 1)

    def experts(w):
        return w.reshape(L, NKEY, NKEY, D).transpose(0, 2, 1, 3)

    arrays = {
        "xT": rows(a["x"][0].T), "memT": rows(a["mem"][0].T),
        "vec": np.concatenate([columns(per_layer[n]) for n in VEC], axis=2),
        "w_in": tiles(a["w_in"]), "w2": a["rw_w2"], "a2": a["rw_a2"], "g2": a["rw_g2"],
        "v1": rows(a["rw_v1"]), "v2": a["rw_v2"],
        "s5_are": pairs(a["s5_a_re"]), "s5_aim": pairs(a["s5_a_im"]),
        "s5_dt": pairs(np.repeat(a["s5_log_dt"], 64, axis=1).reshape(L, 32, 64)),
        "s5_bre": a["s5_b_re"], "s5_bim": a["s5_b_im"],
        "s5_cre": a["s5_c_re"].transpose(0, 1, 3, 2), "s5_cim": a["s5_c_im"].transpose(0, 1, 3, 2),
        "glu_w": tiles(a["s5_glu_w"]), "w_out": tiles(a["w_out"]),
        "xa_wq": tiles(a["xa_wq"]), "xa_wk": tiles(a["xa_wk"]), "xa_wo": tiles(a["xa_wo"]),
        "xa_wv": rows(a["xa_wv"]),
        "peer_wq": tiles(a["peer_wq"]),
        "peer_keys": a["peer_keys"].reshape(L, 2 * PH, NKEY, P).transpose(0, 3, 1, 2),
        "peer_u": experts(a["peer_u"]).reshape(L, NKEY, NKEY, KD, P).transpose(0, 1, 4, 3, 2).reshape(L, NKEY, P, D),
        "peer_v": experts(a["peer_v"]),
    }
    nc = bacc.Bacc("TRN2", target_bir_lowering=False, num_devices=1)
    dram, sent = {}, {}
    for name, v in arrays.items():
        v = np.ascontiguousarray(v)
        sent[f"in_{name}"] = v
        dram[name] = nc.dram_tensor(f"in_{name}", v.shape, mybir.dt.from_np(v.dtype), kind="ExternalInput").ap()
    out = nc.dram_tensor("out", (P, KD, T), F32, kind="ExternalOutput").ap()
    build(nc, dram, out)
    r = run_bass_kernel_spmd(nc, [sent], core_ids=[0])
    y = r.results[0]["out"]
    return y.transpose(1, 0, 2).reshape(D, T).T.reshape(1, T, D)
```

```python
import math
from contextlib import ExitStack

import concourse.bass as bass
from concourse import mybir

F32 = mybir.dt.float32
BF16 = mybir.dt.bfloat16
F32R = mybir.dt.float32r
ALU = mybir.AluOpType
ACT = mybir.ActivationFunctionType
AX = mybir.AxisListType

P = 128
D = 1024
KD = D // P
T = 512
DEPTH = 2
N_MEM = 256
D_HALF = 512
KH = D_HALF // P
RW_TILES = 14
IN_TILES = 18
HEADS, HEAD = 8, 64
CH = 64
NCH = T // CH
TB = T // P
S5_PAIRS = 16
S5_C = 16
SC = 8
SN = T // SC
XA_HEADS, XA_HEAD = 4, 256
PH, NKEY, TOPK = 8, 128, 16
HALF_KEYS = NKEY // 2
RMS_EPS, GN_EPS = 1e-6, 64e-5
DECAY_SCALE = -math.exp(-0.5)
TWO_PI_HI, TWO_PI_LO = 6.28125, 2 * math.pi - 6.28125
PI_IN = 3.1415925
ROUND = 12582912.0
LOWEST = -3.0e38

VEC = {}
_at = 0
for _name, _n in (("norm_mix", 8), ("norm_xa", 8), ("norm_mem", 8), ("norm_ffn", 8), ("norm_final", 8),
                  ("mu", 14), ("w0", 4), ("a0", 4), ("kk", 4), ("ka", 4), ("rk", 4), ("v0", 4),
                  ("lnx_g", 4), ("lnx_b", 4), ("s5_d", 4), ("glu_b", 4), ("out_g", 4)):
    VEC[_name] = _at
    _at += _n
NVEC = _at


FREEING = [f"{n}{b}" for b in range(2) for n in (
    "w_low_made", "proj_summed", "proj_taken", "block_low_made", "block_multiplied", "up_gelued", "up_weighed",
    "gates_taken", "second_made")] + [f"first_used{c}" for c in range(4)]


class Signal:

    def __init__(self, sem):
        self.sem, self.base, self.n = sem, 0, 0

    def at(self, n):
        return self.base + n

    def passed(self, n):
        self.base += n


class Program:

    def __init__(self, nc, ctx, dram):
        self.nc, self.ctx, self.dram, self.known = nc, ctx, dram, {}
        self.c, self.made = {}, 0
        self.xT = self.vec = None

    def counts(self, name):
        if name not in self.known:
            self.known[name] = Signal(self.ctx.enter_context(self.nc.semaphore(name)))
            self.known[name].base = int(name in FREEING)
        return self.known[name]

    def sbuf(self, name, shape, dt):
        self.made += 1
        return self.nc.sbuf_tensor(f"{name}_{self.made}", shape, dt)

    def psum(self, name, shape, dt):
        self.made += 1
        return self.nc.psum_tensor(f"{name}_{self.made}", shape, dt)


def linker(engine, s):
    def link(ins):
        s.n += 1
        ins.then_inc(s.sem, 1)
        engine.wait_ge(s.sem, s.n)
    return link


def constants(pg):
    nc, c = pg.nc, pg.c
    made = pg.counts("constants_made")
    pool_step = pg.counts("pool_step")
    with nc.Block() as block:
        @block.gpsimd
        def _(pool):
            link = linker(pool, pool_step)
            for name in FREEING:
                pool.sem_inc(pg.counts(name).sem, 1)
            link(pool.memset(c["ones"][:, :], 1.0))
            link(pool.memset(c["ident"][:, :], 0.0))
            link(pool.affine_select(out=c["ident"][:, :], in_=c["ident"][:, :], compare_op=ALU.not_equal, fill=1.0,
                                    base=0, pattern=[[-1, P]], channel_multiplier=1))
            link(pool.memset(c["head_ones"][:, :], 0.0))
            link(pool.memset(c["head_ones"][0:64, 0:64], 1.0))
            link(pool.memset(c["head_ones"][64:128, 64:128], 1.0))
            hm = c["head_ones"][:, :]
            m = c["gram_mask"]
            for k in range(4):
                strict = k % 2 == 0
                link(pool.affine_select(out=m[:, k, :], in_=hm, compare_op=ALU.is_gt if strict else ALU.is_ge,
                                        fill=0.0, base=0, pattern=[[1, P]], channel_multiplier=-1))
            link(pool.affine_select(out=c["lower_mask"][:, :], in_=hm, compare_op=ALU.is_gt, fill=0.0, base=0,
                                    pattern=[[-1, P]], channel_multiplier=1))
            for lv in range(6):
                b = 1 << lv
                o = c["level_mask"][:, lv, :].rearrange("p (g h b) -> p g h b", h=2, b=b)
                link(pool.memset(c["level_mask"][:, lv, :], 0.0))
                link(pool.memset(o[:, :, 1, :], 1.0))
                link(pool.affine_select(out=o[:, :, 1, :], in_=o[:, :, 1, :], compare_op=ALU.is_ge, fill=0.0,
                                        base=0, pattern=[[-2 * b, P // (2 * b)], [0, b]], channel_multiplier=1))
                link(pool.affine_select(out=o[:, :, 1, :], in_=o[:, :, 1, :], compare_op=ALU.is_gt, fill=0.0,
                                        base=b, pattern=[[2 * b, P // (2 * b)], [0, b]], channel_multiplier=-1))
            link(pool.memset(c["chunk_keep"][:, :], 1.0))
            link(pool.memset(c["chunk_keep"][:, :].rearrange("p (n s) -> p n s", s=CH)[:, :, 0:1], 0.0))
            link(pool.memset(c["level0_lower"][:, :], 0.0))
            ev = c["level0_lower"][:, :].rearrange("p (g h) -> p g h", h=2)[:, :, 0:1]
            link(pool.affine_select(out=ev, in_=ev, compare_op=ALU.not_equal, fill=1.0, base=-1,
                                    pattern=[[-2, P // 2], [0, 1]], channel_multiplier=1))
            pool.iota(c["ramp"][:, :], pattern=[[1, NKEY]], base=0, channel_multiplier=0,
                      allow_small_or_imprecise_dtypes=True).then_inc(made.sem, 1)
            pool.wait_ge(made.sem, made.at(1))
        @block.sync
        def _(sp):
            sp.dma_start(pg.xT[:, :, :], pg.dram["xT"]).then_inc(pg.counts("x_loaded").sem, 16)
            sp.wait_ge(pg.counts("x_loaded").sem, 16)
    made.passed(1)


def norm(pg, src, gain, dst, n):
    nc = pg.nc
    squared, summed, meaned, rooted = (pg.counts(s) for s in ("norm_squared", "norm_summed", "norm_meaned", "norm_rooted"))
    vec_step = pg.counts("vec_step")
    with ExitStack() as ctx:
        sq = ctx.enter_context(pg.sbuf("norm_sq", [P, KD, n], F32))
        root = ctx.enter_context(pg.sbuf("norm_root", [P, n], F32))
        rstd = ctx.enter_context(pg.sbuf("norm_rstd", [P, n], F32))
        ps = ctx.enter_context(pg.psum("norm_ps", [P, n], F32))
        block = ctx.enter_context(nc.Block())

        @block.scalar
        def _(act):
            for k in range(KD):
                act.activation(sq[:, k, :], src[:, k, :], ACT.Square).then_inc(squared.sem, 1)
            act.wait_ge(meaned.sem, meaned.at(1))
            act.activation(root[:, :], rstd[:, :], ACT.Sqrt).then_inc(rooted.sem, 1)

        @block.tensor
        def _(pe):
            for k in range(KD):
                pe.wait_ge(squared.sem, squared.at(k + 1))
                last = pe.matmul(ps[:, :], pg.c["ones"][:, :], sq[:, k, :], start=(k == 0), stop=(k == KD - 1))
            last.then_inc(summed.sem, 1)

        @block.vector
        def _(dve):
            link = linker(dve, vec_step)
            dve.wait_ge(summed.sem, summed.at(1))
            dve.tensor_scalar(rstd[:, :], ps[:, :], 1.0 / D, RMS_EPS, ALU.mult, ALU.add).then_inc(meaned.sem, 1)
            dve.wait_ge(rooted.sem, rooted.at(1))
            link(dve.reciprocal(rstd[:, :], root[:, :]))
            for k in range(KD):
                last = dve.scalar_tensor_tensor(out=dst[:, k, :], in0=src[:, k, :], scalar=gain[:, k:k + 1],
                                                in1=rstd[:, :], op0=ALU.mult, op1=ALU.mult)
            link(last)
    squared.passed(KD)
    for s in (summed, meaned, rooted):
        s.passed(1)


def split_high(act, out, value):
    return act.activation(out, value, ACT.Copy)


def split_low(dve, out, value, high):
    return dve.tensor_tensor(out, value, high.bitcast(F32), ALU.subtract)


def product(pe, out, weights, moving, first, last):
    (wh, wl), (mh, ml) = weights, moving
    pe.matmul(out, wh, mh, start=first, stop=False)
    pe.matmul(out, wh, ml, start=False, stop=False)
    return pe.matmul(out, wl, mh, start=False, stop=last)


def project(pg, weights, tiles, kt, rhs, n, dest, add=False, parts=None):
    nc = pg.nc
    loaded = [pg.counts(f"w_loaded{b}") for b in range(2)]
    high_made = [pg.counts(f"w_high_made{b}") for b in range(2)]
    low_made = [pg.counts(f"w_low_made{b}") for b in range(2)]
    summed = [pg.counts(f"proj_summed{b}") for b in range(2)]
    taken = [pg.counts(f"proj_taken{b}") for b in range(2)]
    rhs_high, rhs_low = pg.counts("rhs_high_made"), pg.counts("rhs_low_made")
    turns = tiles // 2
    with ExitStack() as ctx:
        def buf(name, shape, dt=F32R):
            return ctx.enter_context(pg.sbuf(name, shape, dt))
        w = [buf(f"proj_w{b}", [P, kt, P], F32) for b in range(2)]
        wh, wl = ([buf(f"proj_{x}{b}", [P, kt, P]) for b in range(2)] for x in ("wh", "wl"))
        rh, rl = parts or (buf("proj_rh", [P, kt, n]), buf("proj_rl", [P, kt, n]))
        ps = [ctx.enter_context(pg.psum(f"proj_ps{b}", [P, n], F32)) for b in range(2)]
        block = ctx.enter_context(nc.Block())
        tile = lambda i, b: dest[:, bass.ds(i * 2 + b, 1), :].rearrange("p a n -> p (a n)")

        @block.sync
        def _(sp):
            with sp.Fori(0, turns) as i:
                for b in range(2):
                    sp.wait_ge(low_made[b].sem, low_made[b].at(0) + i)
                    sp.dma_start(w[b][:, :, :], weights[bass.ds(i * 2 + b, 1), :, :].rearrange("a p (k n) -> p (a k) n", n=P)) \
                        .then_inc(loaded[b].sem, 16)

        @block.tensor
        def _(pe):
            with pe.Fori(0, turns) as i:
                for b in range(2):
                    pe.wait_ge(low_made[b].sem, low_made[b].at(1) + i)
                    pe.wait_ge(taken[b].sem, taken[b].at(0) + i)
                    for k in range(kt):
                        if not parts:
                            pe.wait_ge(rhs_low.sem, rhs_low.at(k + 1))
                        last = product(pe, ps[b][:, :], (wh[b][:, k, :], wl[b][:, k, :]), (rh[:, k, :], rl[:, k, :]),
                                       k == 0, k == kt - 1)
                    last.then_inc(summed[b].sem, 1)

        @block.vector
        def _(dve):
            def rhs_lows(some):
                for k in some:
                    dve.wait_ge(rhs_high.sem, rhs_high.at(k + 1))
                    split_low(dve, rl[:, k, :], rhs[:, k, :], rh[:, k, :]).then_inc(rhs_low.sem, 1)

            def weights_low(b, i):
                dve.wait_ge(high_made[b].sem, high_made[b].at(1) + i)
                split_low(dve, wl[b][:, :, :], w[b][:, :, :], wh[b][:, :, :]).then_inc(low_made[b].sem, 1)

            def take(b, i):
                dve.wait_ge(summed[b].sem, summed[b].at(1) + i)
                dve.tensor_tensor(tile(i, b), tile(i, b), ps[b][:, :], ALU.add).then_inc(taken[b].sem, 1)

            if not parts:
                rhs_lows(range(kt // 2))
            weights_low(0, 0)
            if not parts:
                rhs_lows(range(kt // 2, kt))
            weights_low(1, 0)
            with dve.Fori(0, turns - 1) as i:
                for b in range(2):
                    if add:
                        take(b, i)
                    weights_low(b, i + 1)
            if add:
                take(0, turns - 1)
                take(1, turns - 1)

        @block.scalar
        def _(act):
            for b in range(2):
                for k in range(b * kt // 2, 0 if parts else (b + 1) * kt // 2):
                    split_high(act, rh[:, k, :], rhs[:, k, :]).then_inc(rhs_high.sem, 1)
                act.wait_ge(loaded[b].sem, loaded[b].at(16))
                split_high(act, wh[b][:, :, :], w[b][:, :, :]).then_inc(high_made[b].sem, 1)

            def weights_high(b, i):
                act.wait_ge(loaded[b].sem, loaded[b].at(16) + i * 16)
                act.wait_ge(summed[b].sem, summed[b].at(0) + i)
                split_high(act, wh[b][:, :, :], w[b][:, :, :]).then_inc(high_made[b].sem, 1)

            def take(b, i):
                act.wait_ge(summed[b].sem, summed[b].at(1) + i)
                act.activation(tile(i, b), ps[b][:, :], ACT.Copy).then_inc(taken[b].sem, 1)

            with act.Fori(0, turns - 1) as i:
                for b in range(2):
                    if not add:
                        take(b, i)
                    weights_high(b, i + 1)
            if not add:
                take(0, turns - 1)
                take(1, turns - 1)
    rhs_high.passed(0 if parts else kt)
    rhs_low.passed(0 if parts else kt)
    for b in range(2):
        loaded[b].passed(16 * turns)
        for s in (summed[b], taken[b], high_made[b], low_made[b]):
            s.passed(turns)


def vec(pg, name):
    n = {"mu": RW_TILES}.get(name, KD if name.startswith("norm") else KH)
    return pg.vec[:, VEC[name]:VEC[name] + n]


def load_vectors(pg, layer):
    loaded = pg.counts("vectors_loaded")
    with pg.nc.Block() as block:
        @block.sync
        def _(sp):
            sp.dma_start(pg.vec[:, :], pg.dram["vec"][layer]).then_inc(loaded.sem, 16)
            sp.wait_ge(loaded.sem, loaded.at(16))
    loaded.passed(16)


def mixer(pg, layer):
    nc, dram = pg.nc, pg.dram

    def buf(own, name, shape):
        return own.enter_context(pg.sbuf(name, shape, F32))

    with ExitStack() as whole:
        mixT = buf(whole, "mixT", [P, KD, T])
        with ExitStack() as rw:
            v, rk, wag = buf(rw, "v", [P, KH, T]), buf(rw, "rk", [P, 2, KH, T]), buf(rw, "wag", [P, 2, T])
            h = buf(rw, "h", [P, KD, T])
            norm(pg, pg.xT, vec(pg, "norm_mix"), h, T)
            with ExitStack() as own:
                zb = buf(own, "zb", [P, IN_TILES, T + 1])
                project(pg, dram["w_in"][layer], IN_TILES, KD, h, T, zb[:, :, 1:T + 1])
                token_shift(pg, layer, zb, rk, v, wag, mixT)
            r = {n: buf(rw, n, s) for n, s in (
                ("bonus", [P, KH, T]), ("ar", [P, KH, TB, 2, P]), ("b", [P, KH, T]), ("k", [P, KH, T]),
                ("b_end", [P, KH, T]), ("k_end", [P, KH, T]), ("p_end", [P, KH, NCH]))}
            r["v"] = v
            rwkv_prepare(pg, layer, rk, wag, h, r, mixT)
            st = {"f": rk[:, :, :, :].rearrange("p a t (b n) -> p (a t) b n", n=P),
                  "hh": h[:, :, :].rearrange("p k (b n) -> p k b n", n=P),
                  "xz": wag,
                  "rq": buf(rw, "rq", [P, KH, T]), "y": buf(rw, "y", [P, KH, T])}
            rwkv_chunks(pg, r, st)
            rwkv_states(pg, st)
            rwkv_finish(pg, r, st, mixT)
        s5(pg, layer, mixT)
        project(pg, dram["w_out"][layer], KD, KD, mixT, T, pg.xT, add=True)


def token_shift(pg, layer, zb, rk, v, wag, mixT):
    nc = pg.nc
    cleared, moved = pg.counts("shift_cleared"), pg.counts("u_moved")
    vec_step = pg.counts("vec_step")
    mu = vec(pg, "mu")
    with ExitStack() as ctx:
        diff = [ctx.enter_context(pg.sbuf(f"shift_diff{b}", [P, T], F32)) for b in range(2)]
        block = ctx.enter_context(nc.Block())
        places = [rk[:, 0, i, :] for i in range(4)] + [rk[:, 1, i, :] for i in range(4)] + \
                 [v[:, i, :] for i in range(4)] + [wag[:, i, :] for i in range(2)]

        @block.gpsimd
        def _(pool):
            pool.memset(zb[:, :, 0:1], 0.0).then_inc(cleared.sem, 1)

        @block.scalar
        def _(act):
            act.activation(mixT[:, KH:KD, :], zb[:, RW_TILES:IN_TILES, 1:T + 1], ACT.Copy).then_inc(moved.sem, 1)

        @block.vector
        def _(dve):
            link = linker(dve, vec_step)
            dve.wait_ge(cleared.sem, cleared.at(1))
            for i in range(RW_TILES):
                link(dve.tensor_tensor(diff[i % 2][:, :], zb[:, i, 0:T], zb[:, i, 1:T + 1], ALU.subtract))
                link(dve.scalar_tensor_tensor(out=places[i], in0=diff[i % 2][:, :], scalar=mu[:, i:i + 1],
                                              in1=zb[:, i, 1:T + 1], op0=ALU.mult, op1=ALU.add))
            if layer == 0:
                link(dve.tensor_copy(pg.v_first[:, :, :], v[:, :, :]))
    cleared.passed(1)
    moved.passed(1)


def rwkv_prepare(pg, layer, rk, wag, h, r, mixT):
    nc, dram = pg.nc, pg.dram
    gate = mixT[:, 0:KH, :]
    rT, kT, v = rk[:, 0], rk[:, 1], r["v"]
    small_loaded, squashed = pg.counts("lora_loaded"), pg.counts("lora_squashed")
    lora_in, lora_in_taken = pg.counts("v1_summed"), pg.counts("v1_taken")
    low, low_taken = pg.counts("lora_summed"), pg.counts("lora_taken")
    kk_made, kk_squared, kk_summed, kk_rooted = (pg.counts(s) for s in ("kk_made", "kk_squared", "kk_summed", "kk_rooted"))
    logs_made, exps_made = pg.counts("logs_made"), pg.counts("exps_made")
    rk_made, rk_summed = pg.counts("rk_made"), pg.counts("rk_summed")
    vec_step, act_step = pg.counts("vec_step"), pg.counts("act_step")
    kinds = (["v"] if layer else []) + ["w", "a", "g"]
    with ExitStack() as ctx:
        def buf(name, shape):
            return ctx.enter_context(pg.sbuf(name, shape, F32))
        lw, cum, e, av, kk = (buf(n, [P, KH, T]) for n in ("lw", "cum", "e", "av", "kk"))
        wa, g2 = kk[:, 0, :], kk[:, 1, :]
        v1, v2, vl = kk[:, 2, 0:256].rearrange("p (k n) -> p k n", k=KD), kk[0:32, 3, :], kk[32:64, 3, :]
        vl = cum[0:32, 0, :]
        ps = [ctx.enter_context(pg.psum(f"prep_ps{b}", [P, T], F32)) for b in range(8)]
        block = ctx.enter_context(nc.Block())
        loads = 5 if layer else 3

        @block.sync
        def _(sp):
            sp.dma_start(wa[0:64], dram["w2"][layer]).then_inc(small_loaded.sem, 16)
            sp.dma_start(wa[64:128], dram["a2"][layer]).then_inc(small_loaded.sem, 16)
            sp.dma_start(g2, dram["g2"][layer]).then_inc(small_loaded.sem, 16)
            if layer:
                sp.dma_start(v1, dram["v1"][layer - 1]).then_inc(small_loaded.sem, 16)
                sp.dma_start(v2, dram["v2"][layer - 1]).then_inc(small_loaded.sem, 16)

        @block.tensor
        def _(pe):
            pe.wait_ge(small_loaded.sem, small_loaded.at(16 * loads))
            if layer:
                for k in range(KD):
                    last = pe.matmul(ps[7][0:32, :], v1[:, k, :], h[:, k, :], start=(k == 0), stop=(k == KD - 1))
                last.then_inc(lora_in.sem, 1)
                pe.wait_ge(lora_in_taken.sem, lora_in_taken.at(1))
            pe.wait_ge(squashed.sem, squashed.at(2))
            for m in range(4 * len(kinds)):
                kind, t = kinds[m // 4], m % 4
                if m >= 4:
                    pe.wait_ge(low_taken.sem, low_taken.at(m - 3))
                cols = slice(t * P, (t + 1) * P)
                lhs, rhs = {"v": (v2[:, cols], vl), "w": (wa[0:64, cols], wag[0:64, 0, :]),
                            "a": (wa[64:128, cols], wag[64:128, 0, :]), "g": (g2[:, cols], wag[:, 1, :])}[kind]
                pe.matmul(ps[m % 4][:, :], lhs, rhs, start=True, stop=True).then_inc(low.sem, 1)
            for t in range(KH):
                pe.wait_ge(kk_squared.sem, kk_squared.at(t + 1))
                last = pe.matmul(ps[4 + t][:, :], pg.c["head_ones"][:, :], e[:, t, :], start=True, stop=True)
            last.then_inc(kk_summed.sem, 1)
            pe.wait_ge(rk_made.sem, rk_made.at(1))
            for t in range(KH):
                last = pe.matmul(ps[t][:, :], pg.c["head_ones"][:, :], e[:, t, :], start=True, stop=True)
            last.then_inc(rk_summed.sem, 1)

        @block.scalar
        def _(act):
            link = linker(act, act_step)
            act.activation(wag[0:64, 0, :], wag[0:64, 0, :], ACT.Tanh).then_inc(squashed.sem, 1)
            act.activation(wag[:, 1, :], wag[:, 1, :], ACT.Sigmoid).then_inc(squashed.sem, 1)
            if layer:
                act.wait_ge(lora_in.sem, lora_in.at(1))
                act.activation(vl, ps[7][0:32, :], ACT.Copy).then_inc(lora_in_taken.sem, 1)
            for m in range(4 * len(kinds)):
                kind, t = kinds[m // 4], m % 4
                act.wait_ge(low.sem, low.at(m + 1))
                if kind == "g":
                    act.activation(gate[:, t, :], ps[m % 4][:, :], ACT.Copy).then_inc(low_taken.sem, 1)
                else:
                    out, bias = {"v": (e, "v0"), "w": (lw, "w0"), "a": (av, "a0")}[kind]
                    act.activation(out[:, t, :], ps[m % 4][:, :], ACT.Sigmoid,
                                   bias=vec(pg, bias)[:, t:t + 1]).then_inc(low_taken.sem, 1)
            act.wait_ge(kk_made.sem, kk_made.at(1))
            for t in range(KH):
                act.activation(e[:, t, :], kk[:, t, :], ACT.Square).then_inc(kk_squared.sem, 1)
            act.wait_ge(kk_summed.sem, kk_summed.at(1))
            for t in range(KH):
                last = act.activation(e[:, t, :], ps[4 + t][:, :], ACT.Sqrt)
            last.then_inc(kk_rooted.sem, 1)
            act.wait_ge(logs_made.sem, logs_made.at(1))
            act.activation(lw[:, :, :], lw[:, :, :], ACT.Exp)
            link(act.activation(e[:, :, :], cum[:, :, :], ACT.Exp))
            act.activation(cum[:, :, :], cum[:, :, :], ACT.Exp, scale=-1.0).then_inc(exps_made.sem, 1)

        @block.vector
        def _(dve):
            link = linker(dve, vec_step)
            if layer:
                dve.wait_ge(low_taken.sem, low_taken.at(4))
                difference = r["bonus"]
                link(dve.tensor_tensor(difference[:, :, :], pg.v_first[:, :, :], v[:, :, :], ALU.subtract))
                link(dve.tensor_tensor(e[:, :, :], difference[:, :, :], e[:, :, :], ALU.mult))
                link(dve.tensor_tensor(v[:, :, :], v[:, :, :], e[:, :, :], ALU.add))
            dve.wait_ge(low_taken.sem, low_taken.at(4 * len(kinds)))
            link(dve.tensor_scalar(lw[:, :, :], lw[:, :, :], DECAY_SCALE, None, ALU.mult))
            for t in range(KH):
                dve.tensor_tensor_scan(cum[:, t, :], pg.c["chunk_keep"][:, :], lw[:, t, :], 0.0, ALU.mult, ALU.add)
            for t in range(KH):
                last = dve.tensor_scalar(kk[:, t, :], kT[:, t, :], vec(pg, "kk")[:, t:t + 1], None, ALU.mult)
            link(last)
            dve.sem_inc(kk_made.sem, 1)
            link(dve.tensor_tensor(lw[:, :, :], cum[:, :, :], lw[:, :, :], ALU.subtract))
            dve.wait_ge(kk_rooted.sem, kk_rooted.at(1))
            link(dve.tensor_scalar(e[:, :, :], e[:, :, :], 1e-12, None, ALU.max))
            link(dve.reciprocal(e[:, :, :], e[:, :, :]))
            link(dve.tensor_tensor(kk[:, :, :], kk[:, :, :], e[:, :, :], ALU.mult))
            for t in range(KH):
                last = dve.tensor_scalar(e[:, t, :], av[:, t, :], -1.0, vec(pg, "ka")[:, t:t + 1], ALU.add, ALU.mult)
            link(last)
            link(dve.scalar_tensor_tensor(out=kT, in0=e[:, :, :], scalar=1.0, in1=kT, op0=ALU.add, op1=ALU.mult))
            dve.sem_inc(logs_made.sem, 1)
            dve.wait_ge(exps_made.sem, exps_made.at(1))
            ar = r["ar"]
            view = lambda x: x.rearrange("p t (b s) -> p t b s", s=P)
            chunks = lambda x: x.rearrange("p t (n s) -> p t n s", s=CH)
            for t in range(KH):
                dve.scalar_tensor_tensor(out=ar[:, t, :, 0, :], in0=view(kk[:, :, :])[:, t], scalar=-1.0,
                                         in1=view(lw[:, :, :])[:, t], op0=ALU.mult, op1=ALU.mult)
                dve.tensor_tensor(ar[:, t, :, 1, :], view(rT)[:, t], view(e[:, :, :])[:, t], ALU.mult)
            link(dve.tensor_copy(r["p_end"][:, :, :], chunks(e[:, :, :])[:, :, :, CH - 1]))
            link(dve.tensor_tensor(kk[:, :, :], kk[:, :, :], av[:, :, :], ALU.mult))
            link(dve.tensor_tensor(r["b"][:, :, :], kk[:, :, :], cum[:, :, :], ALU.mult))
            link(dve.tensor_tensor(r["k"][:, :, :], kT, cum[:, :, :], ALU.mult))
            for x in ("b", "k"):
                for t in range(KH):
                    dve.tensor_tensor(chunks(r[x + "_end"][:, :, :])[:, t], chunks(r[x][:, :, :])[:, t],
                                      r["p_end"][:, t, :].rearrange("p (n a) -> p n a", a=1).to_broadcast([P, NCH, CH]),
                                      ALU.mult)
            link(dve.tensor_tensor(e[:, :, :], rT, kT, ALU.mult))
            for t in range(KH):
                last = dve.tensor_scalar(e[:, t, :], e[:, t, :], vec(pg, "rk")[:, t:t + 1], None, ALU.mult)
            link(last)
            dve.sem_inc(rk_made.sem, 1)
            dve.wait_ge(rk_summed.sem, rk_summed.at(1))
            for t in range(KH):
                last = dve.tensor_tensor(r["bonus"][:, t, :], ps[t][:, :], v[:, t, :], ALU.mult)
            link(last)
    small_loaded.passed(16 * loads)
    squashed.passed(2)
    for s in (low, low_taken):
        s.passed(4 * len(kinds))
    kk_squared.passed(KH)
    for s in (kk_made, kk_summed, kk_rooted, logs_made, exps_made, rk_made, rk_summed) + \
            ((lora_in, lora_in_taken) if layer else ()):
        s.passed(1)


LEVELS = 5
TOK, GRAM, LOW = 1, 2, 3
INNER = lambda level: 2 + 2 * level
OUTER = lambda level: 3 + 2 * level
AKV, XZ, RQ, Y, FH = 14, 15, 16, 17, 18
BATCHES = 18
V_GRAM, V_LOW = 1, 2
V_INNER = lambda level: 1 + 2 * level
V_OUTER = lambda level: 2 + 2 * level
V_RQ, V_F = 13, 14
V_BATCHES = 14
A_TOK, A_AKV, A_XZ, A_Y, A_H = 1, 2, 3, 4, 5
A_BATCHES = 5


def rwkv_chunks(pg, r, st):
    nc, c = pg.nc, pg.c
    done, v_taken, a_taken = ([pg.counts(f"{n}{g}") for g in range(2)]
                              for n in ("chunk_summed", "chunk_vector_taken", "chunk_scalar_taken"))
    cleared, vec_step = pg.counts("chunk_cleared"), pg.counts("vec_step")
    with ExitStack() as ctx:
        def buf(name, shape):
            return [ctx.enter_context(pg.sbuf(f"{name}{g}", shape, F32)) for g in range(2)]
        tok = buf("tok", [P, 2, 4, P])
        gram = buf("gram", [P, 4, 3, P])
        low = buf("low", [P, 4, P])
        inv, invT, inner = (buf(n, [P, 4, P]) for n in ("inv", "invT", "inner"))
        akv = buf("akv", [P, 4, HEAD])
        xz = [st["xz"][:, g, :].rearrange("p (u a n) -> p u a n", u=4, a=2) for g in range(2)]
        ps = [ctx.enter_context(pg.psum(f"chunk_ps{b}", [P, 4, P], F32)) for b in range(8)]
        own = [[ps[b] for b in (0, 1, 2, 6)], [ps[b] for b in (3, 4, 5, 7)]]
        block = ctx.enter_context(nc.Block())

        def units(pp):
            return [(u, 2 * pp + u // 2, u // 2, u % 2, slice(64 * (u % 2), 64 * (u % 2) + 64)) for u in range(4)]

        @block.gpsimd
        def _(pool):
            pool.memset(st["f"][:, :, :, :], 0.0).then_inc(cleared.sem, 1)
            pool.memset(st["hh"][:, :, :, :], 0.0).then_inc(cleared.sem, 1)

        @block.tensor
        def _(pe):
            for tb in range(TB):
                tok_s = slice(tb * P, (tb + 1) * P)

                def vector(g, n):
                    pe.wait_ge(v_taken[g].sem, v_taken[g].at(tb * V_BATCHES + n))

                def scalar(g, n):
                    pe.wait_ge(a_taken[g].sem, a_taken[g].at(tb * A_BATCHES + n))

                for g in range(2):
                    if g:
                        vector(0, V_LOW)
                        scalar(0, A_TOK)
                    elif tb:
                        for o in range(2):
                            vector(o, 0)
                            scalar(o, 0)
                    for q in range(2):
                        p = 2 * g + q
                        for j, x in enumerate((r["ar"][:, p, tb, 0, :], r["b_end"][:, p, tok_s],
                                               r["k_end"][:, p, tok_s], r["v"][:, p, tok_s])):
                            last = pe.transpose(ps[q][:, j, :], x, c["ident"][:, :])
                    last.then_inc(done[g].sem, 1)
                    for u, p, q, hh, hs in units(g):
                        rhs = r["ar"][hs, p, tb, :, :]
                        pe.matmul(ps[2 + u][:, 0:2, :], r["b"][hs, p, tok_s], rhs, start=True, stop=True)
                        last = pe.matmul(ps[2 + u][:, 2:4, :], r["k"][hs, p, tok_s], rhs, start=True, stop=True)
                    last.then_inc(done[g].sem, 1)
                    for u, p, q, hh, hs in units(g):
                        last = pe.matmul(ps[6 + hh][:, q, :], r["ar"][hs, p, tb, 0, :], r["b"][hs, p, tok_s],
                                         start=True, stop=True)
                    last.then_inc(done[g].sem, 1)
                vector(1, V_LOW)
                scalar(1, A_TOK)
                for lv in range(1, LEVELS + 1):
                    for g in range(2):
                        vector(g, V_OUTER(lv - 1) if lv > 1 else V_LOW)
                        for u in range(4):
                            last = pe.matmul(own[g][0][:, u, :], low[g][:, u, :], invT[g][:, u, :], start=True, stop=True)
                        last.then_inc(done[g].sem, 1)
                    for g in range(2):
                        vector(g, V_INNER(lv))
                        for u in range(4):
                            last = pe.matmul(own[g][1][:, u, :], inv[g][:, u, :], inner[g][:, u, :], start=True, stop=True)
                        if lv < LEVELS:
                            for u in range(4):
                                last = pe.matmul(own[g][2][:, u, :], inner[g][:, u, :], inv[g][:, u, :],
                                                 start=True, stop=True)
                        last.then_inc(done[g].sem, 1)
                for g in range(2):
                    for u, p, q, hh, hs in units(g):
                        last = pe.matmul(own[g][0][:, u, 0:HEAD], gram[g][:, u, 1, :], tok[g][:, q, 3, hs],
                                         start=True, stop=True)
                    last.then_inc(done[g].sem, 1)
                for g in range(2):
                    vector(g, V_OUTER(LEVELS))
                    scalar(g, A_AKV)
                    for u, p, q, hh, hs in units(g):
                        pe.matmul(own[g][3][:, u, 0:HEAD], invT[g][:, u, :], tok[g][:, q, 0, hs], start=True, stop=True)
                        last = pe.matmul(own[g][3][:, u, HEAD:P], invT[g][:, u, :], akv[g][:, u, :], start=True, stop=True)
                    last.then_inc(done[g].sem, 1)
                for g in range(2):
                    scalar(g, A_XZ)
                    for u, p, q, hh, hs in units(g):
                        last = pe.matmul(own[g][1][hs, q, :], xz[g][:, u, 0, :], gram[g][:, u, 0, :], start=True, stop=True)
                    last.then_inc(done[g].sem, 1)
                    for u, p, q, hh, hs in units(g):
                        pe.matmul(own[g][2][hs, q, :], xz[g][:, u, 1, :], gram[g][:, u, 0, :], start=True, stop=False)
                        last = pe.matmul(own[g][2][hs, q, :], tok[g][:, q, 3, hs], gram[g][:, u, 2, :],
                                         start=False, stop=True)
                    last.then_inc(done[g].sem, 1)
                for g in range(2):
                    vector(g, V_RQ)
                    scalar(g, A_Y)
                    for ch in range(2):
                        rows, f_bank, h_bank = slice(64 * ch, 64 * ch + 64), own[g][3 * ch], own[g][1 + ch]
                        for u, p, q, hh, hs in units(g):
                            pe.matmul(f_bank[hs, q, 0:HEAD], xz[g][rows, u, 0, :], tok[g][rows, q, 1, hs],
                                      start=True, stop=True)
                            pe.matmul(h_bank[hs, q, 0:HEAD], tok[g][rows, q, 1, hs], xz[g][rows, u, 1, :],
                                      start=True, stop=False)
                            last = pe.matmul(h_bank[hs, q, 0:HEAD], tok[g][rows, q, 2, hs], tok[g][rows, q, 3, hs],
                                             start=False, stop=True)
                    last.then_inc(done[g].sem, 1)

        @block.vector
        def _(dve):
            link = linker(dve, vec_step)
            four = lambda x: x.rearrange("p (a n) -> p a n", a=1).to_broadcast([P, 4, P])
            for tb in range(TB):
                def await_sum(g, n):
                    dve.wait_ge(done[g].sem, done[g].at(tb * BATCHES + n))

                for g in range(2):
                    await_sum(g, GRAM)
                    for u in range(4):
                        dve.tensor_tensor(gram[g][:, u, :, :], ps[2 + u][:, 1:4, :], c["gram_mask"][:, 1:4, :], ALU.mult)
                        last = dve.tensor_tensor(invT[g][:, u, :], ps[2 + u][:, 0, :], c["level_mask"][:, 0, :], ALU.mult)
                    last.then_inc(v_taken[g].sem, 1)
                    dve.wait_ge(v_taken[g].sem, v_taken[g].at(tb * V_BATCHES + V_GRAM))
                    dve.tensor_tensor(invT[g][:, :, :], invT[g][:, :, :], four(c["ident"][:, :]), ALU.add)
                    await_sum(g, LOW)
                    for u in range(4):
                        last = dve.tensor_tensor(low[g][:, u, :], ps[6 + u % 2][:, u // 2, :], c["lower_mask"][:, :], ALU.mult)
                    link(last)
                    link(dve.tensor_tensor(inv[g][:, :, :], low[g][:, :, :], four(c["level0_lower"][:, :]), ALU.mult))
                    dve.tensor_tensor(inv[g][:, :, :], inv[g][:, :, :], four(c["ident"][:, :]), ALU.add) \
                        .then_inc(v_taken[g].sem, 1)
                for lv in range(1, LEVELS + 1):
                    for g in range(2):
                        await_sum(g, INNER(lv))
                        dve.tensor_tensor(inner[g][:, :, :], own[g][0][:, :, :], four(c["level_mask"][:, lv, :]), ALU.mult) \
                            .then_inc(v_taken[g].sem, 1)
                    for g in range(2):
                        await_sum(g, OUTER(lv))
                        last = dve.tensor_tensor(invT[g][:, :, :], invT[g][:, :, :], own[g][1][:, :, :], ALU.add)
                        if lv < LEVELS:
                            last = dve.tensor_tensor(inv[g][:, :, :], inv[g][:, :, :], own[g][2][:, :, :], ALU.add)
                        last.then_inc(v_taken[g].sem, 1)
                        dve.wait_ge(v_taken[g].sem, v_taken[g].at(tb * V_BATCHES + V_OUTER(lv)))
                for g in range(2):
                    await_sum(g, RQ)
                    dve.tensor_tensor(st["rq"][:, 2 * g:2 * g + 2, tb * P:(tb + 1) * P], own[g][1][:, 0:2, :],
                                      r["ar"][:, 2 * g:2 * g + 2, tb, 1, :], ALU.add).then_inc(v_taken[g].sem, 1)
                if tb == 0:
                    dve.wait_ge(cleared.sem, cleared.at(2))
                for g in range(2):
                    await_sum(g, FH)
                    for ch in range(2):
                        for u, p, q, hh, hs in units(g):
                            last = dve.scalar_tensor_tensor(
                                out=st["f"][hs, 2 * tb + ch, p, hs], in0=c["ident"][hs, hs],
                                scalar=r["p_end"][hs, p, 2 * tb + ch:2 * tb + ch + 1], in1=own[g][3 * ch][hs, q, 0:HEAD],
                                op0=ALU.mult, op1=ALU.add)
                    last.then_inc(v_taken[g].sem, 1)

        @block.scalar
        def _(act):
            for tb in range(TB):
                def await_sum(g, n):
                    act.wait_ge(done[g].sem, done[g].at(tb * BATCHES + n))

                for g in range(2):
                    await_sum(g, TOK)
                    for q in range(2):
                        last = act.activation(tok[g][:, q, :, :], ps[q][:, :, :], ACT.Copy)
                    last.then_inc(a_taken[g].sem, 1)
                for g in range(2):
                    await_sum(g, AKV)
                    act.activation(akv[g][:, :, :], own[g][0][:, :, 0:HEAD], ACT.Copy).then_inc(a_taken[g].sem, 1)
                for g in range(2):
                    await_sum(g, XZ)
                    act.activation(xz[g].rearrange("p u a n -> p u (a n)"), own[g][3][:, :, :], ACT.Copy) \
                        .then_inc(a_taken[g].sem, 1)
                for g in range(2):
                    await_sum(g, Y)
                    act.activation(st["y"][:, 2 * g:2 * g + 2, tb * P:(tb + 1) * P], own[g][2][:, 0:2, :], ACT.Copy) \
                        .then_inc(a_taken[g].sem, 1)
                if tb == 0:
                    act.wait_ge(cleared.sem, cleared.at(2))
                for g in range(2):
                    await_sum(g, FH)
                    for ch in range(2):
                        for hh in range(2):
                            hs = slice(64 * hh, 64 * hh + 64)
                            last = act.activation(st["hh"][hs, 2 * tb + ch, 2 * g:2 * g + 2, hs],
                                                  own[g][1 + ch][hs, 0:2, 0:HEAD], ACT.Copy)
                    last.then_inc(a_taken[g].sem, 1)
    for g in range(2):
        done[g].passed(BATCHES * TB)
        v_taken[g].passed(V_BATCHES * TB)
        a_taken[g].passed(A_BATCHES * TB)
    cleared.passed(2)


def rwkv_states(pg, st):
    nc = pg.nc
    moved, stepped = pg.counts("state_multiplied"), pg.counts("state_stepped")
    y_summed, y_taken = pg.counts("y_summed"), pg.counts("y_taken")
    with ExitStack() as ctx:
        ps = [ctx.enter_context(pg.psum(f"state_ps{b}", [P, KH, P], F32)) for b in range(2)]
        yps = [ctx.enter_context(pg.psum(f"state_yps{t}", [P, T], F32)) for t in range(KH)]
        block = ctx.enter_context(nc.Block())

        @block.tensor
        def _(pe):
            for n in range(1, NCH):
                if n >= 2:
                    pe.wait_ge(stepped.sem, stepped.at(n - 1))
                for p in range(KH):
                    last = pe.matmul(ps[n % 2][:, p, :], st["f"][:, n, p, :], st["hh"][:, n - 1, p, :],
                                     start=True, stop=True)
                last.then_inc(moved.sem, 1)
                for t in range(KH):
                    last = pe.matmul(yps[t][:, n * CH:(n + 1) * CH], st["hh"][:, n - 1, t, :],
                                     st["rq"][:, t, n * CH:(n + 1) * CH], start=True, stop=True)
                if n == NCH - 1:
                    last.then_inc(y_summed.sem, 1)

        @block.vector
        def _(dve):
            for n in range(1, NCH):
                dve.wait_ge(moved.sem, moved.at(n))
                dve.tensor_tensor(st["hh"][:, n, :, :], st["hh"][:, n, :, :], ps[n % 2][:, :, :], ALU.add) \
                    .then_inc(stepped.sem, 1)
            dve.wait_ge(y_summed.sem, y_summed.at(1))
            for t in range(KH):
                last = dve.tensor_tensor(st["y"][:, t, CH:T], st["y"][:, t, CH:T], yps[t][:, CH:T], ALU.add)
            last.then_inc(y_taken.sem, 1)
    moved.passed(NCH - 1)
    stepped.passed(NCH - 1)
    y_summed.passed(1)
    y_taken.passed(1)


def rwkv_finish(pg, r, st, mixT):
    nc, y, v = pg.nc, st["y"], st["rq"]
    summed, squared, rooted = pg.counts("gn_summed"), pg.counts("gn_squared"), pg.counts("gn_rooted")
    centred, varied = pg.counts("gn_centred"), pg.counts("gn_varied")
    vec_step = pg.counts("vec_step")
    with ExitStack() as ctx:
        ps = [ctx.enter_context(pg.psum(f"gn_ps{b}", [P, T], F32)) for b in range(8)]
        block = ctx.enter_context(nc.Block())

        @block.tensor
        def _(pe):
            for t in range(KH):
                last = pe.matmul(ps[t][:, :], pg.c["head_ones"][:, :], y[:, t, :], start=True, stop=True)
            last.then_inc(summed.sem, 1)
            pe.wait_ge(squared.sem, squared.at(1))
            for t in range(KH):
                last = pe.matmul(ps[4 + t][:, :], pg.c["head_ones"][:, :], v[:, t, :], start=True, stop=True)
            last.then_inc(summed.sem, 1)

        @block.scalar
        def _(act):
            act.wait_ge(centred.sem, centred.at(1))
            act.activation(v[:, :, :], y[:, :, :], ACT.Square).then_inc(squared.sem, 1)
            act.wait_ge(varied.sem, varied.at(1))
            act.activation(v[:, :, :], v[:, :, :], ACT.Sqrt).then_inc(rooted.sem, 1)

        @block.vector
        def _(dve):
            link = linker(dve, vec_step)
            dve.wait_ge(summed.sem, summed.at(1))
            for t in range(KH):
                last = dve.scalar_tensor_tensor(out=y[:, t, :], in0=ps[t][:, :], scalar=-1.0 / HEAD, in1=y[:, t, :],
                                                op0=ALU.mult, op1=ALU.add)
            link(last)
            dve.sem_inc(centred.sem, 1)
            dve.wait_ge(summed.sem, summed.at(2))
            for t in range(KH):
                last = dve.tensor_scalar(v[:, t, :], ps[4 + t][:, :], 1.0 / HEAD, GN_EPS, ALU.mult, ALU.add)
            link(last)
            dve.sem_inc(varied.sem, 1)
            dve.wait_ge(rooted.sem, rooted.at(1))
            link(dve.reciprocal(v[:, :, :], v[:, :, :]))
            link(dve.tensor_tensor(y[:, :, :], y[:, :, :], v[:, :, :], ALU.mult))
            for t in range(KH):
                last = dve.tensor_scalar(y[:, t, :], y[:, t, :], vec(pg, "lnx_g")[:, t:t + 1],
                                         vec(pg, "lnx_b")[:, t:t + 1], ALU.mult, ALU.add)
            link(last)
            link(dve.tensor_tensor(y[:, :, :], y[:, :, :], r["bonus"][:, :, :], ALU.add))
            link(dve.tensor_tensor(mixT[:, 0:KH, :], y[:, :, :], mixT[:, 0:KH, :], ALU.mult))
    summed.passed(2)
    for s in (squared, rooted, centred, varied):
        s.passed(1)


def s5(pg, layer, mixT):
    nc = pg.nc
    with ExitStack() as whole:
        def buf(own, name, shape):
            return own.enter_context(pg.sbuf(name, shape, F32))
        yT = mixT[:, KH:KD, :]
        own = whole.enter_context(ExitStack())
        s = {n: buf(own, n, sh) for n, sh in (
            ("e_in", [P, 2, SC, 4, P]),
            ("g_re", [P, SC + 1, S5_PAIRS, 32]), ("g_im", [P, SC + 1, S5_PAIRS, 32]),
            ("taps", [P, 4, SC, P]), ("rot", [P, 2, S5_PAIRS, SN]), ("keep", [P, S5_PAIRS, SN]))}
        s5_tables(pg, layer, s)
        s5_run(pg, layer, s, mixT, yT)
        own.close()
        glu = buf(whole, "s5_glu", [P, KH, T])
        project(pg, pg.dram["glu_w"][layer], KH, KH, yT, T, glu)
        s5_gate(pg, yT, glu, mixT)


def s5_tables(pg, layer, s):
    nc, dram = pg.nc, pg.dram
    loaded, cleared = pg.counts("s5_loaded"), pg.counts("s5_cleared")
    dt_made, ready, trig = pg.counts("s5_dt_made"), pg.counts("s5_angles_made"), pg.counts("s5_trig_made")
    powers, in_made, out_made = pg.counts("s5_powers_made"), pg.counts("s5_in_made"), pg.counts("s5_out_made")
    flipped, flip_taken = pg.counts("s5_flipped"), pg.counts("s5_flip_taken")
    tapped, vec_step, pool_step = pg.counts("s5_tapped"), pg.counts("vec_step"), pg.counts("pool_step")
    taps_cleared = pg.counts("s5_taps_cleared")
    with ExitStack() as ctx:
        def buf(name, shape):
            return ctx.enter_context(pg.sbuf(name, shape, F32))
        small = buf("s5_small", [P, 24, S5_PAIRS])
        are, aim, dt, lre, ang, ang8, cosv, sinv, mag, den, c1r, c1i, t0, t1, t2, t3, cos8, sin8, m8, er, ei, sq8 = \
            (small[:, i, :] for i in range(22))
        lam = buf("s5_lam", [P, 2, SC + 1, S5_PAIRS])
        b_raw, c_raw = buf("s5_b_raw", [P, 2, S5_PAIRS, 32]), buf("s5_c_raw", [P, 2, S5_PAIRS, 32])
        bb = buf("s5_bb", [P, 2, S5_PAIRS, 32])
        lb = buf("s5_lb", [P, 2, SC, S5_PAIRS, 32])
        tmp_v = buf("s5_tmp_v", [P, 2, S5_PAIRS * 32])
        tmp_p = buf("s5_tmp_p", [P, 2, S5_PAIRS * 32])
        ps = [ctx.enter_context(pg.psum(f"s5t_ps{b}", [P, 4, P], F32)) for b in range(8)]
        block = ctx.enter_context(nc.Block())

        @block.sync
        def _(sp):
            for x, n in ((are, "s5_are"), (aim, "s5_aim"), (dt, "s5_dt")):
                sp.dma_start(x, dram[n][layer]).then_inc(loaded.sem, 16)
            sp.wait_ge(cleared.sem, cleared.at(2))
            for raw, names in ((b_raw, ("s5_bre", "s5_bim")), (c_raw, ("s5_cre", "s5_cim"))):
                for part, n in enumerate(names):
                    view = dram[n][layer].rearrange("(q g) p c -> g p q c", g=2)
                    for g in range(2):
                        sp.dma_start(raw[64 * g:64 * g + 64, part, :, 16 * g:16 * g + 16], view[g]).then_inc(loaded.sem, 16)

        @block.scalar
        def _(act):
            act.wait_ge(loaded.sem, loaded.at(16 * 11))
            act.activation(dt, dt, ACT.Exp).then_inc(dt_made.sem, 1)
            act.wait_ge(ready.sem, ready.at(1))
            act.activation(mag, t0, ACT.Exp)
            act.activation(m8, t0, ACT.Exp, scale=8.0).then_inc(trig.sem, 1)
            act.activation(sinv, t1, ACT.Sin)
            act.activation(cosv, t2, ACT.Sin).then_inc(trig.sem, 1)
            act.wait_ge(ready.sem, ready.at(2))
            act.activation(sin8, t1, ACT.Sin)
            act.activation(cos8, t2, ACT.Sin).then_inc(trig.sem, 1)
            for m in range(16):
                act.wait_ge(flipped.sem, flipped.at(m + 1))
                act.activation(s["e_in"][:, m // 8, m % 8, :, :], ps[m % 4][:, :, :], ACT.Copy).then_inc(flip_taken.sem, 1)

        @block.tensor
        def _(pe):
            for m in range(16):
                part, k = m // 8, m % 8
                if m >= 4:
                    pe.wait_ge(flip_taken.sem, flip_taken.at(m - 3))
                if m == 0:
                    pe.wait_ge(in_made.sem, in_made.at(1))
                for t in range(4):
                    last = pe.transpose(ps[m % 4][:, t, :],
                                        lb[:, part, SC - 1 - k, 4 * t:4 * t + 4, :].rearrange("p q c -> p (q c)"),
                                        pg.c["ident"][:, :])
                last.then_inc(flipped.sem, 1)
            pe.wait_ge(out_made.sem, out_made.at(1))
            for q in range(S5_PAIRS):
                rows = slice(32 * (q % 4), 32 * (q % 4) + 32)
                o = ps[4 + q // 4][rows, :, :].rearrange("p a n -> p (a n)")[:, 0:SC * 32]
                pe.matmul(o, bb[:, 0, q, :], s["g_re"][:, 0:SC, q, :], start=True, stop=False)
                last = pe.matmul(o, bb[:, 1, q, :], s["g_im"][:, 0:SC, q, :], start=False, stop=True)
            last.then_inc(tapped.sem, 1)

        @block.gpsimd
        def _(pool):
            link = linker(pool, pool_step)
            pool.memset(b_raw[:, :, :, :], 0.0).then_inc(cleared.sem, 1)
            pool.memset(c_raw[:, :, :, :], 0.0).then_inc(cleared.sem, 1)
            pool.memset(s["taps"][:, :, :, :], 0.0).then_inc(taps_cleared.sem, 1)
            pool.wait_ge(powers.sem, powers.at(1))
            for k in range(SC):
                lr, li = (lam[:, part, k, :].rearrange("p (q a) -> p q a", a=1).to_broadcast([P, S5_PAIRS, 32])
                          for part in range(2))
                ta, tb = (tmp_p[:, j, :].rearrange("p (q c) -> p q c", c=32) for j in range(2))
                pool.tensor_tensor(ta, bb[:, 0], lr, ALU.mult)
                link(pool.tensor_tensor(tb, bb[:, 1], li, ALU.mult))
                link(pool.tensor_tensor(lb[:, 0, k], ta, tb, ALU.subtract))
                pool.tensor_tensor(ta, bb[:, 0], li, ALU.mult)
                link(pool.tensor_tensor(tb, bb[:, 1], lr, ALU.mult))
                link(pool.tensor_tensor(lb[:, 1, k], ta, tb, ALU.add))
            pool.sem_inc(in_made.sem, 1)

        @block.vector
        def _(dve):
            link = linker(dve, vec_step)
            tt = lambda o, a, b, op: link(dve.tensor_tensor(o, a, b, op))

            def reduce_angle(out, angle, shift):
                link(dve.tensor_scalar(t3, angle, shift, None, ALU.add))
                link(dve.tensor_scalar(den, t3, 1.0 / (2 * math.pi), None, ALU.mult))
                link(dve.tensor_scalar(den, den, ROUND, None, ALU.add))
                link(dve.tensor_scalar(den, den, -ROUND, None, ALU.add))
                link(dve.scalar_tensor_tensor(out=t3, in0=den, scalar=-TWO_PI_HI, in1=t3, op0=ALU.mult, op1=ALU.add))
                link(dve.scalar_tensor_tensor(out=t3, in0=den, scalar=-TWO_PI_LO, in1=t3, op0=ALU.mult, op1=ALU.add))
                link(dve.tensor_scalar(out, t3, PI_IN, -PI_IN, ALU.min, ALU.max))

            dve.wait_ge(dt_made.sem, dt_made.at(1))
            link(dve.tensor_scalar(lre, are, -1e-4, None, ALU.min))
            tt(t0, lre, dt, ALU.mult)
            tt(ang, aim, dt, ALU.mult)
            reduce_angle(t1, ang, 0.0)
            link(dve.tensor_copy(ang, t1))
            reduce_angle(t2, ang, math.pi / 2)
            dve.sem_inc(ready.sem, 1)
            dve.wait_ge(trig.sem, trig.at(2))
            link(dve.tensor_scalar(ang8, ang, float(SC), None, ALU.mult))
            reduce_angle(t1, ang8, 0.0)
            link(dve.tensor_copy(ang8, t1))
            reduce_angle(t2, ang8, math.pi / 2)
            dve.sem_inc(ready.sem, 1)
            link(dve.memset(lam[:, 0, 0, :], 1.0))
            link(dve.memset(lam[:, 1, 0, :], 0.0))
            tt(lam[:, 0, 1, :], mag, cosv, ALU.mult)
            tt(lam[:, 1, 1, :], mag, sinv, ALU.mult)
            dve.wait_ge(trig.sem, trig.at(3))
            lbr, lbi = lam[:, 0, 1, :], lam[:, 1, 1, :]
            tt(t0, lre, lre, ALU.mult)
            tt(t1, aim, aim, ALU.mult)
            tt(den, t0, t1, ALU.add)
            link(dve.reciprocal(den, den))
            link(dve.tensor_scalar(t3, lbr, -1.0, None, ALU.add))
            tt(t0, t3, lre, ALU.mult)
            tt(t1, lbi, aim, ALU.mult)
            tt(t0, t0, t1, ALU.add)
            tt(c1r, t0, den, ALU.mult)
            tt(t0, lbi, lre, ALU.mult)
            tt(t1, t3, aim, ALU.mult)
            tt(t0, t0, t1, ALU.subtract)
            tt(c1i, t0, den, ALU.mult)
            for k in range(2, SC + 1):
                a, b = lam[:, 0, k - 1, :], lam[:, 1, k - 1, :]
                tt(t0, a, lbr, ALU.mult)
                tt(t1, b, lbi, ALU.mult)
                tt(lam[:, 0, k, :], t0, t1, ALU.subtract)
                tt(t0, a, lbi, ALU.mult)
                tt(t1, b, lbr, ALU.mult)
                tt(lam[:, 1, k, :], t0, t1, ALU.add)
            wide = lambda x: x.rearrange("p (q a) -> p q a", a=1).to_broadcast([P, S5_PAIRS, 32])
            ta, tb = (tmp_v[:, j, :].rearrange("p (q c) -> p q c", c=32) for j in range(2))
            dve.wait_ge(loaded.sem, loaded.at(16 * 11))
            tt(ta, b_raw[:, 0], wide(c1r), ALU.mult)
            tt(tb, b_raw[:, 1], wide(c1i), ALU.mult)
            tt(bb[:, 0], ta, tb, ALU.subtract)
            tt(ta, b_raw[:, 1], wide(c1r), ALU.mult)
            tt(tb, b_raw[:, 0], wide(c1i), ALU.mult)
            tt(bb[:, 1], ta, tb, ALU.add)
            dve.sem_inc(powers.sem, 1)
            for k in range(SC + 1):
                lr, li = wide(lam[:, 0, k, :]), wide(lam[:, 1, k, :])
                tt(ta, c_raw[:, 0], lr, ALU.mult)
                tt(tb, c_raw[:, 1], li, ALU.mult)
                tt(s["g_re"][:, k], ta, tb, ALU.subtract)
                tt(ta, c_raw[:, 0], li, ALU.mult)
                tt(tb, c_raw[:, 1], lr, ALU.mult)
                link(dve.scalar_tensor_tensor(out=s["g_im"][:, k], in0=ta, scalar=-1.0, in1=tb, op0=ALU.mult, op1=ALU.subtract))
            dve.sem_inc(out_made.sem, 1)
            rr, ri = s["rot"][:, 0], s["rot"][:, 1]
            link(dve.memset(rr[:, :, 0:1], 1.0))
            link(dve.memset(ri[:, :, 0:1], 0.0))
            link(dve.tensor_copy(er, cos8))
            link(dve.tensor_copy(ei, sin8))
            n = 1
            while n < SN:
                er_n, ei_n = (x.rearrange("p (q a) -> p q a", a=1).to_broadcast([P, S5_PAIRS, n]) for x in (er, ei))
                ta, tb = (tmp_v[:, j, 0:S5_PAIRS * n].rearrange("p (q c) -> p q c", c=n) for j in range(2))
                tt(ta, rr[:, :, 0:n], er_n, ALU.mult)
                tt(tb, ri[:, :, 0:n], ei_n, ALU.mult)
                tt(rr[:, :, n:2 * n], ta, tb, ALU.subtract)
                tt(ta, rr[:, :, 0:n], ei_n, ALU.mult)
                tt(tb, ri[:, :, 0:n], er_n, ALU.mult)
                tt(ri[:, :, n:2 * n], ta, tb, ALU.add)
                tt(t0, er, er, ALU.mult)
                tt(t1, ei, ei, ALU.mult)
                tt(t2, er, ei, ALU.mult)
                tt(er, t0, t1, ALU.subtract)
                tt(ei, t2, t2, ALU.add)
                n *= 2
            link(dve.tensor_copy(s["keep"][:, :, :], m8.rearrange("p (q a) -> p q a", a=1).to_broadcast([P, S5_PAIRS, SN])))
            link(dve.memset(s["keep"][:, :, 0:1], 0.0))
            dve.wait_ge(tapped.sem, tapped.at(1))
            dve.wait_ge(taps_cleared.sem, taps_cleared.at(1))
            for t in range(4):
                for g in range(4):
                    rows = slice(32 * g, 32 * g + 32)
                    last = dve.tensor_copy(s["taps"][rows, t, :, rows],
                                           ps[4 + t][rows, :, :].rearrange("p a n -> p (a n)")[:, 0:SC * 32]
                                           .rearrange("p (k n) -> p k n", n=32))
            link(last)
    loaded.passed(16 * 11)
    for x, k in ((cleared, 2), (dt_made, 1), (ready, 2), (trig, 3), (powers, 1), (in_made, 1), (out_made, 1),
                 (flipped, 16), (flip_taken, 16), (tapped, 1), (taps_cleared, 1)):
        x.passed(k)


def s5_run(pg, layer, s, mixT, yT):
    nc = pg.nc
    uT = mixT[:, KH:KD, :]
    u8 = uT.rearrange("p t (n s) -> p t n s", s=SC)
    s_in, turned, scanned, x_made = (pg.counts(n) for n in ("s5_in_summed", "s5_turned", "s5_scanned", "s5_states_made"))
    y_in, skipped, gelued = pg.counts("s5_y_summed"), pg.counts("s5_skipped"), pg.counts("s5_gelued")
    cleared, vec_step = pg.counts("s5_state_cleared"), pg.counts("vec_step")
    with ExitStack() as ctx:
        def buf(name, shape):
            return ctx.enter_context(pg.sbuf(name, shape, F32))
        rot, sc, x = buf("s5_rot_in", [P, 2, S5_PAIRS, SN]), buf("s5_scan", [P, 2, S5_PAIRS, SN]), buf("s5_x", [P, 2, S5_PAIRS, SN + 1])
        tmp = buf("s5_tmp", [P, 2, S5_PAIRS, SN])
        with ExitStack() as one:
            sps = [one.enter_context(pg.psum(f"s5s_ps{b}", [P, 4, 2, SN], F32)) for b in range(4)]
            yps = [one.enter_context(pg.psum(f"s5y_ps{b}", [P, SN, SC], F32)) for b in range(4)]
            block = one.enter_context(nc.Block())

            @block.gpsimd
            def _(pool):
                pool.memset(x[:, :, :, 0:1], 0.0).then_inc(cleared.sem, 1)

            @block.tensor
            def _(pe):
                for t in range(4):
                    for part in range(2):
                        for k in range(SC):
                            for g in range(4):
                                rows = slice(32 * g, 32 * g + 32)
                                last = pe.matmul(sps[g][:, t, part, :], s["e_in"][rows, part, k, t, :],
                                                 u8[rows, t, :, k], start=(k == 0), stop=(k == SC - 1))
                last.then_inc(s_in.sem, 1)
                for t in range(4):
                    for k in range(SC):
                        pe.matmul(yps[t][:, :, k:SC], s["taps"][:, t, k, :], u8[:, t, :, 0:SC - k],
                                  start=(k == 0), stop=False, skip_group_check=True)
                pe.wait_ge(x_made.sem, x_made.at(1))
                pe.wait_ge(cleared.sem, cleared.at(1))
                for t in range(4):
                    for k in range(SC):
                        for part, g_map in enumerate((s["g_re"], s["g_im"])):
                            for g in range(4):
                                q, rows = 4 * t + g, slice(32 * g, 32 * g + 32)
                                last = pe.matmul(yps[t][rows, :, k], g_map[:, k + 1, q, :], x[:, part, q, 0:SN],
                                                 start=False, stop=part == 1, skip_group_check=True)
                    last.then_inc(y_in.sem, 1)

            @block.vector
            def _(dve):
                link = linker(dve, vec_step)
                tt = lambda o, a, b, op: link(dve.tensor_tensor(o, a, b, op))
                dve.wait_ge(s_in.sem, s_in.at(1))
                by_row = lambda v: v.rearrange("p (t g) n -> p g t n", g=4)
                for g in range(4):
                    sr, si = sps[g][:, :, 0, :], sps[g][:, :, 1, :]
                    cr, ci = by_row(s["rot"][:, 0])[:, g], by_row(s["rot"][:, 1])[:, g]
                    dve.tensor_tensor(by_row(tmp[:, 0])[:, g], sr, cr, ALU.mult)
                    dve.tensor_tensor(by_row(tmp[:, 1])[:, g], si, ci, ALU.mult)
                    dve.tensor_tensor(by_row(sc[:, 0])[:, g], sr, ci, ALU.mult)
                    last = dve.tensor_tensor(by_row(sc[:, 1])[:, g], si, cr, ALU.mult)
                link(last)
                dve.tensor_tensor(rot[:, 0], tmp[:, 0], tmp[:, 1], ALU.add)
                tt(rot[:, 1], sc[:, 1], sc[:, 0], ALU.subtract)
                flat = lambda v: v.rearrange("p q n -> p (q n)")
                for part in range(2):
                    last = dve.tensor_tensor_scan(flat(sc[:, part]), flat(s["keep"][:, :, :]), flat(rot[:, part]),
                                                  0.0, ALU.mult, ALU.add)
                link(last)
                dve.tensor_tensor(tmp[:, 0], sc[:, 0], s["rot"][:, 0], ALU.mult)
                tt(tmp[:, 1], sc[:, 1], s["rot"][:, 1], ALU.mult)
                dve.tensor_tensor(x[:, 0, :, 1:SN + 1], tmp[:, 0], tmp[:, 1], ALU.subtract)
                dve.tensor_tensor(rot[:, 0], sc[:, 0], s["rot"][:, 1], ALU.mult)
                tt(rot[:, 1], sc[:, 1], s["rot"][:, 0], ALU.mult)
                tt(x[:, 1, :, 1:SN + 1], rot[:, 0], rot[:, 1], ALU.add)
                dve.sem_inc(x_made.sem, 1)
                for t in range(4):
                    dve.wait_ge(y_in.sem, y_in.at(t + 1))
                    dve.scalar_tensor_tensor(out=yT[:, t, :], in0=uT[:, t, :], scalar=vec(pg, "s5_d")[:, t:t + 1],
                                             in1=yps[t][:, :, :].rearrange("p n s -> p (n s)"),
                                             op0=ALU.mult, op1=ALU.add).then_inc(skipped.sem, 1)

            @block.scalar
            def _(act):
                for t in range(4):
                    act.wait_ge(skipped.sem, skipped.at(t + 1))
                    act.activation(yT[:, t, :], yT[:, t, :], ACT.Gelu_apprx_tanh).then_inc(gelued.sem, 1)
    for a, k in ((s_in, 1), (x_made, 1), (y_in, 4), (skipped, 4), (gelued, 4), (cleared, 1)):
        a.passed(k)


def s5_gate(pg, yT, glu, mixT):
    nc = pg.nc
    gated, multiplied, squared, summed = (pg.counts(n) for n in ("glu_gated", "glu_multiplied", "glu_squared", "glu_summed"))
    meaned, rooted, vec_step = pg.counts("glu_meaned"), pg.counts("glu_rooted"), pg.counts("vec_step")
    with ExitStack() as ctx:
        rstd = ctx.enter_context(pg.sbuf("glu_rstd", [P, T], F32))
        ps = ctx.enter_context(pg.psum("glu_ps", [P, T], F32))
        block = ctx.enter_context(nc.Block())

        @block.scalar
        def _(act):
            for t in range(KH):
                act.activation(glu[:, t, :], glu[:, t, :], ACT.Sigmoid, bias=vec(pg, "glu_b")[:, t:t + 1]) \
                    .then_inc(gated.sem, 1)
            for t in range(KH):
                act.wait_ge(multiplied.sem, multiplied.at(t + 1))
                act.activation(glu[:, t, :], yT[:, t, :], ACT.Square).then_inc(squared.sem, 1)
            act.wait_ge(meaned.sem, meaned.at(1))
            act.activation(rstd[:, :], rstd[:, :], ACT.Sqrt).then_inc(rooted.sem, 1)

        @block.tensor
        def _(pe):
            for t in range(KH):
                pe.wait_ge(squared.sem, squared.at(t + 1))
                last = pe.matmul(ps[:, :], pg.c["ones"][:, :], glu[:, t, :], start=(t == 0), stop=(t == KH - 1))
            last.then_inc(summed.sem, 1)

        @block.vector
        def _(dve):
            link = linker(dve, vec_step)
            for t in range(KH):
                dve.wait_ge(gated.sem, gated.at(t + 1))
                dve.tensor_tensor(yT[:, t, :], yT[:, t, :], glu[:, t, :], ALU.mult).then_inc(multiplied.sem, 1)
            dve.wait_ge(summed.sem, summed.at(1))
            dve.tensor_scalar(rstd[:, :], ps[:, :], 1.0 / D_HALF, RMS_EPS, ALU.mult, ALU.add).then_inc(meaned.sem, 1)
            dve.wait_ge(rooted.sem, rooted.at(1))
            link(dve.reciprocal(rstd[:, :], rstd[:, :]))
            for t in range(KH):
                last = dve.scalar_tensor_tensor(out=mixT[:, KH + t, :], in0=yT[:, t, :],
                                                scalar=vec(pg, "out_g")[:, t:t + 1], in1=rstd[:, :],
                                                op0=ALU.mult, op1=ALU.mult)
            link(last)
    for a, k in ((gated, KH), (multiplied, KH), (squared, KH), (summed, 1), (meaned, 1), (rooted, 1)):
        a.passed(k)


def cross_attention(pg, layer):
    nc, dram = pg.nc, pg.dram
    loaded = pg.counts("mem_loaded")

    def buf(own, name, shape):
        return own.enter_context(pg.sbuf(name, shape, F32))

    with ExitStack() as whole:
        v = buf(whole, "xa_v", [P, 2, D])
        kT, qT, h = buf(whole, "xa_k", [P, KD, N_MEM]), buf(whole, "xa_q", [P, KD, T]), buf(whole, "xa_h", [P, KD, T])
        with ExitStack() as own:
            mem, mh = buf(own, "mem", [P, KD, N_MEM]), buf(own, "mem_h", [P, KD, N_MEM])
            with nc.Block() as block:
                @block.sync
                def _(sp):
                    sp.dma_start(mem[:, :, :], dram["memT"]).then_inc(loaded.sem, 16)
                    sp.wait_ge(loaded.sem, loaded.at(16))
            loaded.passed(16)
            norm(pg, mem, vec(pg, "norm_mem"), mh, N_MEM)
            project(pg, dram["xa_wk"][layer], KD, KD, mh, N_MEM, kT)
            memory_values(pg, layer, mh, v)
        norm(pg, pg.xT, vec(pg, "norm_xa"), h, T)
        project(pg, dram["xa_wq"][layer], KD, KD, h, T, qT)
        attend(pg, qT, kT, v, h)
        project(pg, dram["xa_wo"][layer], KD, KD, h, T, pg.xT, add=True)


def memory_values(pg, layer, mh, v):
    nc = pg.nc
    loaded, summed, taken = pg.counts("wv_loaded"), pg.counts("v_summed"), pg.counts("v_taken")
    with ExitStack() as ctx:
        w = ctx.enter_context(pg.sbuf("xa_wv", [P, KD, D], F32))
        ps = [ctx.enter_context(pg.psum(f"v_ps{b}", [P, T], F32)) for b in range(4)]
        block = ctx.enter_context(nc.Block())

        @block.sync
        def _(sp):
            sp.dma_start(w[:, :, :], pg.dram["xa_wv"][layer]).then_inc(loaded.sem, 16)

        @block.tensor
        def _(pe):
            pe.wait_ge(loaded.sem, loaded.at(16))
            for m in range(2):
                for half in range(2):
                    for k in range(KD):
                        last = pe.matmul(ps[2 * m + half][:, :], mh[:, k, m * P:(m + 1) * P],
                                         w[:, k, half * T:(half + 1) * T], start=(k == 0), stop=(k == KD - 1))
                    last.then_inc(summed.sem, 1)

        @block.scalar
        def _(act):
            for m in range(2):
                for half in range(2):
                    act.wait_ge(summed.sem, summed.at(2 * m + half + 1))
                    act.activation(v[:, m, half * T:(half + 1) * T], ps[2 * m + half][:, :], ACT.Copy) \
                        .then_inc(taken.sem, 1)
    loaded.passed(16)
    summed.passed(4)
    taken.passed(4)


def attend(pg, qT, kT, v, oT):
    nc = pg.nc
    scale = XA_HEAD ** -0.5
    scored, maxed, exped = pg.counts("xa_scored"), pg.counts("xa_maxed"), pg.counts("xa_exped")
    normed, flipped, flip_taken = pg.counts("xa_normed"), pg.counts("xa_flipped"), pg.counts("xa_flip_taken")
    mixed, mix_taken, vec_step = pg.counts("xa_mixed"), pg.counts("xa_mix_taken"), pg.counts("vec_step")
    units = [(hd, tb) for hd in range(XA_HEADS) for tb in range(TB)]
    n = len(units)
    with ExitStack() as ctx:
        def buf(name, shape):
            return ctx.enter_context(pg.sbuf(name, shape, F32))
        prob, probT = buf("xa_prob", [P, 2, N_MEM]), buf("xa_probT", [P, 2, 2, T])
        stats = buf("xa_stats", [P, 3, n])
        sps = [ctx.enter_context(pg.psum(f"xas_ps{b}", [P, N_MEM], F32)) for b in range(2)]
        fps = [ctx.enter_context(pg.psum(f"xaf_ps{b}", [P, 2, P], F32)) for b in range(2)]
        ops = [ctx.enter_context(pg.psum(f"xao_ps{b}", [P, T], F32)) for b in range(2)]
        block = ctx.enter_context(nc.Block())

        @block.tensor
        def _(pe):
            def scores(i):
                hd, tb = units[i]
                if i >= 2:
                    pe.wait_ge(exped.sem, exped.at(i - 1))
                for j in range(2):
                    last = pe.matmul(sps[i % 2][:, :], qT[:, 2 * hd + j, tb * P:(tb + 1) * P], kT[:, 2 * hd + j, :],
                                     start=(j == 0), stop=(j == 1))
                last.then_inc(scored.sem, 1)

            scores(0)
            for i, (hd, tb) in enumerate(units):
                if i + 1 < n:
                    scores(i + 1)
                pe.wait_ge(normed.sem, normed.at(i + 1))
                if i >= 2:
                    pe.wait_ge(flip_taken.sem, flip_taken.at(i - 1))
                for m in range(2):
                    last = pe.transpose(fps[i % 2][:, m, :], prob[:, i % 2, m * P:(m + 1) * P], pg.c["ident"][:, :])
                last.then_inc(flipped.sem, 1)
                if tb == TB - 1:
                    pe.wait_ge(flip_taken.sem, flip_taken.at(i + 1))
                    for j in range(2):
                        o = 2 * hd + j
                        if o >= 2:
                            pe.wait_ge(mix_taken.sem, mix_taken.at(o - 1))
                        for m in range(2):
                            last = pe.matmul(ops[j][:, :], v[:, m, o * P:(o + 1) * P], probT[:, hd % 2, m, :],
                                             start=(m == 0), stop=(m == 1))
                        last.then_inc(mixed.sem, 1)

        @block.vector
        def _(dve):
            link = linker(dve, vec_step)

            def maximum(i):
                dve.wait_ge(scored.sem, scored.at(i + 1))
                link(dve.reduce_max(stats[:, 0, i:i + 1], sps[i % 2][:, :], AX.X))
                dve.tensor_scalar(stats[:, 0, i:i + 1], stats[:, 0, i:i + 1], -scale, None, ALU.mult).then_inc(maxed.sem, 1)

            maximum(0)
            for i, (hd, tb) in enumerate(units):
                if i + 1 < n:
                    maximum(i + 1)
                dve.wait_ge(exped.sem, exped.at(i + 1))
                link(dve.reciprocal(stats[:, 2, i:i + 1], stats[:, 1, i:i + 1]))
                dve.tensor_scalar(prob[:, i % 2, :], prob[:, i % 2, :], stats[:, 2, i:i + 1], None, ALU.mult) \
                    .then_inc(normed.sem, 1)
                if tb == TB - 1:
                    for j in range(2):
                        o = 2 * hd + j
                        dve.wait_ge(mixed.sem, mixed.at(o + 1))
                        dve.tensor_copy(oT[:, o, :], ops[j][:, :]).then_inc(mix_taken.sem, 1)

        @block.scalar
        def _(act):
            def exponential(i):
                act.wait_ge(maxed.sem, maxed.at(i + 1))
                if i >= 2:
                    act.wait_ge(flipped.sem, flipped.at(i - 1))
                act.activation(prob[:, i % 2, :], sps[i % 2][:, :], ACT.Exp, bias=stats[:, 0, i:i + 1], scale=scale,
                               accum_out=stats[:, 1, i:i + 1]).then_inc(exped.sem, 1)

            exponential(0)
            for i, (hd, tb) in enumerate(units):
                if i + 1 < n:
                    exponential(i + 1)
                act.wait_ge(flipped.sem, flipped.at(i + 1))
                if tb == 0 and hd >= 2:
                    act.wait_ge(mixed.sem, mixed.at(2 * (hd - 1)))
                act.activation(probT[:, hd % 2, :, tb * P:(tb + 1) * P], fps[i % 2][:, :, :], ACT.Copy) \
                    .then_inc(flip_taken.sem, 1)
    for s in (scored, maxed, exped, normed, flipped, flip_taken):
        s.passed(n)
    mixed.passed(KD)
    mix_taken.passed(KD)


def peer(pg, layer):
    nc = pg.nc

    def buf(own, name, shape, dt=F32):
        return own.enter_context(pg.sbuf(name, shape, dt))

    with ExitStack() as whole:
        route = buf(whole, "route", [P, 2, T], BF16)
        parts = buf(whole, "gate_parts", [P, 3, T], BF16)
        h_high, h_low = (buf(whole, n, [P, KD, T], F32R) for n in ("peer_h_high", "peer_h_low"))
        with ExitStack() as own:
            h = buf(own, "peer_h", [P, KD, T])
            norm(pg, pg.xT, vec(pg, "norm_ffn"), h, T)
            split_rhs(pg, h, h_high, h_low)
        peer_route(pg, layer, h_high, h_low, route, parts)
        peer_experts(pg, layer, h_high, h_low, route, parts)


def split_rhs(pg, h, high, low):
    made, left = pg.counts("h_high_made"), pg.counts("h_low_made")
    with pg.nc.Block() as block:
        @block.scalar
        def _(act):
            for k in range(KD):
                split_high(act, high[:, k, :], h[:, k, :]).then_inc(made.sem, 1)

        @block.vector
        def _(dve):
            for k in range(KD):
                dve.wait_ge(made.sem, made.at(k + 1))
                split_low(dve, low[:, k, :], h[:, k, :], high[:, k, :]).then_inc(left.sem, 1)
    made.passed(KD)
    left.passed(KD)


def peer_route(pg, layer, h_high, h_low, route, parts):
    nc = pg.nc
    U32 = mybir.dt.uint32
    keys_loaded = pg.counts("keys_loaded")
    loaded, high_made, low_made, summed, q_taken = ([pg.counts(f"query_{n}{b}") for b in range(2)] for n in (
        "loaded", "high_made", "low_made", "summed", "taken"))
    scored, score_taken = pg.counts("key_scored"), pg.counts("key_score_taken")
    searched, shifted, exped = pg.counts("key_searched"), pg.counts("top_shifted"), pg.counts("top_exped")
    found, flipped, flip_taken = pg.counts("route_found"), pg.counts("route_flipped"), pg.counts("route_flip_taken")
    vec_step = pg.counts("vec_step")
    with ExitStack() as ctx:
        def buf(name, shape, dt=F32):
            return ctx.enter_context(pg.sbuf(name, shape, dt))
        w = [buf(f"query_w{b}", [P, KD, P]) for b in range(2)]
        wh, wl = ([buf(f"query_{x}{b}", [P, KD, P], F32R) for b in range(2)] for x in ("high", "low"))
        keys = buf("keys", [P, 2 * PH, NKEY])
        q = buf("queries", [P, 2, 2, T])
        sc = buf("key_scores", [P, 2, TB, 2, NKEY])
        rest = buf("key_rest", [P, 4, 2 * NKEY])
        top, at, atf = buf("key_top", [P, TB, 2, TOPK]), buf("key_at", [P, TB, 2, TOPK], U32), buf("key_atf", [P, TB, 2, TOPK])
        cand = buf("cand", [P, TB, TOPK, TOPK])
        best, pos = buf("best", [P, TB, TOPK]), buf("pos", [P, TB, TOPK], U32)
        spot = [buf(f"spot{j}", [P, TB, TOPK], U32) for j in range(2)]
        spotf = [buf(f"spotf{j}", [P, TB, TOPK]) for j in range(2)]
        hit = [buf(f"hit{j}", [P, TB, TOPK, TOPK]) for j in range(2)]
        chosen = buf("chosen", [P, TB, 3, PH * TOPK])
        total = buf("total", [P, TB, 1])
        gate = buf("gate", [P, T])
        qps = [ctx.enter_context(pg.psum(f"query_ps{b}", [P, T], F32)) for b in range(2)]
        sps = [[ctx.enter_context(pg.psum(f"key_ps{b}{x}", [P, 2, 2, NKEY], F32)) for x in range(2)] for b in range(2)]
        block = ctx.enter_context(nc.Block())

        @block.sync
        def _(sp):
            for m in range(2 * PH):
                b, n = m % 2, m // 2
                if n:
                    sp.wait_ge(low_made[b].sem, low_made[b].at(n))
                sp.dma_start(w[b][:, :, :].rearrange("p k n -> p (k n)"), pg.dram["peer_wq"][layer][m]) \
                    .then_inc(loaded[b].sem, 16)
                if m == 1:
                    sp.dma_start(keys[:, :, :], pg.dram["peer_keys"][layer]).then_inc(keys_loaded.sem, 16)

        @block.tensor
        def _(pe):
            def queries(hd):
                for b in range(2):
                    pe.wait_ge(low_made[b].sem, low_made[b].at(hd + 1))
                    if hd:
                        pe.wait_ge(q_taken[b].sem, q_taken[b].at(hd))
                    for k in range(KD):
                        last = product(pe, qps[b][:, :], (wh[b][:, k, :], wl[b][:, k, :]), (h_high[:, k, :], h_low[:, k, :]),
                                       k == 0, k == KD - 1)
                    last.then_inc(summed[b].sem, 1)

            queries(0)
            pe.wait_ge(keys_loaded.sem, keys_loaded.at(16))
            for hd in range(PH):
                if hd + 1 < PH:
                    queries(hd + 1)
                for b in range(2):
                    pe.wait_ge(q_taken[b].sem, q_taken[b].at(hd + 1))
                if hd >= 2:
                    pe.wait_ge(score_taken.sem, score_taken.at(2 * (hd - 1)))
                for tb in range(TB):
                    for x in range(2):
                        last = pe.matmul(sps[hd % 2][tb // 2][:, tb % 2, x, :], q[:, hd % 2, x, tb * P:(tb + 1) * P],
                                         keys[:, 2 * hd + x, :], start=True, stop=True)
                last.then_inc(scored.sem, 1)
            pe.wait_ge(found.sem, found.at(PH))
            for tb in range(TB):
                bank = sps[tb // 2][tb % 2][:, :, :, :].rearrange("p a b n -> p (a b) n")
                for j in range(3):
                    last = pe.transpose(bank[:, j, :], chosen[:, tb, j, :], pg.c["ident"][:, :])
                last.then_inc(flipped.sem, 1)

        @block.scalar
        def _(act):
            def high(hd):
                for b in range(2):
                    act.wait_ge(loaded[b].sem, loaded[b].at(16 * (hd + 1)))
                    if hd:
                        act.wait_ge(summed[b].sem, summed[b].at(hd))
                    split_high(act, wh[b][:, :, :], w[b][:, :, :]).then_inc(high_made[b].sem, 1)

            def take_queries(hd):
                for b in range(2):
                    act.wait_ge(summed[b].sem, summed[b].at(hd + 1))
                    if hd >= 2:
                        act.wait_ge(scored.sem, scored.at(hd - 1))
                    act.activation(q[:, hd % 2, b, :], qps[b][:, :], ACT.Copy).then_inc(q_taken[b].sem, 1)

            def take_scores(hd):
                act.wait_ge(scored.sem, scored.at(hd + 1))
                if hd >= 2:
                    act.wait_ge(searched.sem, searched.at(hd - 1))
                for x in range(2):
                    act.activation(sc[:, hd % 2, 2 * x:2 * x + 2, :, :], sps[hd % 2][x][:, :, :, :], ACT.Copy) \
                        .then_inc(score_taken.sem, 1)

            high(0)
            take_queries(0)
            high(1)
            for hd in range(-1, PH):
                if hd + 1 < PH:
                    if hd >= 0:
                        take_queries(hd + 1)
                        if hd + 2 < PH:
                            high(hd + 2)
                    take_scores(hd + 1)
                if hd >= 0:
                    act.wait_ge(shifted.sem, shifted.at(hd + 1))
                    act.activation(best[:, :, :], best[:, :, :], ACT.Exp).then_inc(exped.sem, 1)
            for tb in range(TB):
                act.wait_ge(flipped.sem, flipped.at(tb + 1))
                bank = sps[tb // 2][tb % 2][:, :, :, :].rearrange("p a b n -> p (a b) n")
                act.activation(route[:, :, tb * P:(tb + 1) * P], bank[:, 0:2, :], ACT.Copy)
                act.activation(gate[:, tb * P:(tb + 1) * P], bank[:, 2, :], ACT.Copy).then_inc(flip_taken.sem, 1)

        @block.vector
        def _(dve):
            link = linker(dve, vec_step)

            def lows(hd):
                for b in range(2):
                    dve.wait_ge(high_made[b].sem, high_made[b].at(hd + 1))
                    split_low(dve, wl[b][:, :, :], w[b][:, :, :], wh[b][:, :, :]).then_inc(low_made[b].sem, 1)

            def top16(rows):
                for i in range(0, len(rows), 4):
                    some = rows[i:i + 4]
                    for x, r, v, a in some:
                        last = dve.max(v[:, 0:8], x)
                    link(last)
                    for x, r, v, a in some:
                        dve.max_index(a[:, 0:8], v[:, 0:8], x)
                        last = dve.match_replace(out=r, in_to_replace=v[:, 0:8], in_values=x, imm_value=LOWEST)
                    link(last)
                    for x, r, v, a in some:
                        last = dve.max(v[:, 8:16], r)
                    link(last)
                    for x, r, v, a in some:
                        last = dve.max_index(a[:, 8:16], v[:, 8:16], r)
                    link(last)

            down = lambda x: x.rearrange("p (k a) -> p k a", a=1).to_broadcast([P, TOPK, TOPK])
            across = lambda x: x.rearrange("p (a k) -> p a k", a=1).to_broadcast([P, TOPK, TOPK])
            ramp = across(pg.c["ramp"][:, 0:TOPK])
            lows(0)
            lows(1)
            for hd in range(PH):
                if hd + 2 < PH:
                    lows(hd + 2)
                dve.wait_ge(score_taken.sem, score_taken.at(2 * hd + 2))
                top16([(sc[:, hd % 2, tb, x, :], rest[:, tb, x * NKEY:(x + 1) * NKEY], top[:, tb, x, :], at[:, tb, x, :])
                       for tb in range(TB) for x in range(2)])
                dve.sem_inc(searched.sem, 1)
                dve.tensor_copy(atf[:, :, :, :], at[:, :, :, :])
                for tb in range(TB):
                    last = dve.tensor_tensor(cand[:, tb, :, :], down(top[:, tb, 0, :]), across(top[:, tb, 1, :]), ALU.add)
                link(last)
                top16([(cand[:, tb, :, :].rearrange("p a b -> p (a b)"), rest[:, tb, :], best[:, tb, :], pos[:, tb, :])
                       for tb in range(TB)])
                link(dve.tensor_copy(total[:, :, :], best[:, :, 0:1]))
                link(dve.tensor_tensor(best[:, :, :], best[:, :, :], total[:, :, :].to_broadcast([P, TB, TOPK]), ALU.subtract))
                dve.sem_inc(shifted.sem, 1)
                dve.tensor_scalar(spot[0][:, :, :], pos[:, :, :], 4, None, ALU.logical_shift_right)
                link(dve.tensor_scalar(spot[1][:, :, :], pos[:, :, :], TOPK - 1, None, ALU.bitwise_and))
                for j in range(2):
                    last = dve.tensor_copy(spotf[j][:, :, :], spot[j][:, :, :])
                link(last)
                for j in range(2):
                    for tb in range(TB):
                        last = dve.tensor_tensor(hit[j][:, tb, :, :], down(spotf[j][:, tb, :]), ramp, ALU.is_equal)
                link(last)
                for j in range(2):
                    for tb in range(TB):
                        last = dve.tensor_tensor(hit[j][:, tb, :, :], hit[j][:, tb, :, :], across(atf[:, tb, j, :]), ALU.mult)
                link(last)
                own = slice(hd * TOPK, (hd + 1) * TOPK)
                for j in range(2):
                    last = dve.reduce_sum(chosen[:, :, j, own], hit[j][:, :, :, :], AX.X)
                dve.wait_ge(exped.sem, exped.at(hd + 1))
                link(dve.reduce_sum(total[:, :, :].rearrange("p h a -> p (h a)"), best[:, :, :], AX.X))
                link(dve.reciprocal(total[:, :, :], total[:, :, :]))
                link(dve.tensor_tensor(chosen[:, :, 2, own], best[:, :, :], total[:, :, :].to_broadcast([P, TB, TOPK]), ALU.mult))
                dve.sem_inc(found.sem, 1)
            dve.wait_ge(flip_taken.sem, flip_taken.at(TB))
            for j in range(3):
                link(dve.tensor_copy(parts[:, j, :], gate[:, :]))
                if j < 2:
                    link(dve.tensor_tensor(gate[:, :], gate[:, :], parts[:, j, :], ALU.subtract))
    keys_loaded.passed(16)
    for b in range(2):
        loaded[b].passed(16 * PH)
        for s in (high_made[b], low_made[b], summed[b], q_taken[b]):
            s.passed(PH)
    for s in (scored, searched, shifted, exped, found):
        s.passed(PH)
    score_taken.passed(2 * PH)
    flipped.passed(TB)
    flip_taken.passed(TB)


SLAB = 16
SLABS = NKEY // SLAB
BUFS = 2
TURNS = SLAB // BUFS
AHEAD = 2
GROUP = T // (TURNS * BUFS)
SUB = 8
SUBS = GROUP // SUB


def peer_experts(pg, layer, h_high, h_low, route, parts):
    nc = pg.nc
    loaded, high_made, low_made, multiplied, gelued, weighed = (
        [pg.counts(f"{n}{b}") for b in range(BUFS)]
        for n in ("block_loaded", "block_high_made", "block_low_made", "block_multiplied", "up_gelued", "up_weighed"))
    first, first_used = ([pg.counts(f"{n}{c}") for c in range(SUBS)] for n in ("first_made", "first_used"))
    second, equal, taken = ([pg.counts(f"{n}{b}") for b in range(2)] for n in ("second_made", "second_equal", "gates_taken"))
    added, ramps_made = pg.counts("down_added"), pg.counts("ramps_made")
    with ExitStack() as ctx:
        def buf(name, shape, dt=F32R):
            return [ctx.enter_context(pg.sbuf(f"{name}{b}", shape, dt)) for b in range(2)]
        gates = buf("gates", [P, SLAB, T], F32)
        raw, wh, wl = buf("block", [P, D], F32), buf("block_high", [P, D]), buf("block_low", [P, D])
        gh, gl = buf("gate_high", [P, T]), buf("gate_low", [P, T])
        a = buf("up_act", [P, T], F32)
        one = [ctx.enter_context(pg.sbuf(f"onehot1_{c}", [P, NKEY, SUB], BF16)) for c in range(SUBS)]
        same, two = buf("onehot2", [P, SLAB, GROUP], BF16), buf("weighed2", [P, 3, SLAB, GROUP], BF16)
        ramps = ctx.enter_context(pg.sbuf("ramps", [P, NKEY, GROUP], BF16))
        ps = [ctx.enter_context(pg.psum(f"peer_ps{b}", [P, T], F32)) for b in range(KD)]
        block = ctx.enter_context(nc.Block())
        tables = pg.dram["peer_u"][layer], pg.dram["peer_v"][layer]
        row = lambda g, i, b: g[:, bass.ds(i * BUFS + b, 1), :].rearrange("p a t -> p (a t)")

        def turn_of(slab, down):
            return (2 * slab + down) * TURNS

        @block.sync
        def _(sp):
            for slab in range(SLABS):
                for down in range(2):
                    n = turn_of(slab, down)
                    with sp.Fori(0, TURNS) as i:
                        for b in range(BUFS):
                            sp.wait_ge(low_made[b].sem, low_made[b].at(n) + i)
                            sp.dma_start(raw[b][:, :], tables[down][bass.ds(i * BUFS + (b + slab * SLAB), 1), :, :]
                                         .rearrange("a p n -> p (a n)")).then_inc(loaded[b].sem, 16)

        @block.gpsimd
        def _(pool):
            pool.iota(ramps[:, :, :], pattern=[[1, NKEY], [0, GROUP]], base=0, channel_multiplier=0,
                      allow_small_or_imprecise_dtypes=True).then_inc(ramps_made.sem, 1)
            for slab in range(SLABS):
                with pool.Fori(0, TURNS) as i:
                    for b in range(2):
                        t = bass.ds(i * 2 * GROUP + b * GROUP, GROUP)
                        pool.wait_ge(equal[b].sem, equal[b].at(slab * TURNS + 1) + i)
                        pool.wait_ge(taken[b].sem, taken[b].at(slab * TURNS) + i)
                        for j in range(3):
                            last = pool.tensor_tensor(two[b][:, j, :, :], same[b][:, :, :],
                                                      parts[:, j:j + 1, t].to_broadcast([P, SLAB, GROUP]), ALU.mult)
                        last.then_inc(second[b].sem, 1)

        def make_onehots(dve, slab, i, b):
            dve.wait_ge(second[b].sem, second[b].at(slab * TURNS) + i)
            dve.tensor_tensor(same[b][:, :, :], ramps[:, slab * SLAB:(slab + 1) * SLAB, :],
                              route[:, 1:2, bass.ds(i * 2 * GROUP + b * GROUP, GROUP)].to_broadcast([P, SLAB, GROUP]),
                              ALU.is_equal).then_inc(equal[b].sem, 1)
            for c in range(SUBS):
                dve.wait_ge(first_used[c].sem, first_used[c].at(2 * slab * TURNS + b) + i * 2)
                dve.tensor_tensor(one[c][:, :, :], ramps[:, :, 0:SUB],
                                  route[:, 0:1, bass.ds(i * 2 * GROUP + (b * GROUP + c * SUB), SUB)]
                                  .to_broadcast([P, NKEY, SUB]), ALU.is_equal).then_inc(first[c].sem, 1)

        def spread_gates(pe, slab, i, b):
            pe.wait_ge(second[b].sem, second[b].at(slab * TURNS + 1) + i)
            pe.wait_ge(taken[b].sem, taken[b].at(slab * TURNS) + i)
            for c in range(SUBS):
                pe.wait_ge(first[c].sem, first[c].at(2 * slab * TURNS + b + 1) + i * 2)
                for t in range(SUB):
                    g = c * SUB + t
                    for j in range(3):
                        last = pe.matmul(ps[2 + b][:, g * SLAB:(g + 1) * SLAB], one[c][:, :, t], two[b][:, j, :, g],
                                         start=(j == 0), stop=(j == 2))
                last.then_inc(first_used[c].sem, 1)

        def take_gates(act, slab, i, b):
            act.wait_ge(first_used[-1].sem, first_used[-1].at(2 * slab * TURNS + b + 1) + i * 2)
            act.activation(gates[slab % 2][:, :, bass.ds(i * 2 * GROUP + b * GROUP, GROUP)].rearrange("p k t -> p t k"),
                           ps[2 + b][:, :].rearrange("p (t k) -> p t k", k=SLAB), ACT.Copy).then_inc(taken[b].sem, 1)

        @block.tensor
        def _(pe):
            with pe.Fori(0, TURNS) as i:
                for b in range(2):
                    spread_gates(pe, 0, i, b)
            for slab in range(SLABS):
                n = turn_of(slab, 0)
                with pe.Fori(0, TURNS // AHEAD) as h:
                    for i, b in ((h * AHEAD + s, b) for s in range(AHEAD) for b in range(BUFS)):
                        pe.wait_ge(low_made[b].sem, low_made[b].at(n + 1) + i)
                        pe.wait_ge(gelued[b].sem, gelued[b].at(slab * TURNS) + i)
                        if slab:
                            pe.wait_ge(added.sem, added.at(KD * (slab - 1) + b + 1))
                        for k in range(KD):
                            w = slice(k * P, (k + 1) * P)
                            last = product(pe, ps[b][:, :], (wh[b][:, w], wl[b][:, w]), (h_high[:, k, :], h_low[:, k, :]),
                                           k == 0, k == KD - 1)
                        last.then_inc(multiplied[b].sem, 1)
                        if slab + 1 < SLABS:
                            if slab:
                                pe.wait_ge(added.sem, added.at(KD * (slab - 1) + 2 + b + 1))
                            spread_gates(pe, slab + 1, i, b)
                n = turn_of(slab, 1)
                for b in range(2):
                    pe.wait_ge(gelued[b].sem, gelued[b].at((slab + 1) * TURNS))
                    if slab + 1 < SLABS:
                        pe.wait_ge(taken[b].sem, taken[b].at((slab + 2) * TURNS))
                if slab:
                    pe.wait_ge(added.sem, added.at(KD * slab))

                def down(i, at_start, at_end):
                    for b in range(BUFS):
                        pe.wait_ge(low_made[b].sem, low_made[b].at(n + 1) + i)
                        for k in range(KD):
                            w = slice(k * P, (k + 1) * P)
                            last = product(pe, ps[k][:, :], (wh[b][:, w], wl[b][:, w]), (gh[b][:, :], gl[b][:, :]),
                                           at_start and b == 0, at_end and b == BUFS - 1)
                        last.then_inc(multiplied[b].sem, 1)

                down(0, True, False)
                with pe.Fori(0, (TURNS - 2) // AHEAD) as h:
                    for s in range(AHEAD):
                        down(h * AHEAD + (s + 1), False, False)
                down(TURNS - 1, False, True)

        @block.scalar
        def _(act):
            def high(n, i, b):
                act.wait_ge(loaded[b].sem, loaded[b].at(16 * (n + 1)) + i * 16)
                act.wait_ge(multiplied[b].sem, multiplied[b].at(n) + i)
                split_high(act, wh[b][:, :], raw[b][:, :]).then_inc(high_made[b].sem, 1)

            def up_high(slab, i, b):
                high(turn_of(slab, 0), i, b)

            def down_high(slab, i, b):
                n = turn_of(slab, 1)
                act.wait_ge(multiplied[b].sem, multiplied[b].at(n) + i)
                act.wait_ge(weighed[b].sem, weighed[b].at(slab * TURNS + 1) + i)
                split_high(act, gh[b][:, :], row(gates[slab % 2], i, b))
                high(n, i, b)

            def gelu(slab, i, b):
                act.wait_ge(multiplied[b].sem, multiplied[b].at(turn_of(slab, 0) + 1) + i)
                act.wait_ge(weighed[b].sem, weighed[b].at(slab * TURNS) + i)
                act.activation(a[b][:, :], ps[b][:, :], ACT.Gelu_apprx_tanh).then_inc(gelued[b].sem, 1)

            with act.Fori(0, TURNS) as i:
                for b in range(2):
                    take_gates(act, 0, i, b)
            for b in range(BUFS):
                up_high(0, 0, b)
            for slab in range(SLABS):
                build = slab + 1 < SLABS
                with act.Fori(0, TURNS - 1) as i:
                    for b in range(BUFS):
                        up_high(slab, i + 1, b)
                        gelu(slab, i, b)
                        if build:
                            take_gates(act, slab + 1, i, b)
                for b in range(BUFS):
                    gelu(slab, TURNS - 1, b)
                    down_high(slab, 0, b)
                    if build:
                        take_gates(act, slab + 1, TURNS - 1, b)
                with act.Fori(0, TURNS - 1) as i:
                    for b in range(BUFS):
                        down_high(slab, i + 1, b)
                if build:
                    for b in range(BUFS):
                        up_high(slab + 1, 0, b)

        @block.vector
        def _(dve):
            def low(n, i, b):
                dve.wait_ge(high_made[b].sem, high_made[b].at(n + 1) + i)
                split_low(dve, wl[b][:, :], raw[b][:, :], wh[b][:, :]).then_inc(low_made[b].sem, 1)

            def down_low(slab, i, b):
                n = turn_of(slab, 1)
                dve.wait_ge(high_made[b].sem, high_made[b].at(n + 1) + i)
                split_low(dve, gl[b][:, :], row(gates[slab % 2], i, b), gh[b][:, :])
                low(n, i, b)

            def weigh(slab, i, b):
                dve.wait_ge(gelued[b].sem, gelued[b].at(slab * TURNS + 1) + i)
                for c in range(2):
                    dve.wait_ge(taken[c].sem, taken[c].at((slab + 1) * TURNS))
                g = row(gates[slab % 2], i, b)
                dve.tensor_tensor(g, g, a[b][:, :], ALU.mult).then_inc(weighed[b].sem, 1)

            dve.wait_ge(ramps_made.sem, ramps_made.at(1))
            with dve.Fori(0, TURNS) as i:
                for b in range(2):
                    make_onehots(dve, 0, i, b)
            for b in range(BUFS):
                low(0, 0, b)
            for slab in range(SLABS):
                build = slab + 1 < SLABS
                with dve.Fori(0, TURNS - 1) as i:
                    for b in range(BUFS):
                        if build:
                            make_onehots(dve, slab + 1, i, b)
                        low(turn_of(slab, 0), i + 1, b)
                        weigh(slab, i, b)
                for b in range(BUFS):
                    if build:
                        make_onehots(dve, slab + 1, TURNS - 1, b)
                    weigh(slab, TURNS - 1, b)
                    down_low(slab, 0, b)
                with dve.Fori(0, TURNS - 1) as i:
                    for b in range(BUFS):
                        down_low(slab, i + 1, b)
                if build:
                    for b in range(BUFS):
                        low(turn_of(slab + 1, 0), 0, b)
                dve.wait_ge(multiplied[-1].sem, multiplied[-1].at(turn_of(slab + 1, 0)))
                for k in range(KD):
                    dve.tensor_tensor(pg.xT[:, k, :], pg.xT[:, k, :], ps[k][:, :], ALU.add).then_inc(added.sem, 1)
                dve.wait_ge(added.sem, added.at(KD * (slab + 1)))
    added.passed(KD * SLABS)
    ramps_made.passed(1)
    for b in range(2):
        loaded[b].passed(16 * 2 * TURNS * SLABS)
        for s in (high_made[b], low_made[b], multiplied[b]):
            s.passed(2 * TURNS * SLABS)
        for s in (gelued[b], weighed[b], second[b], equal[b], taken[b]):
            s.passed(TURNS * SLABS)
    for s in first + first_used:
        s.passed(2 * TURNS * SLABS)


def build(nc, dram, out):
    with ExitStack() as ctx:
        def keep(name, shape, dt=F32):
            return ctx.enter_context(nc.sbuf_tensor(name, shape, dt))

        pg = Program(nc, ctx, dram)
        pg.xT = keep("xT", [P, KD, T])
        pg.vec = keep("vec", [P, NVEC])
        pg.v_first = keep("v_first", [P, KH, T])
        for name, shape in (("ones", [P, P]), ("ident", [P, P]), ("head_ones", [P, P]), ("gram_mask", [P, 4, P]),
                            ("lower_mask", [P, P]), ("level_mask", [P, 6, P]), ("level0_lower", [P, P]),
                            ("chunk_keep", [P, T]), ("ramp", [P, NKEY])):
            pg.c[name] = keep(name, shape)
        constants(pg)
        for layer in range(DEPTH):
            load_vectors(pg, layer)
            mixer(pg, layer)
            cross_attention(pg, layer)
            peer(pg, layer)
        with ExitStack() as own:
            yT = own.enter_context(pg.sbuf("yT", [P, KD, T], F32))
            norm(pg, pg.xT, vec(pg, "norm_final"), yT, T)
            stored = pg.counts("out_stored")
            with nc.Block() as block:
                @block.sync
                def _(sp):
                    sp.dma_start(out, yT[:, :, :]).then_inc(stored.sem, 16)
                    sp.wait_ge(stored.sem, stored.at(16))


def kernel(**inputs):
    import numpy as np
    import concourse.bacc as bacc
    from concourse.bass_utils import run_bass_kernel_spmd

    a = {k: np.asarray(v) for k, v in inputs.items()}
    L = DEPTH

    def tiles(w):
        n, k, m = w.shape
        return w.reshape(n, k // P, P, m // P, P).transpose(0, 3, 2, 1, 4).reshape(n, m // P, P, k)

    def rows(w):
        s = w.shape
        w = w.reshape(*s[:-2], s[-2] // P, P, s[-1])
        return np.moveaxis(w, -2, -3)

    def columns(v):
        return v.reshape(v.shape[0], -1, P).transpose(0, 2, 1)

    per_layer = {
        "norm_mix": a["norm_mix"], "norm_xa": a["norm_xa"], "norm_mem": a["norm_mem"], "norm_ffn": a["norm_ffn"],
        "norm_final": np.broadcast_to(a["norm_final"], (L, D)), "mu": a["rw_mu"], "w0": a["rw_w0"], "a0": a["rw_a0"],
        "kk": a["rw_kk"], "ka": a["rw_ka"], "rk": a["rw_rk"].reshape(L, D_HALF),
        "v0": a["rw_v0"][[max(l - 1, 0) for l in range(L)]], "lnx_g": a["rw_lnx_g"], "lnx_b": a["rw_lnx_b"],
        "s5_d": a["s5_d"], "glu_b": a["s5_glu_b"], "out_g": a["s5_out_g"],
    }
    pairs = lambda v: v.reshape(L, S5_PAIRS, P).transpose(0, 2, 1)

    def experts(w):
        return w.reshape(L, NKEY, NKEY, D).transpose(0, 2, 1, 3)

    arrays = {
        "xT": rows(a["x"][0].T), "memT": rows(a["mem"][0].T),
        "vec": np.concatenate([columns(per_layer[n]) for n in VEC], axis=2),
        "w_in": tiles(a["w_in"]), "w2": a["rw_w2"], "a2": a["rw_a2"], "g2": a["rw_g2"],
        "v1": rows(a["rw_v1"]), "v2": a["rw_v2"],
        "s5_are": pairs(a["s5_a_re"]), "s5_aim": pairs(a["s5_a_im"]),
        "s5_dt": pairs(np.repeat(a["s5_log_dt"], 64, axis=1).reshape(L, 32, 64)),
        "s5_bre": a["s5_b_re"], "s5_bim": a["s5_b_im"],
        "s5_cre": a["s5_c_re"].transpose(0, 1, 3, 2), "s5_cim": a["s5_c_im"].transpose(0, 1, 3, 2),
        "glu_w": tiles(a["s5_glu_w"]), "w_out": tiles(a["w_out"]),
        "xa_wq": tiles(a["xa_wq"]), "xa_wk": tiles(a["xa_wk"]), "xa_wo": tiles(a["xa_wo"]),
        "xa_wv": rows(a["xa_wv"]),
        "peer_wq": tiles(a["peer_wq"]),
        "peer_keys": a["peer_keys"].reshape(L, 2 * PH, NKEY, P).transpose(0, 3, 1, 2),
        "peer_u": experts(a["peer_u"]).reshape(L, NKEY, NKEY, KD, P).transpose(0, 1, 4, 3, 2).reshape(L, NKEY, P, D),
        "peer_v": experts(a["peer_v"]),
    }
    nc = bacc.Bacc("TRN2", target_bir_lowering=False, num_devices=1)
    dram, sent = {}, {}
    for name, v in arrays.items():
        v = np.ascontiguousarray(v)
        sent[f"in_{name}"] = v
        dram[name] = nc.dram_tensor(f"in_{name}", v.shape, mybir.dt.from_np(v.dtype), kind="ExternalInput").ap()
    out = nc.dram_tensor("out", (P, KD, T), F32, kind="ExternalOutput").ap()
    build(nc, dram, out)
    r = run_bass_kernel_spmd(nc, [sent], core_ids=[0])
    y = r.results[0]["out"]
    return y.transpose(1, 0, 2).reshape(D, T).T.reshape(1, T, D)
```
